# Optimizing a Trainium2 kernel written in Bass

```python
import math
import jax, jax.numpy as jnp
from jax import lax
import numpy as np

D_MODEL = 2048
BATCH = 1
SEQ = 256
DEPTH = 1

HEAD_DIM = 64
ATTN_WIDTH = D_MODEL // 2
N_Q_HEADS = ATTN_WIDTH // HEAD_DIM
N_KV_HEADS = N_Q_HEADS // 4
GQA_GROUP = N_Q_HEADS // N_KV_HEADS
N_BRANCH = 3
CMP_LEN = 32
CMP_STRIDE = 16
CMP_OVERLAP = CMP_LEN // CMP_STRIDE
SLC_LEN = 64
SLC_TOPK = 16
WINDOW = 512
Q_BLOCK = 64
CONV_CHANNELS = D_MODEL - ATTN_WIDTH
CONV_TAPS = 31
D_MIX = ATTN_WIDTH + CONV_CHANNELS
D_FF = ((8 * D_MODEL // 3 + 255) // 256) * 256
FFN_CONV_TAPS = 3
N_BUCKETS = 32
MAX_DISTANCE = 128
NORM_EPS = 1e-6
NEG_INF = -1e30

Q_COLS = ATTN_WIDTH
KV_COLS = N_BRANCH * 2 * N_KV_HEADS * HEAD_DIM
GATE_COLS = N_BRANCH * N_Q_HEADS
CONV_IN_COLS = 2 * CONV_CHANNELS
IN_COLS = Q_COLS + KV_COLS + GATE_COLS + CONV_IN_COLS


def rms_norm(x, g):
    xf = x.astype(jnp.float32)
    y = xf * lax.rsqrt(jnp.mean(xf * xf, axis=-1, keepdims=True) + NORM_EPS)
    return (y * g.astype(jnp.float32)).astype(x.dtype)

def layer_norm(x, g, b):
    xf = x.astype(jnp.float32)
    mu = jnp.mean(xf, axis=-1, keepdims=True)
    xc = xf - mu
    var = jnp.mean(xc * xc, axis=-1, keepdims=True)
    y = xc * lax.rsqrt(var + NORM_EPS) * g.astype(jnp.float32) + b.astype(jnp.float32)
    return y.astype(x.dtype)

def t5_bucket(dist):
    n = jnp.maximum(dist, 0)
    max_exact = N_BUCKETS // 2
    nf = jnp.maximum(n, 1).astype(jnp.float32)
    large = max_exact + (jnp.log(nf / max_exact) / math.log(MAX_DISTANCE / max_exact)
                         * (N_BUCKETS - max_exact)).astype(jnp.int32)
    large = jnp.minimum(large, N_BUCKETS - 1)
    return jnp.where(n < max_exact, n, large)

def masked_softmax(s, mask):
    s = jnp.where(mask, s.astype(jnp.float32), NEG_INF)
    p = jax.nn.softmax(s, axis=-1)
    return jnp.where(mask, p, 0.0)

def causal_depthwise_conv(x, w, b):
    taps, c = w.shape
    y = lax.conv_general_dilated(x, w[:, None, :].astype(x.dtype), window_strides=(1,),
                                 padding=[(taps - 1, 0)],
                                 dimension_numbers=('NWC', 'WIO', 'NWC'),
                                 feature_group_count=c)
    return y + b.astype(x.dtype)

def compress_tokens(tok, pos, w1, w2):
    b, t, h, d = tok.shape
    n_chunk = t // CMP_STRIDE
    n_cmp = n_chunk - CMP_OVERLAP + 1
    chunks = tok.reshape(b, n_chunk, CMP_STRIDE, h, d)
    blocks = jnp.concatenate([chunks[:, o:o + n_cmp] for o in range(CMP_OVERLAP)], axis=2)
    blocks = blocks + pos[None, None, :, None, :].astype(tok.dtype)
    flat = blocks.transpose(0, 1, 3, 2, 4).reshape(b, n_cmp, h, CMP_LEN * d)
    return jax.nn.silu(flat @ w1) @ w2

def nsa_attention(q, kv, gates, rel_bias, cmp_pos, cmp_w1, cmp_w2):
    b, t_len, hkv, g, dh = q.shape
    scale = HEAD_DIM ** -0.5
    k_cmp = compress_tokens(kv[:, :, 0, 0], cmp_pos[0], cmp_w1[0], cmp_w2[0])
    v_cmp = compress_tokens(kv[:, :, 0, 1], cmp_pos[1], cmp_w1[1], cmp_w2[1])
    n_cmp = k_cmp.shape[1]
    n_slc = t_len // SLC_LEN
    k_sel = min(SLC_TOPK, n_slc)
    k_slc = kv[:, :, 1, 0].reshape(b, n_slc, SLC_LEN, hkv, dh).transpose(0, 3, 1, 2, 4)
    v_slc = kv[:, :, 1, 1].reshape(b, n_slc, SLC_LEN, hkv, dh).transpose(0, 3, 1, 2, 4)
    pad = ((0, 0), (WINDOW, 0), (0, 0), (0, 0))
    k_win = jnp.pad(kv[:, :, 2, 0], pad)
    v_win = jnp.pad(kv[:, :, 2, 1], pad)
    ci_ = jnp.arange(n_cmp)[:, None]
    sj_ = jnp.arange(n_slc)[None, :]
    sel_map = ((ci_ * CMP_STRIDE < (sj_ + 1) * SLC_LEN) &
               (ci_ * CMP_STRIDE + CMP_LEN > sj_ * SLC_LEN)).astype(jnp.float32)
    cmp_end = jnp.arange(n_cmp, dtype=jnp.int32) * CMP_STRIDE + CMP_LEN - 1
    blk_ids = jnp.arange(n_slc, dtype=jnp.int32)[None, :]
    tab_t = rel_bias.reshape(N_BUCKETS, hkv, g).transpose(1, 0, 2)
    h_ar = jnp.arange(hkv)[None, :, None, None, None]
    gather_blocks = jax.vmap(jax.vmap(lambda blk, ii: blk[ii]))

    n_chunks = t_len // Q_BLOCK
    q_ch = q.reshape(b, n_chunks, Q_BLOCK, hkv, g, dh).transpose(1, 0, 3, 2, 4, 5)
    g_ch = gates.reshape(b, n_chunks, Q_BLOCK, hkv, g, N_BRANCH).transpose(1, 0, 3, 2, 4, 5)

    def chunk_fn(args):
        ci, qc, gc = args
        t = ci * Q_BLOCK + jnp.arange(Q_BLOCK, dtype=jnp.int32)
        qs = qc * scale
        s_cmp = jnp.einsum('bhqgd,bnhd->bhqgn', qs, k_cmp).astype(jnp.float32)
        bias_c = rel_bias[t5_bucket(t[:, None] - cmp_end[None, :])]
        bias_c = bias_c.reshape(Q_BLOCK, n_cmp, hkv, g).transpose(2, 0, 3, 1)
        valid_c = (cmp_end[None, :] <= t[:, None])[None, None, :, None, :]
        p_cmp = masked_softmax(s_cmp + bias_c.astype(jnp.float32), valid_c)
        o_cmp = jnp.einsum('bhqgn,bnhd->bhqgd', p_cmp.astype(v_cmp.dtype), v_cmp)
        imp = jnp.einsum('bhqgn,nj->bhqj', p_cmp, sel_map)
        cur = (t // SLC_LEN)[:, None]
        forced = (blk_ids == 0) | (blk_ids == cur) | (blk_ids == cur - 1)
        causal_blk = blk_ids * SLC_LEN <= t[:, None]
        imp = jnp.where(forced, jnp.inf, imp)
        imp = jnp.where(causal_blk, imp, -jnp.inf)
        _, idx = lax.top_k(imp, k_sel)
        kg = gather_blocks(k_slc, idx)
        vg = gather_blocks(v_slc, idx)
        pos = idx[..., None] * SLC_LEN + jnp.arange(SLC_LEN, dtype=jnp.int32)
        dist_s = t[None, None, :, None, None] - pos
        bias_s = jnp.moveaxis(tab_t[h_ar, t5_bucket(dist_s)], -1, 3)
        s_sel = jnp.einsum('bhqgd,bhqkld->bhqgkl', qs, kg).astype(jnp.float32)
        s_sel = (s_sel + bias_s.astype(jnp.float32)).reshape(b, hkv, Q_BLOCK, g, k_sel * SLC_LEN)
        valid_s = (dist_s >= 0).reshape(b, hkv, Q_BLOCK, 1, k_sel * SLC_LEN)
        p_sel = masked_softmax(s_sel, valid_s).reshape(b, hkv, Q_BLOCK, g, k_sel, SLC_LEN)
        o_sel = jnp.einsum('bhqgkl,bhqkld->bhqgd', p_sel.astype(vg.dtype), vg)
        kw = lax.dynamic_slice_in_dim(k_win, ci * Q_BLOCK, Q_BLOCK + WINDOW, axis=1)
        vw = lax.dynamic_slice_in_dim(v_win, ci * Q_BLOCK, Q_BLOCK + WINDOW, axis=1)
        kpos = ci * Q_BLOCK - WINDOW + jnp.arange(Q_BLOCK + WINDOW, dtype=jnp.int32)
        dist_w = t[:, None] - kpos[None, :]
        valid_w = ((dist_w >= 0) & (dist_w < WINDOW) & (kpos[None, :] >= 0))[None, None, :, None, :]
        bias_w = rel_bias[t5_bucket(dist_w)].reshape(Q_BLOCK, Q_BLOCK + WINDOW, hkv, g).transpose(2, 0, 3, 1)
        s_win = jnp.einsum('bhqgd,bshd->bhqgs', qs, kw).astype(jnp.float32)
        p_win = masked_softmax(s_win + bias_w.astype(jnp.float32), valid_w)
        o_win = jnp.einsum('bhqgs,bshd->bhqgd', p_win.astype(vw.dtype), vw)
        return gc[..., 0:1] * o_cmp + gc[..., 1:2] * o_sel + gc[..., 2:3] * o_win

    out = lax.map(chunk_fn, (jnp.arange(n_chunks, dtype=jnp.int32), q_ch, g_ch))
    out = out.transpose(1, 0, 3, 2, 4, 5)
    return out.reshape(b, t_len, ATTN_WIDTH)

def conformer_conv(h2, conv_w, conv_b, ln_g, ln_b):
    a, gate = jnp.split(h2, 2, axis=-1)
    u = a * jax.nn.sigmoid(gate)
    u = causal_depthwise_conv(u, conv_w, conv_b)
    u = layer_norm(u, ln_g, ln_b)
    return jax.nn.silu(u)

def conv_glu_ffn(h, w_up, cw, cb, w_down):
    u = causal_depthwise_conv(h @ w_up, cw, cb)
    a, gate = jnp.split(u, 2, axis=-1)
    return (jax.nn.silu(gate) * a) @ w_down

def first_inputs(seed: int = 0) -> dict:
    key = jax.random.key(seed)
    ks = jax.random.split(key, 18)
    f32 = jnp.float32
    nrm = lambda k, shape, s: jax.random.normal(k, shape, f32) * s
    return {
        "x": nrm(ks[0], (BATCH, SEQ, D_MODEL), 1.0),
        "rel_bias": nrm(ks[1], (N_BUCKETS, N_Q_HEADS), 0.5),
        "mix_norm_g": 1.0 + nrm(ks[2], (DEPTH, D_MODEL), 0.02),
        "w_in": nrm(ks[3], (DEPTH, D_MODEL, IN_COLS), D_MODEL ** -0.5),
        "cmp_pos": nrm(ks[4], (DEPTH, 2, CMP_LEN, HEAD_DIM), 0.1),
        "cmp_w1": nrm(ks[5], (DEPTH, 2, CMP_LEN * HEAD_DIM, HEAD_DIM), (CMP_LEN * HEAD_DIM) ** -0.5),
        "cmp_w2": nrm(ks[6], (DEPTH, 2, HEAD_DIM, HEAD_DIM), HEAD_DIM ** -0.5),
        "conv_w": nrm(ks[7], (DEPTH, CONV_TAPS, CONV_CHANNELS), CONV_TAPS ** -0.5),
        "conv_b": nrm(ks[8], (DEPTH, CONV_CHANNELS), 0.01),
        "conv_ln_g": 1.0 + nrm(ks[9], (DEPTH, CONV_CHANNELS), 0.02),
        "conv_ln_b": nrm(ks[10], (DEPTH, CONV_CHANNELS), 0.01),
        "w_out": nrm(ks[11], (DEPTH, D_MIX, D_MODEL), D_MIX ** -0.5),
        "ffn_norm_g": 1.0 + nrm(ks[12], (DEPTH, D_MODEL), 0.02),
        "w_up": nrm(ks[13], (DEPTH, D_MODEL, 2 * D_FF), D_MODEL ** -0.5),
        "ffn_conv_w": nrm(ks[14], (DEPTH, FFN_CONV_TAPS, 2 * D_FF), FFN_CONV_TAPS ** -0.5),
        "ffn_conv_b": nrm(ks[15], (DEPTH, 2 * D_FF), 0.01),
        "w_down": nrm(ks[16], (DEPTH, D_FF, D_MODEL), D_FF ** -0.5),
        "final_norm_g": 1.0 + nrm(ks[17], (D_MODEL,), 0.02),
    }

def first_block(x, rel_bias, mix_norm_g, w_in, cmp_pos, cmp_w1, cmp_w2, conv_w, conv_b,
              conv_ln_g, conv_ln_b, w_out, ffn_norm_g, w_up, ffn_conv_w, ffn_conv_b,
              w_down, final_norm_g):
    b, t_len, _ = x.shape
    splits = [Q_COLS, Q_COLS + KV_COLS, Q_COLS + KV_COLS + GATE_COLS]
    for l in range(DEPTH):
        h = rms_norm(x, mix_norm_g[l])
        proj = h @ w_in[l]
        q, kv, gate_logits, conv_in = jnp.split(proj, splits, axis=-1)
        q = q.reshape(b, t_len, N_KV_HEADS, GQA_GROUP, HEAD_DIM)
        kv = kv.reshape(b, t_len, N_BRANCH, 2, N_KV_HEADS, HEAD_DIM)
        gates = jax.nn.sigmoid(gate_logits).reshape(b, t_len, N_KV_HEADS, GQA_GROUP, N_BRANCH)
        attn = nsa_attention(q, kv, gates, rel_bias, cmp_pos[l], cmp_w1[l], cmp_w2[l])
        conv = conformer_conv(conv_in, conv_w[l], conv_b[l], conv_ln_g[l], conv_ln_b[l])
        x = x + jnp.concatenate([attn, conv], axis=-1) @ w_out[l]
        h = rms_norm(x, ffn_norm_g[l])
        x = x + conv_glu_ffn(h, w_up[l], ffn_conv_w[l], ffn_conv_b[l], w_down[l])
    return rms_norm(x, final_norm_g)


MLA_HEADS = 8
MLA_Q_RANK = 512
MLA_KV_RANK = 256
MLA_NOPE_DIM = 128
MLA_ROPE_DIM = 64
MLA_QK_DIM = MLA_NOPE_DIM + MLA_ROPE_DIM
MLA_V_DIM = 128
MLA_WIDTH = MLA_HEADS * MLA_V_DIM
ROPE_THETA = 10000.0
Q_BLOCK_2 = 128
NEG_INF_2 = -1e30

GLA_HEADS = 4
GLA_VALUE_DIM = D_MODEL // 2
GLA_KEY_DIM = GLA_VALUE_DIM // 2
GLA_HEAD_K = GLA_KEY_DIM // GLA_HEADS
GLA_HEAD_V = GLA_VALUE_DIM // GLA_HEADS
GLA_GATE_RANK = 16
GLA_GATE_TAU = 16.0
GLA_CHUNK = 64

MIX_WIDTH = MLA_WIDTH + GLA_VALUE_DIM
IN_SPLITS = (MLA_Q_RANK, MLA_KV_RANK, MLA_ROPE_DIM,
             GLA_KEY_DIM, GLA_KEY_DIM, GLA_VALUE_DIM, GLA_GATE_RANK, GLA_VALUE_DIM)
IN_COLS_2 = sum(IN_SPLITS)

D_FF_2 = -(-8 * D_MODEL // (3 * 256)) * 256
N_MOD = 6
RMS_EPS = 1e-6


def rms_norm_2(x, w, eps=RMS_EPS):
    xf = x.astype(jnp.float32)
    y = xf * lax.rsqrt(jnp.mean(xf * xf, axis=-1, keepdims=True) + eps)
    return (y * w.astype(jnp.float32)).astype(x.dtype)

def split_cols(z, sizes):
    out, start = [], 0
    for s in sizes:
        out.append(z[..., start:start + s])
        start += s
    return out

def rope_cos_sin(positions, dim):
    inv_freq = 1.0 / (ROPE_THETA ** (jnp.arange(0, dim, 2, dtype=jnp.float32) / dim))
    ang = positions.astype(jnp.float32)[..., None] * inv_freq
    return jnp.cos(ang), jnp.sin(ang)

def apply_rope(x, cos, sin):
    half = x.shape[-1] // 2
    x1 = x[..., :half].astype(jnp.float32)
    x2 = x[..., half:].astype(jnp.float32)
    out = jnp.concatenate([x1 * cos - x2 * sin, x2 * cos + x1 * sin], axis=-1)
    return out.astype(x.dtype)

def mla_mixer(c_q, c_kv, k_rope, positions, g_q, w_uq, g_kv, w_uk, w_uv):
    B, S, _ = c_q.shape
    H = MLA_HEADS
    q = (rms_norm_2(c_q, g_q) @ w_uq).reshape(B, S, H, MLA_QK_DIM)
    c_kv = rms_norm_2(c_kv, g_kv)
    k_nope = (c_kv @ w_uk).reshape(B, S, H, MLA_NOPE_DIM)
    v = (c_kv @ w_uv).reshape(B, S, H, MLA_V_DIM)
    cos, sin = rope_cos_sin(positions, MLA_ROPE_DIM)
    q_rope = apply_rope(q[..., MLA_NOPE_DIM:], cos[:, :, None, :], sin[:, :, None, :])
    k_rope = apply_rope(k_rope, cos, sin)
    q = jnp.concatenate([q[..., :MLA_NOPE_DIM], q_rope], axis=-1) * (MLA_QK_DIM ** -0.5)
    k = jnp.concatenate(
        [k_nope, jnp.broadcast_to(k_rope[:, :, None, :], (B, S, H, MLA_ROPE_DIM))], axis=-1)
    q = q.transpose(0, 2, 1, 3)
    k = k.transpose(0, 2, 1, 3)
    v = v.transpose(0, 2, 1, 3)
    nb = S // Q_BLOCK_2
    q_blocks = q.reshape(B, H, nb, Q_BLOCK_2, MLA_QK_DIM).transpose(2, 0, 1, 3, 4)
    k_pos = jnp.arange(S)

    def attend(args):
        q_blk, blk = args
        q_pos = blk * Q_BLOCK_2 + jnp.arange(Q_BLOCK_2)
        s = jnp.einsum('bhqd,bhkd->bhqk', q_blk, k).astype(jnp.float32)
        s = jnp.where(k_pos[None, :] <= q_pos[:, None], s, NEG_INF_2)
        p = jax.nn.softmax(s, axis=-1).astype(v.dtype)
        return jnp.einsum('bhqk,bhkd->bhqd', p, v)

    o = lax.map(attend, (q_blocks, jnp.arange(nb)))
    return o.transpose(1, 0, 3, 2, 4).reshape(B, S, MLA_WIDTH)

def gla_mixer(q, k, v, a_lr, r, w_gate_up, b_gate, g_gla):
    B, S, _ = q.shape
    H, dk, dv, C = GLA_HEADS, GLA_HEAD_K, GLA_HEAD_V, GLA_CHUNK
    N = S // C
    f32 = jnp.float32
    log_a = jax.nn.log_sigmoid((a_lr @ w_gate_up + b_gate).astype(f32)) / GLA_GATE_TAU

    def chunked(t, d):
        return t.reshape(B, N, C, H, d).transpose(0, 3, 1, 2, 4).astype(f32)

    qc = chunked(q, dk) * (dk ** -0.5)
    kc = chunked(k, dk)
    vc = chunked(v, dv)
    bc = jnp.cumsum(chunked(log_a, dk), axis=3)
    b_last = bc[:, :, :, -1:, :]
    q_dec = qc * jnp.exp(bc)
    k_inv = kc * jnp.exp(-bc)
    k_dec = kc * jnp.exp(b_last - bc)
    causal = jnp.tril(jnp.ones((C, C), dtype=bool))
    attn = jnp.einsum('bhncd,bhnjd->bhncj', q_dec, k_inv)
    attn = jnp.where(causal, attn, 0.0)
    o_intra = jnp.einsum('bhncj,bhnjv->bhncv', attn, vc)
    d_state = jnp.einsum('bhncd,bhncv->bhndv', k_dec, vc)
    decay = jnp.exp(b_last[:, :, :, 0, :])

    def step(state, inp):
        q_n, ds_n, decay_n = inp
        o_n = jnp.einsum('bhcd,bhdv->bhcv', q_n, state)
        state = decay_n[..., None] * state + ds_n
        return state, o_n

    init = jnp.zeros((B, H, dk, dv), f32)
    _, o_inter = lax.scan(step, init, (jnp.moveaxis(q_dec, 2, 0),
                                       jnp.moveaxis(d_state, 2, 0),
                                       jnp.moveaxis(decay, 2, 0)))
    o = o_intra + jnp.moveaxis(o_inter, 0, 2)
    o = o.transpose(0, 2, 3, 1, 4).reshape(B, S, H, dv)
    o = rms_norm_2(o, g_gla) * jax.nn.silu(r.reshape(B, S, H, dv).astype(f32))
    return o.reshape(B, S, GLA_VALUE_DIM).astype(q.dtype)

def second_inputs(seed: int = 0) -> dict:
    key = jax.random.key(seed)
    ks = jax.random.split(key, 24)
    f32 = jnp.float32
    L = DEPTH

    def nrm(k, shape, scale):
        return jax.random.normal(k, shape, f32) * scale

    def gain(k, shape):
        return 1.0 + 0.02 * jax.random.normal(k, shape, f32)

    offsets = jax.random.randint(ks[2], (BATCH, 1), 0, 4096, dtype=jnp.int32)
    positions = offsets + jnp.arange(SEQ, dtype=jnp.int32)[None, :]
    return {
        'x': nrm(ks[0], (BATCH, SEQ, D_MODEL), 1.0),
        'c': nrm(ks[1], (BATCH, D_MODEL), 1.0),
        'positions': positions,
        'w_ada': nrm(ks[3], (L, D_MODEL, N_MOD * D_MODEL), D_MODEL ** -0.5),
        'b_ada': nrm(ks[4], (L, N_MOD * D_MODEL), 0.01),
        'g_pre_mix': gain(ks[5], (L, D_MODEL)),
        'g_post_mix': gain(ks[6], (L, D_MODEL)),
        'w_in': nrm(ks[7], (L, D_MODEL, IN_COLS_2), D_MODEL ** -0.5),
        'g_q': gain(ks[8], (L, MLA_Q_RANK)),
        'w_uq': nrm(ks[9], (L, MLA_Q_RANK, MLA_HEADS * MLA_QK_DIM), MLA_Q_RANK ** -0.5),
        'g_kv': gain(ks[10], (L, MLA_KV_RANK)),
        'w_uk': nrm(ks[11], (L, MLA_KV_RANK, MLA_HEADS * MLA_NOPE_DIM), MLA_KV_RANK ** -0.5),
        'w_uv': nrm(ks[12], (L, MLA_KV_RANK, MLA_HEADS * MLA_V_DIM), MLA_KV_RANK ** -0.5),
        'w_gate_up': nrm(ks[13], (L, GLA_GATE_RANK, GLA_KEY_DIM), GLA_GATE_RANK ** -0.5),
        'b_gate': nrm(ks[14], (L, GLA_KEY_DIM), 0.1),
        'g_gla': gain(ks[15], (L, GLA_HEAD_V)),
        'w_out': nrm(ks[16], (L, MIX_WIDTH, D_MODEL), MIX_WIDTH ** -0.5),
        'g_pre_ffn': gain(ks[17], (L, D_MODEL)),
        'g_post_ffn': gain(ks[18], (L, D_MODEL)),
        'w_ffn_gate': nrm(ks[19], (L, D_MODEL, D_FF_2), D_MODEL ** -0.5),
        'w_ffn_up': nrm(ks[20], (L, D_MODEL, D_FF_2), D_MODEL ** -0.5),
        'w_ffn_down': nrm(ks[21], (L, D_FF_2, D_MODEL), D_FF_2 ** -0.5),
    }

def second_block(x, c, positions, w_ada, b_ada, g_pre_mix, g_post_mix, w_in, g_q, w_uq,
              g_kv, w_uk, w_uv, w_gate_up, b_gate, g_gla, w_out, g_pre_ffn, g_post_ffn,
              w_ffn_gate, w_ffn_up, w_ffn_down):
    for l in range(DEPTH):
        ada = jax.nn.silu(c) @ w_ada[l] + b_ada[l]
        shift_m, scale_m, gate_m, shift_f, scale_f, gate_f = [
            t[:, None, :] for t in jnp.split(ada, N_MOD, axis=-1)]

        h = rms_norm_2(x, g_pre_mix[l]) * (1.0 + scale_m) + shift_m
        z = h @ w_in[l]
        c_q, c_kv, k_rope, q_g, k_g, v_g, a_g, r_g = split_cols(z, IN_SPLITS)
        o_mla = mla_mixer(c_q, c_kv, k_rope, positions, g_q[l], w_uq[l],
                          g_kv[l], w_uk[l], w_uv[l])
        o_gla = gla_mixer(q_g, k_g, v_g, a_g, r_g, w_gate_up[l], b_gate[l], g_gla[l])
        o = jnp.concatenate([o_mla, o_gla], axis=-1) @ w_out[l]
        x = x + gate_m * rms_norm_2(o, g_post_mix[l])

        h = rms_norm_2(x, g_pre_ffn[l]) * (1.0 + scale_f) + shift_f
        f = (jax.nn.silu(h @ w_ffn_gate[l]) * (h @ w_ffn_up[l])) @ w_ffn_down[l]
        x = x + gate_f * rms_norm_2(f, g_post_ffn[l])
    return x


def setup_inputs(seed=0):
    out = dict(first_inputs(seed))
    for name, value in second_inputs(seed + 1).items():
        if name != "x":
            out[name + "_2"] = value
    return out


def reference(
    x, rel_bias, mix_norm_g, w_in, cmp_pos, cmp_w1, cmp_w2, conv_w, conv_b, conv_ln_g,
    conv_ln_b, w_out, ffn_norm_g, w_up, ffn_conv_w, ffn_conv_b, w_down, final_norm_g, c_2,
    positions_2, w_ada_2, b_ada_2, g_pre_mix_2, g_post_mix_2, w_in_2, g_q_2, w_uq_2, g_kv_2,
    w_uk_2, w_uv_2, w_gate_up_2, b_gate_2, g_gla_2, w_out_2, g_pre_ffn_2, g_post_ffn_2,
    w_ffn_gate_2, w_ffn_up_2, w_ffn_down_2,
):
    x = first_block(
        x, rel_bias, mix_norm_g, w_in, cmp_pos, cmp_w1, cmp_w2, conv_w, conv_b, conv_ln_g,
        conv_ln_b, w_out, ffn_norm_g, w_up, ffn_conv_w, ffn_conv_b, w_down, final_norm_g,
    )
    return second_block(
        x, c_2, positions_2, w_ada_2, b_ada_2, g_pre_mix_2, g_post_mix_2, w_in_2, g_q_2, w_uq_2,
        g_kv_2, w_uk_2, w_uv_2, w_gate_up_2, b_gate_2, g_gla_2, w_out_2, g_pre_ffn_2,
        g_post_ffn_2, w_ffn_gate_2, w_ffn_up_2, w_ffn_down_2,
    )


_drawn_inputs = setup_inputs


def setup_inputs(seed=0):
    import zlib

    import numpy as np

    out = dict(_drawn_inputs(seed))
    spreads = {}
    factors = {'mix_norm_g': 4.098,
     'conv_b': 4.257,
     'conv_ln_g': 4.16,
     'conv_ln_b': 8.0,
     'ffn_norm_g': 3.388,
     'ffn_conv_b': 6.464,
     'b_ada_2': 2.714,
     'g_pre_mix_2': 3.229,
     'g_post_mix_2': 5.002,
     'g_q_2': 8.0,
     'g_kv_2': 8.0,
     'g_gla_2': 18.528,
     'g_pre_ffn_2': 4.539,
     'g_post_ffn_2': 21.602}
    for name, (base, spread) in spreads.items():
        noise = np.random.default_rng([zlib.crc32(name.encode()), seed]).standard_normal(out[name].shape)
        drawn = base * np.exp(spread * noise) if base else spread * noise
        out[name] = __import__('jax').numpy.asarray(drawn.astype(out[name].dtype))
    for name, factor in factors.items():
        out[name] = (out[name] * factor).astype(out[name].dtype)
    return out
```

```python
import concourse.bass as bass
from concourse import mybir
from contextlib import ExitStack
import numpy as np

F32 = mybir.dt.float32
F32R = mybir.dt.float32r
I32 = mybir.dt.int32
ALU = mybir.AluOpType
ACT = mybir.ActivationFunctionType
AX = mybir.AxisListType

P = 128
T = 256
TT = T // P
D = 2048
KD = D // P
HALF = 1024

HEADS, KV_HEADS, GQA, DH = 16, 4, 4, 64
CMP_LEN, CMP_STRIDE = 32, 16
NCMP = T // CMP_STRIDE - CMP_LEN // CMP_STRIDE + 1
N_BRANCH = 3
BUCKETS, MAX_DISTANCE = 32, 128
CONV_TAPS, CONV_CH = 31, 1024
CONV_TILES = CONV_CH // P
DFF = 5632
FF_TILES = DFF // P
FF_HALF = FF_TILES // 2
EPS = 1e-6
MASKED = -1e30

MLA_HEADS, Q_RANK, KV_RANK, NOPE, ROPE = 8, 512, 256, 128, 64
ROPE2 = ROPE // 2
MLA_SCALE = float(np.float32((NOPE + ROPE) ** -0.5))
GLA_HEADS, GLA_K, GLA_V, GLA_CHUNK, GATE_RANK = 4, 128, 256, 64, 16
N_CHUNKS = T // GLA_CHUNK
GLA_TAU = 16.0

CHUNK = 1024
RAW_SLOTS = 7
PART_SLOTS = 4
AHEAD = PART_SLOTS - 1



def q_columns():
    cols = []
    for pair in range(KV_HEADS // 2):
        for g in range(GQA):
            for hk in (2 * pair, 2 * pair + 1):
                h = hk * GQA + g
                cols += range(h * DH, (h + 1) * DH)
    return cols


def query_place(h):
    hk, g = divmod(h, GQA)
    return (hk // 2) * GQA + g, DH * (hk % 2)


class Plan:

    def __init__(self):
        self.chunks = []
        self.kinds = []
        self.groups = {}
        self.ada = [(v, half, kt) for v in range(6) for half in range(2) for kt in range(KD)]
        self.rate = 0.0
        self.due = 0.0
        self.open = False

    def new_chunk(self, kind):
        self.chunks.append([])
        self.kinds.append(kind)
        self.open = kind == "split"

    def put_ada(self):
        v, half, kt = self.ada.pop(0)
        self.new_chunk("ada")
        self.chunks[-1].append(("w_ada", kt, v * D + half * HALF, HALF))

    def piece(self, mat, kt, col, n):
        used = sum(x[3] for x in self.chunks[-1]) if self.open else CHUNK
        if used + n > CHUNK:
            self.due += self.rate
            while self.due >= 1 and self.ada:
                self.put_ada()
                self.due -= 1
            self.new_chunk("split")
            used = 0
        self.chunks[-1].append((mat, kt, col, n))
        return len(self.chunks) - 1, used, kt

    def project(self, key, mat, col, n, k0=0, nk=KD):
        self.groups[key] = [self.piece(mat, kt, col, n) for kt in range(k0, k0 + nk)]

    def raw(self, key, mat, pieces):
        self.groups[key] = []
        for c in range(pieces):
            self.new_chunk("raw")
            self.chunks[-1].append((mat, 0, c * CHUNK, CHUNK))
            self.groups[key].append(len(self.chunks) - 1)

    def finish_ada(self, left):
        while len(self.ada) > left:
            self.put_ada()


def make_plan():
    p = Plan()
    kv = HEADS * DH
    for s in range(2):
        for j in range(2):
            p.project(("cmp", s, j), "w_in", kv + 256 * s + P * j, P)
    p.raw("cmp_w1", "cmp_w1", 2 * CMP_LEN * DH // CHUNK)
    for br in (1, 2):
        for j in range(2):
            p.project(("key", br, j), "w_in", kv + 512 * br + P * j, P)
    for j in range(8):
        p.project(("query", j), "w_in", P * j, P)
    p.project("value", "w_in_v", 0, 512)
    gates = kv + N_BRANCH * 512
    p.project("gates", "w_in", gates, N_BRANCH * HEADS)
    conv = gates + N_BRANCH * HEADS
    for j in range(CONV_TILES):
        p.project(("conv_a", j), "w_in", conv + P * j, P)
        p.project(("conv_g", j), "w_in", conv + CONV_CH + P * j, P)
    for n in range(4):
        p.project(("out1", n), "w_out", 512 * n, 512)
        p.rate = 0.68
    for half in range(2):
        for j in range(FF_HALF * half, FF_HALF * (half + 1)):
            p.project(("up_a", j), "w_up", P * j, P)
            p.project(("up_g", j), "w_up", DFF + P * j, P)
        for n in range(4):
            p.project(("down1", half, n), "w_down", 512 * n, 512, FF_HALF * half, FF_HALF)
    p.finish_ada(0)
    p.rate = 0.0
    p.project("c_q", "w_in_2", 0, Q_RANK)
    p.project("c_kv", "w_in_2_kv", 0, KV_RANK + ROPE + GATE_RANK)
    at = Q_RANK + KV_RANK + ROPE
    for h in range(GLA_HEADS):
        p.project(("gla_q", h), "w_in_2", at + P * h, P)
    at += GLA_HEADS * GLA_K
    for h in range(GLA_HEADS):
        p.project(("gla_k", h), "w_in_2", at + P * h, P)
    at += GLA_HEADS * GLA_K
    for n in range(2):
        p.project(("gla_v", n), "w_in_2", at + 512 * n, 512)
    at += GLA_HEADS * GLA_V + GATE_RANK
    for n in range(2):
        p.project(("gla_r", n), "w_in_2", at + 512 * n, 512)
    p.project("q_rope", "w_uq_rope", 0, MLA_HEADS * ROPE, 0, Q_RANK // P)
    for h in range(MLA_HEADS):
        p.project(("q_nope", h), "w_uq_nope", P * h, P, 0, Q_RANK // P)
    for h in range(MLA_HEADS):
        p.project(("k_nope", h), "w_uk", P * h, P, 0, KV_RANK // P)
    for n in range(2):
        p.project(("mla_v", n), "w_uv", 512 * n, 512, 0, KV_RANK // P)
    for n in range(4):
        p.project(("out2", n), "w_out_2", 512 * n, 512)
    for half in range(2):
        for j in range(FF_HALF * half, FF_HALF * (half + 1)):
            p.project(("gate", j), "w_ffn_gate", P * j, P)
            p.project(("up", j), "w_ffn_up", P * j, P)
        for n in range(4):
            p.project(("down2", half, n), "w_ffn_down", 512 * n, 512, FF_HALF * half, FF_HALF)
    return p


def chunk_widths(plan):
    return [sum(x[3] for x in c) for c in plan.chunks]



def fields(sizes):
    at, out = 0, {}
    for name, n in sizes:
        out[name] = (at, at + n)
        at += n
    out["_width"] = at
    return out


LASTING = fields([
    ("identity", P), ("ones", P), ("causal", 2 * P), ("mix_norm_g", KD), ("ffn_norm_g", KD),
    ("final_norm_g", KD), ("g_pre_mix", KD), ("g_post_mix", KD), ("g_pre_ffn", KD),
    ("g_post_ffn", KD), ("b_ada", 6 * KD), ("c", KD), ("ffn_conv_w", 3 * 2 * FF_TILES),
    ("ffn_conv_b", 2 * FF_TILES), ("g_q", Q_RANK // P), ("g_kv", KV_RANK // P),
    ("b_gate", GLA_HEADS), ("g_gla", GLA_V // P),
])
N_DIST = 2 * T + P
DIST0 = 2 * P - 1
PHASE1 = fields([
    ("one_hot", N_DIST), ("rel_bias", HEADS), ("cmp_w2", 2 * DH), ("cmp_pos", 2 * CMP_LEN),
    ("conv_w", CONV_TILES * CONV_TAPS), ("conv_b", CONV_TILES), ("conv_ln_g", CONV_TILES),
    ("conv_ln_b", CONV_TILES), ("any_block", TT),
])
PHASE2 = fields([
    ("w_gate_up", GLA_HEADS * GLA_K), ("chunk_restart", T), ("inv_freq", ROPE2),
    ("chunk_causal", P),
])



class Line:

    def __init__(self, sem, name):
        self.sem, self.name, self.count, self.seen, self.steps = sem, name, 0, {}, []

    def wait(self, *tokens):
        for t in tokens:
            if t is None:
                continue
            if isinstance(t, list):
                self.wait(*t)
                continue
            name, sem, value = t
            if self.seen.get(name, 0) < value:
                self.seen[name] = value
                self.steps.append(lambda e, s=sem, v=value: e.wait_ge(s, v))

    def do(self, step, *after, signal=True):
        self.wait(*after)
        if not signal:
            self.steps.append(step)
            return None
        self.count += 1
        self.steps.append(lambda e: step(e).then_inc(self.sem, 1))
        return self.name, self.sem, self.count

    def play(self, engine):
        for step in self.steps:
            step(engine)


def two_blocks(nc, WEIGHTS, X, PARAMS, PARAMS1, PARAMS2, POSITIONS, OUT):
    plan = make_plan()
    widths = chunk_widths(plan)
    starts = [P * s for s in np.concatenate([[0], np.cumsum(widths)]).tolist()]

    ctx = ExitStack()
    with ctx:
        base = -(-nc.sbuf_base // 64) * 64
        at = {}
        cursor = base
        LAST_BYTES = -(-LASTING["_width"] * 4 // 64) * 64
        PHASE_BYTES = -(-max(PHASE1["_width"], PHASE2["_width"]) * 4 // 64) * 64
        for name, size in (
            ("raw", RAW_SLOTS * CHUNK * 4), ("hi", PART_SLOTS * CHUNK * 4), ("lo", PART_SLOTS * CHUNK * 4),
            ("h", 2 * KD * T * 4), ("mid", 2 * FF_HALF * T * 4), ("x", TT * D * 4), ("wide", TT * D * 4),
            ("acc", 2 * HALF * 4), ("last", LAST_BYTES), ("phase", PHASE_BYTES), ("stat", 2048),
        ):
            at[name] = cursor
            cursor += size
        at["free"] = cursor
        assert nc.sbuf_usable_end - cursor >= 19 * 1024, nc.sbuf_usable_end - cursor

        def place(name, region, offset, shape, dt=F32):
            return nc.alloc_sbuf_tensor_at(name, shape, dt, offset=at[region] + offset)

        raw = place("raw", "raw", 0, [P, RAW_SLOTS, CHUNK])
        w_hi = place("w_hi", "hi", 0, [P, PART_SLOTS, CHUNK], F32R)
        w_lo = place("w_lo", "lo", 0, [P, PART_SLOTS, CHUNK], F32R)
        h_hi = place("h_hi", "h", 0, [P, KD, T], F32R)
        h_lo = place("h_lo", "h", KD * T * 4, [P, KD, T], F32R)
        mix_hi = place("mix_hi", "mid", 0, [P, KD, T], F32R)
        mix_lo = place("mix_lo", "mid", KD * T * 4, [P, KD, T], F32R)
        ff_hi = place("ff_hi", "mid", 0, [P, FF_HALF, T], F32R)
        ff_lo = place("ff_lo", "mid", FF_HALF * T * 4, [P, FF_HALF, T], F32R)
        mid_tail = 2 * KD * T * 4
        x = place("x", "x", 0, [P, TT, D])
        wide = place("wide", "wide", 0, [P, TT, D])
        ada_acc = place("ada_acc", "acc", 0, [P, 2, HALF])
        lasting = place("lasting", "last", 0, [P, LASTING["_width"]])
        stat = place("stat", "stat", 0, [P, 512])

        def param(name):
            a, b = LASTING[name]
            return lasting[:, a:b]

        identity, ones, causal = param("identity"), param("ones"), param("causal")

        stat_used = [0]

        def stats(n):
            a = stat_used[0]
            stat_used[0] += n
            assert stat_used[0] <= 512
            return stat[:, a:a + n]

        banks = [ctx.enter_context(nc.psum_tensor(f"bank{b}", [P, 512], F32)) for b in range(8)]
        bank_read = [None] * 8
        GROUP_BANKS = ((0, 1), (2, 3))
        TILE_BANKS = (4, 5)
        ODD_BANKS = (6, 7)

        def sem(name):
            return ctx.enter_context(nc.semaphore(name))

        PE = Line(sem("pe_done"), "pe")
        DVE = Line(sem("dve_done"), "dve")
        ACTE = Line(sem("act_done"), "act")
        POOL = Line(sem("pool_done"), "pool")
        SP = Line(sem("sp_done"), "sp")
        raw_sems = [sem(f"raw_landed{i}") for i in range(RAW_SLOTS)]

        def load(name, dst, src, *after, line=None):
            s = sem(name)
            (line or SP).wait(*after)
            (line or SP).steps.append(lambda e: e.dma_start(dst, src).then_inc(s, 16))
            return name, s, 16

        minus_half = stats(1)
        minus_half_done = POOL.do(lambda e: e.memset(minus_half, -0.5))

        released = [None] * len(widths)
        part_of = {}
        part_used = []
        pieces_left = [len(c) for c in plan.chunks]
        state = {"loaded": 0, "prepared": 0, "ada": None, "ada_slot": [None, None]}
        deferred = []

        def arrived(i):
            return f"raw{i % RAW_SLOTS}", raw_sems[i % RAW_SLOTS], 16 * (i // RAW_SLOTS + 1)

        def load_chunks():
            while state["loaded"] < len(widths):
                i = state["loaded"]
                if i >= RAW_SLOTS:
                    if released[i - RAW_SLOTS] is None:
                        return
                    SP.wait(released[i - RAW_SLOTS])
                src = WEIGHTS[starts[i]:starts[i + 1]].rearrange("(p w) -> p w", p=P)
                dst = raw[:, i % RAW_SLOTS, 0:widths[i]]
                SP.steps.append(lambda e, d=dst, s=src, k=i % RAW_SLOTS: e.dma_start(d, s).then_inc(raw_sems[k], 16))
                state["loaded"] += 1

        def split(dst_hi, dst_lo, src, *after):
            hi = ACTE.do(lambda e: e.activation(dst_hi, src, ACT.Copy), *after)
            return DVE.do(lambda e: e.tensor_tensor(dst_lo, src, dst_hi.bitcast(F32), ALU.subtract), hi)

        def prepare(upto):
            while state["prepared"] <= min(upto, len(widths) - 1):
                i = state["prepared"]
                src = raw[:, i % RAW_SLOTS, 0:widths[i]]
                if plan.kinds[i] == "split":
                    n = len(part_of)
                    slot_free = part_used[n - PART_SLOTS] if n >= PART_SLOTS else None
                    slot = n % PART_SLOTS
                    token = split(w_hi[:, slot, 0:widths[i]], w_lo[:, slot, 0:widths[i]], src, arrived(i), slot_free)
                    part_of[i] = slot, token
                    released[i] = token
                elif plan.kinds[i] == "ada":
                    released[i] = ada_step(i, src)
                state["prepared"] += 1
                load_chunks()

        ada_T = place("ada_T", "phase", 0, [1, 1]) if False else None
        vectors = {}

        def ada_step(i, src):
            _, kt, col, _ = plan.chunks[i][0]
            v, half = col // D, (col % D) // HALF
            slot = (2 * v + half) % 2
            acc, s = ada_acc[:, slot, :], silu_c[:, kt:kt + 1]
            if kt == 0:
                t = DVE.do(lambda e: e.tensor_scalar(acc, src, s, None, ALU.mult), arrived(i),
                           state["ada_slot"][slot], silu_c_done)
            else:
                t = DVE.do(lambda e: e.scalar_tensor_tensor(acc, src, s, acc, ALU.mult, ALU.add),
                           arrived(i), state["ada"])
            state["ada"] = t
            if kt == KD - 1:
                deferred.append([AHEAD + 1, v, half, slot, t])
                state["ada_slot"][slot] = "pending"
            return t

        def ada_reduce(v, half, slot, acc_done):
            b = ODD_BANKS[0]
            n = HALF // P
            for k in range(n):
                t = PE.do(lambda e, k=k: e.matmul(banks[b][:, k:k + 1], ada_acc[:, slot, k * P:(k + 1) * P],
                                                  ones[:, 0:1], start=True, stop=True),
                          acc_done, bank_read[b], signal=k == n - 1)
            state["ada_slot"][slot] = t
            lo, hi = LASTING["b_ada"][0] + v * KD + half * n, LASTING["b_ada"][0] + v * KD + (half + 1) * n
            t = DVE.do(lambda e: e.tensor_tensor(lasting[:, lo:hi], banks[b][:, 0:n], lasting[:, lo:hi], ALU.add), t)
            bank_read[b] = t
            vectors[v, half] = t

        def run_deferred(now=False):
            while deferred and (now or deferred[0][0] <= 0):
                ada_reduce(*deferred.pop(0)[1:])
            for d in deferred:
                d[0] -= 1

        def piece_used(i, token):
            pieces_left[i] -= 1
            if pieces_left[i] == 0:
                part_used.append(token)
                run_deferred()

        def parts(i, off, n):
            slot, _ = part_of[i]
            return w_hi[:, slot, off:off + n], w_lo[:, slot, off:off + n]

        def projection(key, n, out_of, outs, act_hi, act_lo, after, tile):
            got = plan.groups[key]
            last = None
            for at_piece, (i, off, kt) in enumerate(got):
                prepare(i)
                k = kt - got[0][2]
                hi, lo = parts(i, off, n)
                ends = pieces_left[i] == 1
                first_k, last_k = at_piece == 0, at_piece == len(got) - 1
                need = after(k) if callable(after) else after
                for o, out in enumerate(outs):
                    if tile:
                        a_hi, a_lo = act_hi[:, k, :], act_lo[:, k, :]
                        trio = ((hi, a_hi), (hi, a_lo), (lo, a_hi))
                    else:
                        a_hi, a_lo = act_hi[:, k, o * P:(o + 1) * P], act_lo[:, k, o * P:(o + 1) * P]
                        trio = ((a_hi, hi), (a_hi, lo), (a_lo, hi))
                    for q, (s, m) in enumerate(trio):
                        final = o == len(outs) - 1 and q == 2
                        last = PE.do(lambda e, s=s, m=m, out=out, st=first_k and q == 0, en=last_k and q == 2:
                                     e.matmul(out, s, m, start=st, stop=en),
                                     part_of[i][1], need, [bank_read[b] for b in out_of] if first_k else None,
                                     signal=final and (ends or last_k))
                if ends:
                    piece_used(i, last)
                    prepare(i + AHEAD)
                else:
                    pieces_left[i] -= 1
            return last

        turn = {"tile": 0, "group": 0, "odd": 0}

        def tile(key, act_hi, act_lo, after):
            b = TILE_BANKS[turn["tile"] % 2]
            turn["tile"] += 1
            out = banks[b][:, 0:T]
            return out, b, projection(key, P, [b], [out], act_hi, act_lo, after, True)

        def group(key, n, act_hi, act_lo, after):
            pair = GROUP_BANKS[turn["group"] % 2]
            turn["group"] += 1
            outs = [banks[b][:, 0:n] for b in pair]
            return outs, pair, projection(key, n, list(pair), outs, act_hi, act_lo, after, False)

        def odd_bank():
            b = ODD_BANKS[turn["odd"] % 2]
            turn["odd"] += 1
            return b

        def rms_factors(src, n, junk, after):
            out, tokens, sq = stats(TT), [], stats(TT)
            t_act = None
            for tt in range(TT):
                t = t_act = ACTE.do(lambda e, tt=tt: e.activation(junk(tt), src(tt), ACT.Square, accum_out=sq[:, tt:tt + 1]),
                            after(tt), t_act)
                t = POOL.do(lambda e, tt=tt: e.tensor_scalar(out[:, tt:tt + 1], sq[:, tt:tt + 1], 1.0 / n, EPS,
                                                             ALU.mult, ALU.add), t)
                t = POOL.do(lambda e, tt=tt: e.tensor_tensor(out[:, tt:tt + 1], out[:, tt:tt + 1], minus_half, ALU.pow), t, minus_half_done)
                tokens.append(t)
            return out, tokens

        def transpose_split(src, nk, gain, shift, dst_hi, dst_lo, work, work_free, after, dst_free=None):
            done = []
            for k in range(nk):
                b = odd_bank()
                for tt in range(TT):
                    t = PE.do(lambda e, tt=tt, k=k, b=b: e.transpose(banks[b][:, tt * P:(tt + 1) * P], src(tt, k), identity),
                              after(tt, k), bank_read[b], signal=tt == TT - 1)
                tmp = work[:, k % 2, :]
                free = work_free[k % 2]
                g = gain(k)
                if shift is None:
                    t = DVE.do(lambda e, b=b, tmp=tmp, g=g: e.tensor_scalar(tmp, banks[b][:, 0:T], g, None, ALU.mult), t, free)
                else:
                    t = DVE.do(lambda e, b=b, tmp=tmp, g=g, s=shift(k): e.tensor_scalar(tmp, banks[b][:, 0:T], g, s, ALU.mult, ALU.add), t, free)
                bank_read[b] = t
                t = split(dst_hi(k), dst_lo(k), tmp, t, dst_free)
                work_free[k % 2] = t
                done.append(t)
            return done

        def norm_to_h(after, gain, shift, work, work_free, h_free, wide_free):
            rs, rs_done = rms_factors(lambda tt: x[:, tt, :], D, lambda tt: wide[:, tt, :],
                                      lambda tt: [after[tt], wide_free])
            scaled = [DVE.do(lambda e, tt=tt: e.tensor_scalar(wide[:, tt, :], x[:, tt, :], rs[:, tt:tt + 1], None, ALU.mult),
                             rs_done[tt], after[tt], wide_free) for tt in range(TT)]
            return transpose_split(lambda tt, k: wide[:, tt, k * P:(k + 1) * P], KD, gain, shift,
                                   lambda k: h_hi[:, k, :], lambda k: h_lo[:, k, :], work, work_free,
                                   lambda tt, k: scaled[tt], h_free)

        x_landed = [load(f"x_landed{tt}", x[:, tt, :], X[tt * P:(tt + 1) * P, :]) for tt in range(TT)]
        params_landed = load("params_landed", lasting[:, :], PARAMS)
        phase1 = place("phase1", "phase", 0, [P, PHASE1["_width"]])
        params1_landed = load("params1_landed", phase1[:, :], PARAMS1)
        load_chunks()

        def param1(name):
            a, b = PHASE1[name]
            return phase1[:, a:b]

        work1 = place("work1", "free", 0, [P, 2, T])
        work1_free = [None, None]
        silu_c = stats(KD)
        silu_c_done = ACTE.do(lambda e: e.activation(silu_c, param("c"), ACT.Silu), params_landed)
        g1 = param("mix_norm_g")
        h_ready = norm_to_h(x_landed, lambda k: g1[:, k:k + 1], None, work1, work1_free, None, params_landed)
        h_of = lambda k: h_ready[k]

        FR = "free"
        bias = place("bias", "wide", 0, [P, HEADS, T])
        cmp_bias = place("cmp_bias", FR, 17408, [P, TT * HEADS * NCMP])
        one_hot, rel = param1("one_hot"), param1("rel_bias")
        K1 = BUCKETS + 1
        bias_done = []
        for c0 in range(0, T, 32):
            b = GROUP_BANKS[0][0] + (c0 // 32) % 4
            for c in range(c0, c0 + 32):
                a = DIST0 + P - c
                t = PE.do(lambda e, a=a, c=c, c0=c0, b=b: e.matmul(banks[b][:, (c - c0) * HEADS:(c - c0 + 1) * HEADS],
                                                                   one_hot[0:K1, a:a + P], rel[0:K1, :], start=True, stop=True),
                          params1_landed, bank_read[b], signal=c == c0 + 31)
            view = banks[b][:, 0:512].rearrange("p (c h) -> p h c", h=HEADS)
            t = DVE.do(lambda e, c0=c0, view=view: e.tensor_copy(bias[:, :, c0:c0 + 32], view), t, h_ready[-1])
            bank_read[b] = t
            bias_done.append(t)
        b = 0
        for tt in range(TT):
            for n in range(NCMP):
                a = DIST0 + tt * P - (n * CMP_STRIDE + CMP_LEN - 1)
                lo = tt * HEADS * NCMP + n
                t = PE.do(lambda e, a=a, lo=lo: e.matmul(banks[0][:, lo:lo + HEADS * NCMP - NCMP + 1:NCMP],
                                                         one_hot[0:K1, a:a + P], rel[0:K1, :], start=True, stop=True),
                          bank_read[0], signal=n == NCMP - 1)
        cmp_bias_done = bank_read[0] = DVE.do(lambda e: e.tensor_copy(cmp_bias[:, :], banks[0][:, 0:TT * HEADS * NCMP]), t)

        tokens = place("tokens", FR, 2048, [P, 2, 2, 2, T])
        pos = param1("cmp_pos").rearrange("p (s l) -> p s l", s=2)
        tokens_done = []
        for s in range(2):
            for j in range(2):
                out, b, t = tile(("cmp", s, j), h_hi, h_lo, h_of)
                for half in range(2):
                    add = pos[:, s, half * CMP_STRIDE:(half + 1) * CMP_STRIDE].unsqueeze(1).to_broadcast([P, T // CMP_STRIDE, CMP_STRIDE])
                    u = DVE.do(lambda e, s=s, j=j, half=half, out=out, add=add: e.tensor_tensor(
                        tokens[:, s, half, j, :].rearrange("p (n l) -> p n l", l=CMP_STRIDE),
                        out.rearrange("p (n l) -> p n l", l=CMP_STRIDE), add, ALU.add), t, params1_landed)
                bank_read[b] = u
                tokens_done.append(u)
        hidden = place("hidden", FR, 17408 + 1920, [P, 2, 2 * NCMP])
        kcmp = place("kcmp", FR, 17408 + 1920 + 256, [P, 2 * NCMP])
        vcmp = place("vcmp", "mid", mid_tail + 12288 - 1024, [NCMP, KV_HEADS, DH]) if False else place("vcmp", FR, 17408 + 1920 + 384, [NCMP, KV_HEADS, DH])
        w2 = param1("cmp_w2").rearrange("p (s e) -> p s e", s=2)
        chunks_w1 = plan.groups["cmp_w1"]
        per = CHUNK // DH
        for s in range(2):
            b = odd_bank()
            for base_p in (0, DH):
                rows = slice(base_p, base_p + DH)
                for l in range(CMP_LEN):
                    i = chunks_w1[(s * CMP_LEN + l) // per]
                    w1_ap = raw[rows, i % RAW_SLOTS, (l % per) * DH:(l % per + 1) * DH]
                    half, within = divmod(l, CMP_STRIDE)
                    first = half * CMP_STRIDE + within
                    moving = tokens[rows, s, half, :, first:first + CMP_STRIDE * (NCMP - 1) + 1:CMP_STRIDE]
                    t = PE.do(lambda e, b=b, rows=rows, w1_ap=w1_ap, moving=moving, l=l: e.matmul(
                        banks[b][rows, 0:2 * NCMP].rearrange("p (j n) -> p j n", j=2), w1_ap, moving, start=l == 0, stop=l == CMP_LEN - 1),
                        arrived(i), tokens_done[2 * s + 1], bank_read[b],
                        signal=(base_p == DH and l % per == per - 1) or l == CMP_LEN - 1)
                    if base_p == DH and l % per == per - 1:
                        released[i] = t
            prepare(chunks_w1[2 * s + 1])
            load_chunks()
            t = ACTE.do(lambda e, s=s, b=b: e.activation(hidden[:, s, :], banks[b][:, 0:2 * NCMP], ACT.Silu), t)
            bank_read[b] = t
            b2 = odd_bank()
            if s == 0:
                for base_p in (0, DH):
                    rows = slice(base_p, base_p + DH)
                    u = PE.do(lambda e, b=b2, rows=rows: e.matmul(banks[b][rows, 0:2 * NCMP], w2[rows, 0, :], hidden[rows, 0, :], start=True, stop=True),
                              t, bank_read[b2])
                kcmp_done = bank_read[b2] = DVE.do(lambda e, b=b2: e.tensor_copy(kcmp[:, :], banks[b][:, 0:2 * NCMP]), u)
            else:
                u = None
                for hk in (0, 2, 1, 3):
                    base_p = DH * (hk % 2)
                    rows = slice(base_p, base_p + DH)
                    j = hk // 2
                    u = PE.do(lambda e, b=b2, rows=rows, hk=hk, j=j: e.matmul(banks[b][0:NCMP, hk * DH:(hk + 1) * DH], hidden[rows, 1, j * NCMP:(j + 1) * NCMP],
                                                                             w2[rows, 1, :], start=True, stop=True), t, u, bank_read[b2])
                vcmp_done = bank_read[b2] = DVE.do(lambda e, b=b2: e.tensor_copy(vcmp[:, :, :].rearrange("p h d -> p (h d)"), banks[b][0:NCMP, 0:KV_HEADS * DH]), u)
        w1_used = t

        keys = place("keys", "mid", mid_tail + 8192, [P, 2, 2, T])
        queries = place("queries", "mid", mid_tail, [P, 8, T])
        values = place("values", FR, 10240, [P, TT, 2, KV_HEADS * DH])
        gates = place("gates", FR, 14336, [P, TT, HEADS, N_BRANCH])
        for br in range(2):
            for j in range(2):
                out, b, t = tile(("key", br + 1, j), h_hi, h_lo, h_of)
                keys_done = bank_read[b] = ACTE.do(lambda e, br=br, j=j, out=out: e.activation(keys[:, br, j, :], out, ACT.Copy), t)
        for j in range(8):
            out, b, t = tile(("query", j), h_hi, h_lo, h_of)
            queries_done = bank_read[b] = ACTE.do(lambda e, j=j, out=out: e.activation(queries[:, j, :], out, ACT.Copy, scale=DH ** -0.5), t)
        outs, pair, t = group("value", 512, h_hi, h_lo, h_of)
        for tt in range(TT):
            values_done = bank_read[pair[tt]] = ACTE.do(
                lambda e, tt=tt, out=outs[tt]: e.activation(values[:, tt, :, :].rearrange("p b c -> p (b c)"), out, ACT.Copy), t)
        outs, pair, t = group("gates", N_BRANCH * HEADS, h_hi, h_lo, h_of)
        for tt in range(TT):
            gates_done = bank_read[pair[tt]] = ACTE.do(
                lambda e, tt=tt, out=outs[tt]: e.activation(gates[:, tt, :, :].rearrange("p h b -> p (h b)"), out, ACT.Sigmoid), t)

        NU = TT * HEADS
        cmp_p = place("cmp_p", FR, 14336 + 384, [P, NU, NCMP])
        b = ODD_BANKS[0]
        t = None
        by_rows = sorted((query_place(h)[1], h, tt) for h in range(HEADS) for tt in range(TT))
        for at_h, (base_p, h, tt) in enumerate(by_rows):
                j = query_place(h)[0]
                rows = slice(base_p, base_p + DH)
                u = tt * HEADS + h
                pair_j = h // GQA // 2
                half_done = t if at_h == NU // 2 else None
                t = PE.do(lambda e, b=b, j=j, rows=rows, u=u, tt=tt, pair_j=pair_j: e.matmul(
                    banks[b][:, u * NCMP:(u + 1) * NCMP], queries[rows, j, tt * P:(tt + 1) * P],
                    kcmp[rows, pair_j * NCMP:(pair_j + 1) * NCMP], start=True, stop=True),
                    queries_done, kcmp_done, half_done, bank_read[b], signal=at_h in (NU // 2 - 1, NU - 1))
        flat = cmp_p[:, :, :].rearrange("p u n -> p (u n)")
        t = DVE.do(lambda e: e.tensor_tensor(flat, banks[6][:, 0:NU * NCMP], cmp_bias[:, :], ALU.add), t, cmp_bias_done)
        bank_read[b] = t
        cmp_max, cmp_sum, cmp_coef = stats(NU), stats(NU), stats(NU)
        t = DVE.do(lambda e: e.tensor_reduce(cmp_max, cmp_p[:, :, :], AX.X, ALU.max), t)
        t = DVE.do(lambda e: e.tensor_tensor(cmp_p[:, :, :], cmp_p[:, :, :], cmp_max.unsqueeze(2).to_broadcast([P, NU, NCMP]), ALU.subtract), t)
        t = ACTE.do(lambda e: e.activation(flat, flat, ACT.Exp), t)
        t = DVE.do(lambda e: e.tensor_reduce(cmp_sum, cmp_p[:, :, :], AX.X, ALU.add), t)
        t = DVE.do(lambda e: e.reciprocal(cmp_coef, cmp_sum), t)
        t = DVE.do(lambda e: e.tensor_tensor(cmp_coef.rearrange("p (t h) -> p t h", t=TT), cmp_coef.rearrange("p (t h) -> p t h", t=TT),
                                             gates[:, :, :, 0], ALU.mult), t, gates_done)
        some = param1("any_block").unsqueeze(2).to_broadcast([P, TT, HEADS])
        t = DVE.do(lambda e: e.tensor_tensor(cmp_coef.rearrange("p (t h) -> p t h", t=TT), cmp_coef.rearrange("p (t h) -> p t h", t=TT), some, ALU.mult), t)
        cmp_p_done = DVE.do(lambda e: e.tensor_tensor(cmp_p[:, :, :], cmp_p[:, :, :], cmp_coef.unsqueeze(2).to_broadcast([P, NU, NCMP]), ALU.mult), t)

        scores = place("scores", FR, 0, [P, 2, 2, T])
        weights_T = place("weights_T", FR, 4096, [P, 4, P])
        cmp_T = place("cmp_T", FR, 6144, [NCMP, P])
        conv_u = place("conv_u", FR, 6656, [P, 2, T + CONV_TAPS - 1 + 2])
        PAD = CONV_TAPS - 1
        conv_y = place("conv_y", "acc", 0, [P, CONV_TILES, T])
        sig = place("sig", FR, 8960, [P, T])
        neg_max, row_sum, coef = stats(2 * NU), stats(2 * NU), stats(2 * NU)
        unit_free = {"scores": [w1_used, w1_used], "T": w1_used, "cmp_T": w1_used}
        units = [(h, tt) for h in range(HEADS) for tt in range(TT)]

        def unit_scores(u):
            h, tt = units[u]
            n = P * (tt + 1)
            j, base_p = query_place(h)
            rows = slice(base_p, base_p + DH)
            hk = h // GQA
            b = u % 2
            for br in range(2):
                t = PE.do(lambda e, br=br: e.matmul(banks[b][:, br * n:(br + 1) * n], queries[rows, j, tt * P:(tt + 1) * P],
                                                    keys[rows, br, hk // 2, 0:n], start=True, stop=True),
                          queries_done, keys_done, bank_read[b], signal=br == 1)
            s = scores[:, u % 2, :, 0:n]
            add = bias[:, h, T - n:T].unsqueeze(1).to_broadcast([P, 2, n])
            t = DVE.do(lambda e: e.tensor_tensor(s, banks[b][:, 0:2 * n].rearrange("p (b c) -> p b c", b=2), add, ALU.add),
                       t, unit_free["scores"][u % 2], bias_done[-1])
            bank_read[b] = t
            m = neg_max[:, 2 * u:2 * u + 2]
            t = DVE.do(lambda e: e.tensor_reduce(m, s, AX.X, ALU.max, negate=True), t)
            for br in range(2):
                t = ACTE.do(lambda e, br=br: e.activation(s[:, br, :], s[:, br, :], ACT.Exp, bias=m[:, br:br + 1],
                                                          accum_out=row_sum[:, 2 * u + br:2 * u + br + 1]), t)
            c = coef[:, 2 * u:2 * u + 2]
            t = DVE.do(lambda e: e.reciprocal(c, row_sum[:, 2 * u:2 * u + 2]), t)
            t = DVE.do(lambda e: e.tensor_tensor(c, c, gates[:, tt, h, 1:3], ALU.mult), t, gates_done)
            for br in range(2):
                v = DVE.do(lambda e, br=br: e.tensor_scalar(s[:, br, :], s[:, br, :], c[:, br:br + 1], None, ALU.mult), t)
            return v

        def unit_output(u, p_done):
            h, tt = units[u]
            hk = h // GQA
            nb = tt + 1
            for br in range(2):
                for sb in range(nb):
                    t = PE.do(lambda e, br=br, sb=sb: e.transpose(banks[3][:, (br * nb + sb) * P:(br * nb + sb + 1) * P],
                                                                  scores[:, u % 2, br, sb * P:(sb + 1) * P], identity),
                              p_done, bank_read[3], signal=br == 1 and sb == nb - 1)
            unit_free["scores"][u % 2] = t
            wt = ACTE.do(lambda e: e.activation(weights_T[:, 0:2 * nb, :].rearrange("p a c -> p (a c)"), banks[3][:, 0:2 * nb * P], ACT.Copy), t, unit_free["T"])
            bank_read[3] = wt
            t = PE.do(lambda e: e.transpose(banks[2][0:NCMP, 2 * P:3 * P], cmp_p[:, tt * HEADS + h, :], identity), cmp_p_done, bank_read[2])
            ct = ACTE.do(lambda e: e.activation(cmp_T[:, :], banks[2][0:NCMP, 2 * P:3 * P], ACT.Copy), t, unit_free["cmp_T"])
            base_p = DH * (h % 2)
            rows = slice(base_p, base_p + DH)
            out = banks[2][rows, 0:P]
            PE.do(lambda e: e.matmul(out, vcmp[:, hk, :], cmp_T[:, :], start=True, stop=False), ct, vcmp_done, signal=False)
            for br in range(2):
                for sb in range(nb):
                    end = br == 1 and sb == nb - 1
                    t = PE.do(lambda e, br=br, sb=sb, end=end: e.matmul(out, values[:, sb, br, hk * DH:(hk + 1) * DH],
                                                                        weights_T[:, br * nb + sb, :], start=False, stop=end),
                              wt, values_done, signal=end)
            unit_free["T"] = unit_free["cmp_T"] = t
            cols = slice(tt * P, (tt + 1) * P)
            t = split(mix_hi[rows, h // 2, cols], mix_lo[rows, h // 2, cols], out, t)
            bank_read[2] = t
            return t

        pad_done = [DVE.do(lambda e, s=s: e.memset(conv_u[:, s, 0:PAD], 0.0), w1_used) for s in range(2)]
        conv_w = param1("conv_w").rearrange("p (j t) -> p j t", j=CONV_TILES)
        conv_b = param1("conv_b")
        conv_free = [None, None]
        conv_steps = []

        def conv_project(j):
            out_a, ba, ta = tile(("conv_a", j), h_hi, h_lo, h_of)
            out_g, bg, tg = tile(("conv_g", j), h_hi, h_lo, h_of)
            s = ACTE.do(lambda e: e.activation(sig[:, :], out_g, ACT.Sigmoid), tg, conv_free[1], w1_used)
            bank_read[bg] = s
            u = conv_u[:, j % 2, :]
            t = DVE.do(lambda e: e.tensor_tensor(u[:, PAD:PAD + T], out_a, sig[:, :], ALU.mult), s, ta, conv_free[0], pad_done[1])
            conv_free[1] = bank_read[ba] = t
            y = conv_y[:, j, :]
            t = DVE.do(lambda e: e.tensor_scalar(y, u[:, PAD:PAD + T], conv_w[:, j, PAD:PAD + 1], conv_b[:, j:j + 1], ALU.mult, ALU.add), t)

            def taps(t=t):
                for tap in range(PAD):
                    t = DVE.do(lambda e, tap=tap: e.scalar_tensor_tensor(y, u[:, tap:tap + T], conv_w[:, j, tap:tap + 1], y, ALU.mult, ALU.add), t)
                    yield t
            conv_steps.append(taps())

        y_done = [None]

        def conv_advance(n):
            while n and conv_steps:
                for t in conv_steps[0]:
                    y_done[0] = t
                    n -= 1
                    if not n:
                        return
                else:
                    conv_steps.pop(0)

        pending = None
        for u in range(NU):
            p_done = unit_scores(u)
            if u % 4 == 0:
                conv_advance(PAD + 1)
                conv_project(u // 4)
            else:
                conv_advance(10)
            if pending is not None:
                mix_done = unit_output(*pending)
            pending = (u, p_done)
        mix_done = unit_output(*pending)
        conv_advance(10000)

        b = ODD_BANKS[0]
        for j in range(CONV_TILES):
            t = PE.do(lambda e, j=j: e.matmul(banks[6][:, 0:T], ones, conv_y[:, j, :], start=j == 0, stop=j == CONV_TILES - 1),
                      y_done[0], bank_read[b], signal=j == CONV_TILES - 1)
        ln_mean = place("ln_mean", FR, 0, [P, T])
        ln_sq = place("ln_sq", FR, 1024, [P, 2, T])
        ln_rs = place("ln_rs", FR, 3072, [P, T])
        t = ACTE.do(lambda e: e.activation(ln_mean[:, :], banks[6][:, 0:T], ACT.Copy, scale=1.0 / CONV_CH), t, mix_done)
        bank_read[b] = t
        mean_all = ln_mean[:, :].unsqueeze(1).to_broadcast([P, CONV_TILES, T])
        centred = DVE.do(lambda e: e.tensor_tensor(conv_y[:, :, :], conv_y[:, :, :], mean_all, ALU.subtract), t)
        sq_free = [None, None]
        b = ODD_BANKS[1]
        for j in range(CONV_TILES):
            t = ACTE.do(lambda e, j=j: e.activation(ln_sq[:, j % 2, :], conv_y[:, j, :], ACT.Square), centred, sq_free[j % 2])
            t = sq_free[j % 2] = PE.do(lambda e, j=j: e.matmul(banks[7][:, 0:T], ones, ln_sq[:, j % 2, :], start=j == 0, stop=j == CONV_TILES - 1),
                                       t, bank_read[b])
        t = DVE.do(lambda e: e.tensor_scalar(ln_rs[:, :], banks[7][:, 0:T], 1.0 / CONV_CH, EPS, ALU.mult, ALU.add), t)
        bank_read[b] = t
        t = POOL.do(lambda e: e.tensor_tensor(ln_rs[:, :], ln_rs[:, :], minus_half.to_broadcast([P, T]), ALU.pow), t)
        rs_all = ln_rs[:, :].unsqueeze(1).to_broadcast([P, CONV_TILES, T])
        scaled = DVE.do(lambda e: e.tensor_tensor(conv_y[:, :, :], conv_y[:, :, :], rs_all, ALU.mult), t)
        ln_g, ln_b = param1("conv_ln_g"), param1("conv_ln_b")
        for j in range(CONV_TILES):
            t = ACTE.do(lambda e, j=j: e.activation(conv_y[:, j, :], conv_y[:, j, :], ACT.Silu, scale=ln_g[:, j:j + 1], bias=ln_b[:, j:j + 1]), scaled)
            mix_done = split(mix_hi[:, KD // 2 + j, :], mix_lo[:, KD // 2 + j, :], conv_y[:, j, :], t)
        conv_done = mix_done
        state["ada_slot"] = [conv_done, conv_done]

        def residual_groups(name, act_hi, act_lo, after, add_to):
            done = [None, None]
            for n in range(4):
                outs, pair, t = group((*name, n), 512, act_hi, act_lo, after)
                for tt in range(TT):
                    dst = add_to[:, tt, n * 512:(n + 1) * 512]
                    done[tt] = bank_read[pair[tt]] = DVE.do(
                        lambda e, dst=dst, out=outs[tt]: e.tensor_tensor(dst, out, dst, ALU.add), t)
            return done

        def fresh_groups(name, act_hi, act_lo, after, dst_of, dst_free):
            done = [None, None]
            for n in range(4):
                outs, pair, t = group((*name, n), 512, act_hi, act_lo, after)
                for tt in range(TT):
                    dst = dst_of[:, tt, n * 512:(n + 1) * 512]
                    done[tt] = bank_read[pair[tt]] = ACTE.do(
                        lambda e, dst=dst, out=outs[tt]: e.activation(dst, out, ACT.Copy), t, dst_free)
            return done

        x_done = residual_groups(("out1",), mix_hi, mix_lo, mix_done, x)

        work2 = place("work2", FR, 0, [P, 2, T])
        work2_free = [conv_done, conv_done]
        g2 = param("ffn_norm_g")
        h_ready = norm_to_h(x_done, lambda k: g2[:, k:k + 1], None, work2, work2_free, None, conv_done)
        ff_w = param("ffn_conv_w").rearrange("p (j t) -> p j t", t=3)
        ff_b = param("ffn_conv_b")
        ffn_a = place("ffn_a", FR, 2048, [P, 2, T])
        ffn_g = place("ffn_g", FR, 4096, [P, 2, T])
        ff_free = [conv_done, conv_done]

        def conv3(out, b, t, y, j, free):
            t = ACTE.do(lambda e: e.activation(y, out, ACT.Identity, scale=ff_w[:, j, 2:3], bias=ff_b[:, j:j + 1]), t, free)
            t = DVE.do(lambda e: e.scalar_tensor_tensor(y[:, 1:T], out[:, 0:T - 1], ff_w[:, j, 1:2], y[:, 1:T], ALU.mult, ALU.add), t)
            t = DVE.do(lambda e: e.scalar_tensor_tensor(y[:, 2:T], out[:, 0:T - 2], ff_w[:, j, 0:1], y[:, 2:T], ALU.mult, ALU.add), t)
            bank_read[b] = t
            return t

        mid_free = PE_last = None
        for half in range(2):
            ff_done = []
            for j in range(FF_HALF * half, FF_HALF * (half + 1)):
                s = j % 2
                out, b, t = tile(("up_a", j), h_hi, h_lo, h_of)
                ya = conv3(out, b, t, ffn_a[:, s, :], j, ff_free[s])
                out, b, t = tile(("up_g", j), h_hi, h_lo, h_of)
                yg = conv3(out, b, t, ffn_g[:, s, :], FF_TILES + j, ff_free[s])
                t = ACTE.do(lambda e, s=s: e.activation(ffn_g[:, s, :], ffn_g[:, s, :], ACT.Silu), yg)
                t = DVE.do(lambda e, s=s: e.tensor_tensor(ffn_a[:, s, :], ffn_a[:, s, :], ffn_g[:, s, :], ALU.mult), t, ya)
                jj = j - FF_HALF * half
                t = ff_free[s] = split(ff_hi[:, jj, :], ff_lo[:, jj, :], ffn_a[:, s, :], t)
                ff_done.append(t)
            x_done = residual_groups(("down1", half), ff_hi, ff_lo, lambda k, d=ff_done: d[k], x)
        prepare(plan.groups["c_q"][0][0] - 1)
        run_deferred(True)
        phase2 = place("phase2", "phase", 0, [P, PHASE2["_width"]])
        params2_landed = load("params2_landed", phase2[:, :], PARAMS2, conv_done)
        positions = place("positions", "phase", -(-PHASE2["_width"] * 4 // 64) * 64, [P, TT], I32)
        positions_landed = load("positions_landed", positions[:, :], POSITIONS, conv_done)

        def param2(name):
            a, b = PHASE2[name]
            return phase2[:, a:b]

        def broadcast_row(vec, bank, diag, diag_free, vec_done):
            for q in range(4):
                for k in range(4):
                    t = DVE.do(lambda e, q=q, k=k: e.tensor_scalar(diag[:, q % 2, k * P:(k + 1) * P], identity, vec(4 * q + k), None, ALU.mult),
                               diag_free[q % 2], vec_done)
                diag_free[q % 2] = t = PE.do(lambda e, q=q: e.matmul(banks[q][:, :], ones, diag[:, q % 2, :], start=True, stop=True), t, bank_read[q])
            return t

        diag = place("diag", FR, 6144, [P, 2, 512])
        diag_free = [conv_done, conv_done]
        junk = place("junk", FR, 10240, [P, D])
        rs, rs_done = rms_factors(lambda tt: x[:, tt, :], D, lambda tt: junk[:, :], lambda tt: [x_done[tt], conv_done])
        gf = param("final_norm_g")
        t = broadcast_row(lambda k: gf[:, k:k + 1], 0, diag, diag_free, params_landed)
        x_done = [None, None]
        for tt in range(TT):
            for q in range(4):
                x_q = x[:, tt, q * 512:(q + 1) * 512]
                x_done[tt] = bank_read[q] = DVE.do(lambda e, tt=tt, q=q, x_q=x_q: e.scalar_tensor_tensor(
                    x_q, x_q, rs[:, tt:tt + 1], banks[q][:, :], ALU.mult, ALU.mult), rs_done[tt], t)

        def ada(v):
            a = LASTING["b_ada"][0] + v * KD
            return lasting[:, a:a + KD]

        def ada_done(v):
            return [vectors[v, 0], vectors[v, 1]]

        def fold(gain, scale_v):
            return DVE.do(lambda e: e.scalar_tensor_tensor(ada(scale_v), ada(scale_v), 1.0, param(gain), ALU.add, ALU.mult), ada_done(scale_v))

        def fold_gate(gain, gate_v):
            return DVE.do(lambda e: e.tensor_tensor(ada(gate_v), ada(gate_v), param(gain), ALU.mult), ada_done(gate_v))

        folded = fold("g_pre_mix", 1)
        folded_gate = fold_gate("g_post_mix", 2)
        folded_ffn = fold("g_pre_ffn", 4)
        folded_gate_ffn = fold_gate("g_post_ffn", 5)
        h_ready = norm_to_h([x_done[0], x_done[1]], lambda k: ada(1)[:, k:k + 1], lambda k: ada(0)[:, k:k + 1],
                            work2, work2_free, None, [folded, ada_done(0)])
        wide_free = h_ready[-1]
        ffn1_done = ff_free[:]

        c_q = place("c_q", "acc", 0, [P, TT, Q_RANK])
        c_kv = place("c_kv", "acc", TT * Q_RANK * 4, [P, TT, KV_RANK + ROPE + GATE_RANK])
        outs, pair, t = group("c_q", Q_RANK, h_hi, h_lo, h_of)
        for tt in range(TT):
            c_q_done = bank_read[pair[tt]] = ACTE.do(lambda e, tt=tt, out=outs[tt]: e.activation(c_q[:, tt, :], out, ACT.Copy), t, ada_done(5))
        outs, pair, t = group("c_kv", KV_RANK + ROPE + GATE_RANK, h_hi, h_lo, h_of)
        for tt in range(TT):
            c_kv_done = bank_read[pair[tt]] = ACTE.do(lambda e, tt=tt, out=outs[tt]: e.activation(c_kv[:, tt, :], out, ACT.Copy), t, ada_done(5))
        small_junk = place("small_junk", FR, 4096, [P, Q_RANK])
        rs_q, rs_q_done = rms_factors(lambda tt: c_q[:, tt, :], Q_RANK, lambda tt: small_junk[:, :], lambda tt: [c_q_done, ffn1_done])
        rs_kv, rs_kv_done = rms_factors(lambda tt: c_kv[:, tt, 0:KV_RANK], KV_RANK, lambda tt: small_junk[:, 0:KV_RANK], lambda tt: [c_kv_done, rs_q_done])
        c_q_ok = [DVE.do(lambda e, tt=tt: e.tensor_scalar(c_q[:, tt, :], c_q[:, tt, :], rs_q[:, tt:tt + 1], None, ALU.mult), rs_q_done[tt]) for tt in range(TT)]
        c_kv_ok = [DVE.do(lambda e, tt=tt: e.tensor_scalar(c_kv[:, tt, 0:KV_RANK], c_kv[:, tt, 0:KV_RANK], rs_kv[:, tt:tt + 1], None, ALU.mult), rs_kv_done[tt]) for tt in range(TT)]

        rope_w = place("rope_w", FR, 6144, [P, 8, TT, ROPE2])
        pos_f = stats(TT)
        angle, turns_, cosine, sine = (rope_w[:, i, :, :] for i in range(4))
        r_t = DVE.do(lambda e: e.tensor_copy(pos_f, positions[:, :]), positions_landed)
        for tt in range(TT):
            r_u = DVE.do(lambda e, tt=tt: e.tensor_scalar(angle[:, tt, :], param2("inv_freq"), pos_f[:, tt:tt + 1], None, ALU.mult), r_t, params2_landed, diag_free, ffn1_done)
        MAGIC = 12582912.0
        r_t = DVE.do(lambda e: e.tensor_scalar(turns_, angle, float(np.float32(1 / (2 * np.pi))), MAGIC, ALU.mult, ALU.add), r_u)
        r_t = DVE.do(lambda e: e.tensor_scalar(turns_, turns_, -MAGIC, None, ALU.add), r_t)
        rest = 2 * np.pi
        for bits in (7, 8, 8, 24):
            m, ex = np.frexp(rest)
            part = float(np.ldexp(np.round(m * 2 ** bits), int(ex) - bits))
            rest -= part
            r_t = DVE.do(lambda e, part=part: e.scalar_tensor_tensor(angle, turns_, -part, angle, ALU.mult, ALU.add), r_t)
        PI = float(np.float32(np.pi))
        PI_IN = float(np.nextafter(np.float32(np.pi), np.float32(0)))
        r_t = DVE.do(lambda e: e.tensor_scalar(angle, angle, PI_IN, -PI_IN, ALU.min, ALU.max), r_t)
        r_c = DVE.do(lambda e: e.tensor_scalar(cosine, angle, -1.0, None, ALU.mult), r_t)
        r_c = DVE.do(lambda e: e.tensor_tensor(cosine, cosine, angle, ALU.min), r_c)
        r_c = DVE.do(lambda e: e.tensor_scalar(cosine, cosine, PI / 2, None, ALU.add), r_c)
        ACTE.do(lambda e: e.activation(cosine, cosine, ACT.Sin), r_c)
        rope_done = ACTE.do(lambda e: e.activation(sine, angle, ACT.Sin), r_t)

        gla_q = place("gla_q", "mid", mid_tail, [P, GLA_HEADS, T])
        gla_k = place("gla_k", "mid", mid_tail + 4096, [P, GLA_HEADS, T])
        gla_kd = place("gla_kd", "mid", mid_tail + 8192, [P, GLA_HEADS, T])
        down_done = x_done[1]
        for h in range(GLA_HEADS):
            out, b, t = tile(("gla_q", h), h_hi, h_lo, h_of)
            gla_q_done = bank_read[b] = ACTE.do(lambda e, h=h, out=out: e.activation(gla_q[:, h, :], out, ACT.Copy, scale=float(np.float32(GLA_K ** -0.5))), t, down_done)
        for h in range(GLA_HEADS):
            out, b, t = tile(("gla_k", h), h_hi, h_lo, h_of)
            gla_k_done = bank_read[b] = ACTE.do(lambda e, h=h, out=out: e.activation(gla_k[:, h, :], out, ACT.Copy), t, down_done)

        KQ, KKV = Q_RANK // P, KV_RANK // P
        cq_hi = place("cq_hi", FR, 8192, [P, KQ, T], F32R)
        cq_lo = place("cq_lo", FR, 12288, [P, KQ, T], F32R)
        ckv_hi = place("ckv_hi", FR, 16384, [P, KKV, T], F32R)
        ckv_lo = place("ckv_lo", FR, 18432, [P, KKV, T], F32R)
        g_q, g_kv = param("g_q"), param("g_kv")
        c_free = [diag_free, rs_done[1]]
        cq_ready = transpose_split(lambda tt, k: c_q[:, tt, k * P:(k + 1) * P], KQ, lambda k: g_q[:, k:k + 1], None,
                                   lambda k: cq_hi[:, k, :], lambda k: cq_lo[:, k, :], work2, work2_free, lambda tt, k: c_q_ok[tt], c_free)
        ckv_ready = transpose_split(lambda tt, k: c_kv[:, tt, k * P:(k + 1) * P], KKV, lambda k: g_kv[:, k:k + 1], None,
                                    lambda k: ckv_hi[:, k, :], lambda k: ckv_lo[:, k, :], work2, work2_free, lambda tt, k: c_kv_ok[tt], c_free)
        a_lr = place("a_lr", FR, 2048, [GATE_RANK, T])
        b = odd_bank()
        for tt in range(TT):
            t = PE.do(lambda e, tt=tt, b=b: e.transpose(banks[b][0:GATE_RANK, tt * P:(tt + 1) * P], c_kv[:, tt, KV_RANK + ROPE:], identity),
                      c_kv_ok, bank_read[b])
        a_lr_done = bank_read[b] = DVE.do(lambda e, b=b: e.tensor_copy(a_lr[:, :], banks[b][0:GATE_RANK, 0:T]), t, ffn1_done)

        rope_last = [None]

        def rope(src1, src2, dst1, dst2, heads, tt, after, temps):
            cos_b = cosine[:, tt, :].unsqueeze(1).to_broadcast([P, heads, ROPE2])
            sin_b = sine[:, tt, :].unsqueeze(1).to_broadcast([P, heads, ROPE2])
            ta, tb = temps
            a = DVE.do(lambda e: e.tensor_tensor(ta, src1, cos_b, ALU.mult), after, rope_done, rope_last[0])
            b_ = DVE.do(lambda e: e.tensor_tensor(tb, src2, sin_b, ALU.mult), after)
            o1 = DVE.do(lambda e: e.tensor_tensor(dst1, ta, tb, ALU.subtract), a, b_)
            a = DVE.do(lambda e: e.tensor_tensor(ta, src2, cos_b, ALU.mult), o1)
            b_ = DVE.do(lambda e: e.tensor_tensor(tb, src1, sin_b, ALU.mult), o1)
            rope_last[0] = DVE.do(lambda e: e.tensor_tensor(dst2, ta, tb, ALU.add), a, b_)
            return rope_last[0]

        k_rot = place("k_rot", "stat", 2048 - 512 - 0, [P, 1]) if False else place("k_rot", FR, 3072, [P, TT, 2, ROPE])
        tmp_k = rope_w[:, 4, :, :]
        k_rope_T = place("k_rope_T", "h", 29 * 1024, [P, T])
        b = odd_bank()
        for tt in range(TT):
            k1 = c_kv[:, tt, KV_RANK:KV_RANK + ROPE2].unsqueeze(1)
            k2 = c_kv[:, tt, KV_RANK + ROPE2:KV_RANK + ROPE].unsqueeze(1)
            t = rope(k1, k2, k_rot[:, tt, 0:1, 0:ROPE2], k_rot[:, tt, 0:1, ROPE2:ROPE], 1, tt, [c_kv_done, ffn1_done],
                     (tmp_k[:, 0:1, :], tmp_k[:, 1:2, :]))
            t = DVE.do(lambda e, tt=tt: e.tensor_copy(k_rot[:, tt, 1, :], k_rot[:, tt, 0, :]), t)
            t = PE.do(lambda e, tt=tt, b=b: e.transpose(banks[b][:, tt * P:(tt + 1) * P], k_rot[:, tt, :, :].rearrange("p a c -> p (a c)"), identity), t, bank_read[b])
        k_rope_bank, k_rope_t = b, t
        k_rope_x = place("k_rope_x", FR, 5120, [P, T])
        k_rope_done = bank_read[b] = DVE.do(lambda e, b=b: e.tensor_copy(k_rope_x[:, :], banks[b][:, 0:T]), t, rs_kv_done)

        gla_v = place("gla_v", "wide", 0, [P, TT, GLA_HEADS * GLA_V])
        gla_o = place("gla_o", "wide", TT * GLA_HEADS * GLA_V * 4, [P, TT, GLA_HEADS * GLA_V])
        for name, dst, func in (("gla_v", gla_v, ACT.Copy), ("gla_r", gla_o, ACT.Silu)):
            for n in range(2):
                outs, pair, t = group((name, n), 512, h_hi, h_lo, h_of)
                h_used = t
                for tt in range(TT):
                    u = bank_read[pair[tt]] = ACTE.do(lambda e, tt=tt, n=n, out=outs[tt], dst=dst, func=func: e.activation(
                        dst[:, tt, n * 512:(n + 1) * 512], out, func), t, wide_free)
            if name == "gla_v":
                gla_v_done = u
            else:
                gla_r_done = u

        q_nope = place("q_nope", "h", 0, [P, MLA_HEADS, T])
        k_nope = place("k_nope", "h", 8192, [P, MLA_HEADS, T])
        mla_v = place("mla_v", "h", 16384, [P, TT, MLA_HEADS * NOPE])
        q_rope_T = place("q_rope_T", "h", 24576, [P, 4, T])
        q_rot = place("q_rot", "acc", 0, [P, TT, MLA_HEADS * ROPE])
        rope_tmp = place("rope_tmp", "h", 29696, [P, 2, MLA_HEADS, ROPE2])
        outs, pair, t = group("q_rope", MLA_HEADS * ROPE, cq_hi, cq_lo, lambda k: cq_ready[k])
        for tt in range(TT):
            src = outs[tt].rearrange("p (h c) -> p h c", h=MLA_HEADS)
            dst = q_rot[:, tt, :].rearrange("p (h c) -> p h c", h=MLA_HEADS)
            u = rope(src[:, :, 0:ROPE2], src[:, :, ROPE2:ROPE], dst[:, :, 0:ROPE2], dst[:, :, ROPE2:ROPE], MLA_HEADS, tt,
                     [t, h_used, cq_ready], (rope_tmp[:, 0, :, :], rope_tmp[:, 1, :, :]))
            bank_read[pair[tt]] = u
        q_rot_done = u
        for h in range(MLA_HEADS):
            out, b, t = tile(("q_nope", h), cq_hi, cq_lo, lambda k: cq_ready[k])
            q_nope_done = bank_read[b] = ACTE.do(lambda e, h=h, out=out: e.activation(q_nope[:, h, :], out, ACT.Copy, scale=MLA_SCALE), t, h_used)
        for j in range(4):
            b = odd_bank()
            for tt in range(TT):
                t = PE.do(lambda e, j=j, tt=tt, b=b: e.transpose(banks[b][:, tt * P:(tt + 1) * P], q_rot[:, tt, j * P:(j + 1) * P], identity), q_rot_done, bank_read[b])
            q_rope_done = bank_read[b] = ACTE.do(lambda e, j=j, b=b: e.activation(q_rope_T[:, j, :], banks[b][:, 0:T], ACT.Copy, scale=MLA_SCALE), t, h_used)
        for h in range(MLA_HEADS):
            out, b, t = tile(("k_nope", h), ckv_hi, ckv_lo, lambda k: ckv_ready[k])
            k_nope_done = bank_read[b] = ACTE.do(lambda e, h=h, out=out: e.activation(k_nope[:, h, :], out, ACT.Copy), t, h_used)
        for n in range(2):
            outs, pair, t = group(("mla_v", n), 512, ckv_hi, ckv_lo, lambda k: ckv_ready[k])
            for tt in range(TT):
                mla_v_done = bank_read[pair[tt]] = ACTE.do(lambda e, tt=tt, n=n, out=outs[tt]: e.activation(
                    mla_v[:, tt, n * 512:(n + 1) * 512], out, ACT.Copy), t, h_used)
        latents_used = t

        G = 8192
        g_a = place("g_a", FR, G, [P, T])
        g_b = place("g_b", FR, G + 1024, [P, T])
        g_sum = place("g_sum", FR, G + 2048, [P, T])
        g_kdn = place("g_kdn", FR, G + 3072, [P, TT, P])
        g_at = place("g_at", FR, G + 4096, [P, TT, P])
        g_state = place("g_state", FR, G + 5120, [P, N_CHUNKS - 1, GLA_V])
        g_junk = place("g_junk", FR, G + 8192, [P, GLA_V])
        b_last, decay, gla_ss, gla_rs = stats(N_CHUNKS), stats(N_CHUNKS), stats(GLA_HEADS * TT), stats(GLA_HEADS * TT)
        keep = param2("chunk_causal").bitcast(I32)
        restart = param2("chunk_restart")
        wgu, b_gate = param2("w_gate_up"), param("b_gate")
        C = GLA_CHUNK
        at_zero = DVE.do(lambda e: e.memset(g_at[:, :, :], 0.0), latents_used)
        prev_read = [latents_used, at_zero]
        prev_out = junk_written = None
        for h in range(GLA_HEADS):
            b = odd_bank()
            t = PE.do(lambda e, h=h, b=b: e.matmul(banks[b][:, 0:T], wgu[0:GATE_RANK, h * P:(h + 1) * P], a_lr[:, :], start=True, stop=True),
                      a_lr_done, params2_landed, bank_read[b])
            bg = b_gate[:, h:h + 1]
            t1 = DVE.do(lambda e, b=b, bg=bg: e.tensor_scalar(g_sum[:, :], banks[b][:, 0:T], bg, 0.0, ALU.add, ALU.min), t, prev_read)
            t2 = DVE.do(lambda e, b=b, bg=bg: e.tensor_scalar(g_b[:, :], banks[b][:, 0:T], bg, 0.0, ALU.add, ALU.max), t, prev_read)
            bank_read[b] = t2
            t = DVE.do(lambda e: e.tensor_tensor(g_a[:, :], g_sum[:, :], g_b[:, :], ALU.subtract), t1, t2)
            t = ACTE.do(lambda e: e.activation(g_a[:, :], g_a[:, :], ACT.Exp), t)
            t = DVE.do(lambda e: e.tensor_scalar(g_a[:, :], g_a[:, :], 1.0, None, ALU.add), t)
            t = ACTE.do(lambda e: e.activation(g_a[:, :], g_a[:, :], ACT.Ln), t)
            t = DVE.do(lambda e: e.tensor_tensor(g_a[:, :], g_sum[:, :], g_a[:, :], ALU.subtract), t)
            t = DVE.do(lambda e: e.tensor_tensor_scan(g_sum[:, :], restart, g_a[:, :], 0.0, ALU.mult, ALU.add), t)
            sums = t
            t = DVE.do(lambda e: e.tensor_scalar(b_last, g_sum[:, C - 1::C], 1.0 / GLA_TAU, None, ALU.mult), sums)
            dec = ACTE.do(lambda e: e.activation(decay, b_last, ACT.Exp), t)
            for n in range(N_CHUNKS):
                cs = slice(n * C, (n + 1) * C)
                u = ACTE.do(lambda e, n=n, cs=cs: e.activation(g_a[:, cs], g_sum[:, cs], ACT.Exp, scale=-1.0 / GLA_TAU, bias=b_last[:, n:n + 1]), t)
            kd = DVE.do(lambda e, h=h: e.tensor_tensor(gla_kd[:, h, :], gla_k[:, h, :], g_a[:, :], ALU.mult), u, gla_k_done)
            u = ACTE.do(lambda e: e.activation(g_b[:, :], g_sum[:, :], ACT.Exp, scale=1.0 / GLA_TAU), sums)
            qd = DVE.do(lambda e, h=h: e.tensor_tensor(gla_q[:, h, :], gla_q[:, h, :], g_b[:, :], ALU.mult), u, gla_q_done)
            u = ACTE.do(lambda e: e.activation(g_a[:, :], g_sum[:, :], ACT.Exp, scale=-1.0 / GLA_TAU), kd)
            ki = DVE.do(lambda e, h=h: e.tensor_tensor(gla_k[:, h, :], gla_k[:, h, :], g_a[:, :], ALU.mult), u)
            b = odd_bank()
            for tt in range(TT):
                t = PE.do(lambda e, h=h, tt=tt, b=b: e.transpose(banks[b][:, tt * P:(tt + 1) * P], gla_kd[:, h, tt * P:(tt + 1) * P], identity), kd, bank_read[b])
            kdn = bank_read[b] = ACTE.do(lambda e, b=b: e.activation(g_kdn[:, :, :].rearrange("p t c -> p (t c)"), banks[b][:, 0:T], ACT.Copy), t, prev_out)
            b = odd_bank()
            for tt in range(TT):
                t = PE.do(lambda e, h=h, tt=tt, b=b: e.matmul(banks[b][:, tt * P:(tt + 1) * P], gla_k[:, h, tt * P:(tt + 1) * P],
                                                              gla_q[:, h, tt * P:(tt + 1) * P], start=True, stop=True), ki, qd, bank_read[b])
            for tt in range(TT):
                a_done = DVE.do(lambda e, tt=tt, b=b: e.copy_predicated(g_at[:, tt, :], keep, banks[b][:, tt * P:(tt + 1) * P]), t, prev_out)
            bank_read[b] = a_done
            v_h = slice(h * GLA_V, (h + 1) * GLA_V)
            s_prev = None
            for n in range(N_CHUNKS - 1):
                b = TILE_BANKS[n % 2]
                rows = slice(C * (n % 2), C * (n % 2) + C)
                t = PE.do(lambda e, n=n, b=b, rows=rows, v_h=v_h: e.matmul(banks[b][:, 0:GLA_V], g_kdn[rows, n // 2, :], gla_v[rows, n // 2, v_h], start=True, stop=True),
                          kdn, gla_v_done, bank_read[b])
                if n == 0:
                    s_prev = DVE.do(lambda e, b=b: e.tensor_copy(g_state[:, 0, :], banks[b][:, 0:GLA_V]), t, prev_out)
                else:
                    s_prev = DVE.do(lambda e, b=b, n=n: e.scalar_tensor_tensor(g_state[:, n, :], g_state[:, n - 1, :], decay[:, n:n + 1], banks[b][:, 0:GLA_V], ALU.mult, ALU.add),
                                    t, s_prev, dec)
                bank_read[b] = s_prev
            for tt in range(TT):
                b = tt
                out = banks[b][:, 0:GLA_V]
                t = PE.do(lambda e, tt=tt, out=out, v_h=v_h: e.matmul(out, g_at[:, tt, :], gla_v[:, tt, v_h], start=True, stop=False, skip_group_check=True),
                          a_done, gla_v_done, bank_read[b])
                for n in (2 * tt, 2 * tt + 1):
                    if n == 0:
                        continue
                    rows = slice(C * (n % 2), C * (n % 2) + C)
                    t = PE.do(lambda e, n=n, h=h, b=b, rows=rows: e.matmul(banks[b][rows, 0:GLA_V], gla_q[:, h, n * C:(n + 1) * C], g_state[:, n - 1, :],
                                                                          start=False, stop=n % 2 == 1, skip_group_check=True), s_prev)
                i = h * TT + tt
                u = ACTE.do(lambda e, out=out, i=i: e.activation(g_junk[:, :], out, ACT.Square, accum_out=gla_ss[:, i:i + 1]), t, latents_used, junk_written)
                junk_written = u
                u = POOL.do(lambda e, i=i: e.tensor_scalar(gla_rs[:, i:i + 1], gla_ss[:, i:i + 1], 1.0 / GLA_V, EPS, ALU.mult, ALU.add), u)
                u = POOL.do(lambda e, i=i: e.tensor_tensor(gla_rs[:, i:i + 1], gla_rs[:, i:i + 1], minus_half, ALU.pow), u)
                gla_o_done = bank_read[b] = DVE.do(lambda e, out=out, i=i, tt=tt, v_h=v_h: e.scalar_tensor_tensor(
                    gla_o[:, tt, v_h], out, gla_rs[:, i:i + 1], gla_o[:, tt, v_h], ALU.mult, ALU.mult), u, gla_r_done)
            prev_out = t
            prev_read = [s_prev, kd, qd, ki, t]

        g_gla = param("g_gla")
        gla_ready = transpose_split(lambda tt, k: gla_o[:, tt, k * P:(k + 1) * P], KD // 2, lambda k: g_gla[:, k % 2:k % 2 + 1], None,
                                    lambda k: mix_hi[:, KD // 2 + k, :], lambda k: mix_lo[:, KD // 2 + k, :], work2, work2_free,
                                    lambda tt, k: gla_o_done, down_done)

        m_scores = place("m_scores", FR, G, [P, 2, T])
        m_T = place("m_T", FR, G + 2048, [P, TT, P])
        NM = MLA_HEADS * TT
        m_max, m_sum = stats(NM), stats(NM)
        m_units = [(h, tt) for h in range(MLA_HEADS) for tt in range(TT)]
        m_free = {"s": [gla_o_done, gla_o_done], "T": gla_o_done}

        def latent_scores(u):
            h, tt = m_units[u]
            n = P * (tt + 1)
            b = u % 2
            rows = slice(ROPE * (h % 2), ROPE * (h % 2) + ROPE)
            toks = slice(tt * P, (tt + 1) * P)
            PE.do(lambda e: e.matmul(banks[b][:, 0:n], q_nope[:, h, toks], k_nope[:, h, 0:n], start=True, stop=False),
                  q_nope_done, k_nope_done, bank_read[b], signal=False)
            t = PE.do(lambda e: e.matmul(banks[b][:, 0:n], q_rope_T[rows, h // 2, toks], k_rope_x[rows, 0:n], start=False, stop=True),
                      q_rope_done, k_rope_done)
            s = m_scores[:, u % 2, 0:n]
            t = DVE.do(lambda e: e.tensor_tensor(s, banks[b][:, 0:n], causal[:, T - n:T], ALU.add), t, m_free["s"][u % 2], prev_out)
            bank_read[b] = t
            t = DVE.do(lambda e: e.tensor_reduce(m_max[:, u:u + 1], s, AX.X, ALU.max, negate=True), t)
            t = ACTE.do(lambda e: e.activation(s, s, ACT.Exp, bias=m_max[:, u:u + 1], accum_out=m_sum[:, u:u + 1]), t)
            t = DVE.do(lambda e: e.reciprocal(m_sum[:, u:u + 1], m_sum[:, u:u + 1]), t)
            return DVE.do(lambda e: e.tensor_scalar(s, s, m_sum[:, u:u + 1], None, ALU.mult), t)

        def latent_output(u, p_done):
            h, tt = m_units[u]
            for sb in range(tt + 1):
                t = PE.do(lambda e, sb=sb: e.transpose(banks[3][:, sb * P:(sb + 1) * P], m_scores[:, u % 2, sb * P:(sb + 1) * P], identity),
                          p_done, bank_read[3])
            m_free["s"][u % 2] = t
            wt = bank_read[3] = ACTE.do(lambda e: e.activation(m_T[:, 0:tt + 1, :].rearrange("p a c -> p (a c)"), banks[3][:, 0:(tt + 1) * P], ACT.Copy), t, m_free["T"])
            for sb in range(tt + 1):
                t = PE.do(lambda e, sb=sb: e.matmul(banks[2][:, 0:P], mla_v[:, sb, h * NOPE:(h + 1) * NOPE], m_T[:, sb, :], start=sb == 0, stop=sb == tt),
                          wt, mla_v_done, bank_read[2])
            m_free["T"] = t
            toks = slice(tt * P, (tt + 1) * P)
            t = bank_read[2] = split(mix_hi[:, h, toks], mix_lo[:, h, toks], banks[2][:, 0:P], t, down_done)
            return t

        pending = None
        for u in range(NM):
            p_done = latent_scores(u)
            if pending is not None:
                latent_output(*pending)
            pending = (u, p_done)
        mla_ready = latent_output(*pending)

        def gated_residual(gate_v, o_done, folded_token, after_junk, free_after):
            rs, rs_done = rms_factors(lambda tt: wide[:, tt, :], D, lambda tt: junk[:, :], lambda tt: [o_done[tt], after_junk])
            t = broadcast_row(lambda k: ada(gate_v)[:, k:k + 1], 0, diag, free_after, folded_token)
            done = [None, None]
            for tt in range(TT):
                for q in range(4):
                    w_q, x_q = wide[:, tt, q * 512:(q + 1) * 512], x[:, tt, q * 512:(q + 1) * 512]
                    u = bank_read[q] = DVE.do(lambda e, tt=tt, q=q, w_q=w_q: e.scalar_tensor_tensor(w_q, w_q, rs[:, tt:tt + 1], banks[q][:, :], ALU.mult, ALU.mult), rs_done[tt], t)
                    done[tt] = DVE.do(lambda e, w_q=w_q, x_q=x_q: e.tensor_tensor(x_q, x_q, w_q, ALU.add), u)
            return done

        mixed = [gla_ready[-1], mla_ready]
        o_done = fresh_groups(("out2",), mix_hi, mix_lo, mixed, wide, gla_ready[-1])
        attn_free = [mla_ready, mla_ready]
        x_done = gated_residual(2, o_done, folded_gate, mla_ready, attn_free)
        h_ready = norm_to_h(x_done, lambda k: ada(4)[:, k:k + 1], lambda k: ada(3)[:, k:k + 1], work2, work2_free,
                            mla_ready, [folded_ffn, x_done[0], x_done[1]])
        x_mid = x_done

        sw_g = place("sw_g", FR, 2048, [P, 2, T])
        sw_free = [h_ready[-1], h_ready[-1]]
        for half in range(2):
            ff_done = []
            for j in range(FF_HALF * half, FF_HALF * (half + 1)):
                s = j % 2
                out_g, bg, t = tile(("gate", j), h_hi, h_lo, h_of)
                t = bank_read[bg] = ACTE.do(lambda e, s=s, out=out_g: e.activation(sw_g[:, s, :], out, ACT.Silu), t, sw_free[s])
                out_u, bu, tu = tile(("up", j), h_hi, h_lo, h_of)
                t = bank_read[bu] = DVE.do(lambda e, s=s, out=out_u: e.tensor_tensor(sw_g[:, s, :], out, sw_g[:, s, :], ALU.mult), t, tu)
                jj = j - FF_HALF * half
                t = sw_free[s] = split(ff_hi[:, jj, :], ff_lo[:, jj, :], sw_g[:, s, :], t)
                ff_done.append(t)
            after = lambda k, d=ff_done: d[k]
            if half == 0:
                o_done = fresh_groups(("down2", 0), ff_hi, ff_lo, after, wide, h_ready[-1])
                first_done = o_done
                DVE.wait(*first_done)
            else:
                o_done = residual_groups(("down2", 1), ff_hi, ff_lo, after, wide)
        x_done = gated_residual(5, o_done, folded_gate_ffn, h_ready[-1], [h_ready[-1], h_ready[-1]])
        stored = sem("stored")
        for tt in range(TT):
            SP.wait(x_done[tt])
            SP.steps.append(lambda e, tt=tt: e.dma_start(OUT[tt * P:(tt + 1) * P, :], x[:, tt, :]).then_inc(stored, 16))
        SP.wait(("stored", stored, 16 * TT))

        assert state["prepared"] == state["loaded"] == len(widths), state
        assert not any(pieces_left[i] for i in range(len(widths)) if plan.kinds[i] == "split")

        block = ctx.enter_context(nc.Block())

        @block.sync
        def _(e):
            SP.play(e)

        @block.gpsimd
        def _(e):
            POOL.play(e)

        @block.scalar
        def _(e):
            ACTE.play(e)

        @block.vector
        def _(e):
            DVE.play(e)

        @block.tensor
        def _(e):
            PE.play(e)



def bucket_of(distance):
    n = np.maximum(distance, 0)
    exact = BUCKETS // 2
    nf = np.maximum(n, 1).astype(np.float32)
    large = exact + (np.log(nf / np.float32(exact)) / np.float32(np.log(MAX_DISTANCE / exact)) * (BUCKETS - exact)).astype(np.int32)
    return np.where(n < exact, n, np.minimum(large, BUCKETS - 1))


def by_partition(v):
    return np.ascontiguousarray(v.reshape(-1, P).T)


def pack(table, values):
    out = np.zeros((P, table["_width"]), np.float32)
    for name, v in values.items():
        a, b = table[name]
        out[:v.shape[0], a:b] = v
    return out


def layout(i):
    mats = {
        "w_in_v": np.concatenate([i["w_in"][0][:, 1024 + 512 * br + 256:1024 + 512 * br + 512] for br in (1, 2)], 1),
        "w_ada": i["w_ada_2"][0], "w_out": i["w_out"][0], "w_up": i["w_up"][0], "w_down": i["w_down"][0],
        "w_in_2": i["w_in_2"][0], "w_uk": i["w_uk_2"][0], "w_uv": i["w_uv_2"][0], "w_out_2": i["w_out_2"][0],
        "w_ffn_gate": i["w_ffn_gate_2"][0], "w_ffn_up": i["w_ffn_up_2"][0], "w_ffn_down": i["w_ffn_down_2"][0],
    }
    w_in = i["w_in"][0]
    mats["w_in"] = np.concatenate([w_in[:, q_columns()], w_in[:, HEADS * DH:]], 1)
    latent = Q_RANK + KV_RANK + ROPE
    a_g = latent + 2 * GLA_HEADS * GLA_K + GLA_HEADS * GLA_V
    w2 = mats["w_in_2"]
    mats["w_in_2_kv"] = np.concatenate([w2[:, Q_RANK:latent], w2[:, a_g:a_g + GATE_RANK]], 1)
    uq = i["w_uq_2"][0].reshape(Q_RANK, MLA_HEADS, NOPE + ROPE)
    mats["w_uq_nope"] = uq[:, :, :NOPE].reshape(Q_RANK, -1)
    mats["w_uq_rope"] = uq[:, :, NOPE:].reshape(Q_RANK, -1)
    w1 = i["cmp_w1"][0].reshape(2, CMP_LEN, DH, DH).transpose(2, 0, 1, 3).reshape(DH, -1)
    mats["cmp_w1"] = np.concatenate([w1, w1], 0)
    plan = make_plan()
    weights = np.empty(P * sum(chunk_widths(plan)), np.float32)
    at = 0
    for chunk in plan.chunks:
        w = sum(c[3] for c in chunk)
        view = weights[at:at + P * w].reshape(P, w)
        c0 = 0
        for mat, kt, col, n in chunk:
            view[:, c0:c0 + n] = mats[mat][kt * P:(kt + 1) * P, col:col + n]
            c0 += n
        at += P * w
    p, c = np.arange(P)[:, None], np.arange(2 * P)[None, :]
    conv_w = lambda w: w.T.reshape(-1, P, w.shape[0]).transpose(1, 0, 2).reshape(P, -1)
    lasting = pack(LASTING, {
        "identity": np.eye(P), "ones": np.ones((P, P)),
        "causal": np.where(P + p - c >= 0, 0.0, MASKED),
        "mix_norm_g": by_partition(i["mix_norm_g"][0]), "ffn_norm_g": by_partition(i["ffn_norm_g"][0]),
        "final_norm_g": by_partition(i["final_norm_g"]), "g_pre_mix": by_partition(i["g_pre_mix_2"][0]),
        "g_post_mix": by_partition(i["g_post_mix_2"][0]), "g_pre_ffn": by_partition(i["g_pre_ffn_2"][0]),
        "g_post_ffn": by_partition(i["g_post_ffn_2"][0]), "b_ada": by_partition(i["b_ada_2"][0]),
        "c": by_partition(i["c_2"][0]), "ffn_conv_w": conv_w(i["ffn_conv_w"][0]),
        "ffn_conv_b": by_partition(i["ffn_conv_b"][0]), "g_q": by_partition(i["g_q_2"][0]),
        "g_kv": by_partition(i["g_kv_2"][0]), "b_gate": by_partition(i["b_gate_2"][0]),
        "g_gla": by_partition(i["g_gla_2"][0]),
    })
    distance = np.arange(N_DIST) - DIST0
    one_hot = np.zeros((BUCKETS + 1, N_DIST), np.float32)
    one_hot[bucket_of(distance), np.arange(N_DIST)] = distance >= 0
    one_hot[BUCKETS] = distance < 0
    rel = np.concatenate([i["rel_bias"], np.full((1, HEADS), MASKED, np.float32)], 0)
    twice = lambda a: np.concatenate([a, a], 0)
    phase1 = pack(PHASE1, {
        "one_hot": one_hot, "rel_bias": rel,
        "cmp_w2": twice(i["cmp_w2"][0].transpose(1, 0, 2).reshape(DH, -1)),
        "cmp_pos": twice(i["cmp_pos"][0].transpose(2, 0, 1).reshape(DH, -1)),
        "conv_w": conv_w(i["conv_w"][0]), "conv_b": by_partition(i["conv_b"][0]),
        "conv_ln_g": by_partition(i["conv_ln_g"][0]), "conv_ln_b": by_partition(i["conv_ln_b"][0]),
        "any_block": (np.arange(T) >= CMP_LEN - 1).astype(np.float32).reshape(TT, P).T,
    })
    q, k = np.arange(P)[None, :], np.arange(P)[:, None]
    same = (q // GLA_CHUNK == k // GLA_CHUNK) & (k <= q)
    inv_freq = (1.0 / (np.float32(10000.0) ** (np.arange(0, ROPE, 2, dtype=np.float32) / np.float32(ROPE)))).astype(np.float32)
    phase2 = pack(PHASE2, {
        "w_gate_up": i["w_gate_up_2"][0], "inv_freq": np.broadcast_to(inv_freq, (P, ROPE2)),
        "chunk_restart": np.broadcast_to((np.arange(T) % GLA_CHUNK != 0).astype(np.float32), (P, T)),
        "chunk_causal": same.astype(np.float32),
    })
    return {
        "weights": weights, "x": np.ascontiguousarray(i["x"][0]), "params": lasting, "params1": phase1,
        "params2": phase2, "positions": np.ascontiguousarray(i["positions_2"][0].reshape(TT, P).T),
    }


def kernel(**inputs):
    import concourse.bacc as bacc
    from concourse.bass_utils import run_bass_kernel_spmd

    arrays = layout({name: np.asarray(v) for name, v in inputs.items()})
    nc = bacc.Bacc("TRN2", target_bir_lowering=False, num_devices=1)
    args = [nc.dram_tensor(name, a.shape, mybir.dt.from_np(a.dtype), kind="ExternalInput").ap()
            for name, a in arrays.items()]
    out = nc.dram_tensor("out", (T, D), F32, kind="ExternalOutput").ap()
    two_blocks(nc, *args, out)
    r = run_bass_kernel_spmd(nc, [arrays], core_ids=[0])
    return r.results[0]["out"].reshape(1, T, D)
```

```python
import concourse.bass as bass
from concourse import mybir
from contextlib import ExitStack
import numpy as np

F32 = mybir.dt.float32
F32R = mybir.dt.float32r
I32 = mybir.dt.int32
ALU = mybir.AluOpType
ACT = mybir.ActivationFunctionType
AX = mybir.AxisListType

P = 128
T = 256
TT = T // P
D = 2048
KD = D // P
HALF = 1024

HEADS, KV_HEADS, GQA, DH = 16, 4, 4, 64
CMP_LEN, CMP_STRIDE = 32, 16
NCMP = T // CMP_STRIDE - CMP_LEN // CMP_STRIDE + 1
N_BRANCH = 3
BUCKETS, MAX_DISTANCE = 32, 128
CONV_TAPS, CONV_CH = 31, 1024
CONV_TILES = CONV_CH // P
DFF = 5632
FF_TILES = DFF // P
FF_HALF = FF_TILES // 2
EPS = 1e-6
MASKED = -1e30

MLA_HEADS, Q_RANK, KV_RANK, NOPE, ROPE = 8, 512, 256, 128, 64
ROPE2 = ROPE // 2
MLA_SCALE = float(np.float32((NOPE + ROPE) ** -0.5))
GLA_HEADS, GLA_K, GLA_V, GLA_CHUNK, GATE_RANK = 4, 128, 256, 64, 16
N_CHUNKS = T // GLA_CHUNK
GLA_TAU = 16.0

CHUNK = 1024
RAW_SLOTS = 7
PART_SLOTS = 4
AHEAD = PART_SLOTS - 1



def q_columns():
    cols = []
    for pair in range(KV_HEADS // 2):
        for g in range(GQA):
            for hk in (2 * pair, 2 * pair + 1):
                h = hk * GQA + g
                cols += range(h * DH, (h + 1) * DH)
    return cols


def query_place(h):
    hk, g = divmod(h, GQA)
    return (hk // 2) * GQA + g, DH * (hk % 2)


MIX_ORDER = [*range(KD // 2, KD), *range(KD // 2)]


class Plan:

    def __init__(self):
        self.chunks = []
        self.kinds = []
        self.groups = {}
        self.ada = [(v, half, kt) for v in range(6) for half in range(2) for kt in range(KD)]
        self.rate = 0.0
        self.due = 0.0
        self.keep = 0
        self.open = False

    def new_chunk(self, kind):
        self.chunks.append([])
        self.kinds.append(kind)
        self.open = kind == "split"

    def put_ada(self):
        v, half, kt = self.ada.pop(0)
        self.new_chunk("ada")
        self.chunks[-1].append(("w_ada", kt, v * D + half * HALF, HALF))

    def piece(self, mat, kt, col, n):
        used = sum(x[3] for x in self.chunks[-1]) if self.open else CHUNK
        if used + n > CHUNK:
            self.due += self.rate
            while self.due >= 1 and len(self.ada) > self.keep:
                self.put_ada()
                self.due -= 1
            self.new_chunk("split")
            used = 0
        self.chunks[-1].append((mat, kt, col, n))
        return len(self.chunks) - 1, used, kt

    def project(self, key, mat, col, n, k0=0, nk=KD, order=None):
        self.groups[key] = [self.piece(mat, kt, col, n) for kt in order or range(k0, k0 + nk)]

    def raw(self, key, mat, pieces):
        self.groups[key] = []
        for c in range(pieces):
            self.new_chunk("raw")
            self.chunks[-1].append((mat, 0, c * CHUNK, CHUNK))
            self.groups[key].append(len(self.chunks) - 1)

    def ada_until(self, left, rate):
        self.keep, self.rate = left, rate

    def finish_ada(self):
        while len(self.ada) > self.keep:
            self.put_ada()


def make_plan():
    p = Plan()
    kv = HEADS * DH
    for s in range(2):
        for j in range(2):
            p.project(("cmp", s, j), "w_in", kv + 256 * s + P * j, P)
    p.raw("cmp_w1", "cmp_w1", 2 * CMP_LEN * DH // CHUNK)
    for br in (1, 2):
        for j in range(2):
            p.project(("key", br, j), "w_in", kv + 512 * br + P * j, P)
    for j in range(8):
        p.project(("query", j), "w_in", P * j, P)
    p.project("value", "w_in_v", 0, 512)
    gates = kv + N_BRANCH * 512
    p.project("gates", "w_in", gates, N_BRANCH * HEADS)
    conv = gates + N_BRANCH * HEADS
    for j in range(CONV_TILES):
        p.project(("conv_a", j), "w_in", conv + P * j, P)
        p.project(("conv_g", j), "w_in", conv + CONV_CH + P * j, P)
    for n in range(4):
        p.project(("out1", n), "w_out", 512 * n, 512, order=MIX_ORDER)
        p.ada_until(2 * 2 * KD, 0.46)
    for half in range(2):
        for j in range(FF_HALF * half, FF_HALF * (half + 1)):
            p.project(("up_a", j), "w_up", P * j, P)
            p.project(("up_g", j), "w_up", DFF + P * j, P)
        for n in range(4):
            p.project(("down1", half, n), "w_down", 512 * n, 512, FF_HALF * half, FF_HALF)
    p.finish_ada()
    p.project("c_q", "w_in_2", 0, Q_RANK)
    p.project("c_kv", "w_in_2_kv", 0, KV_RANK + ROPE + GATE_RANK)
    at = Q_RANK + KV_RANK + ROPE
    for h in range(GLA_HEADS):
        p.project(("gla_q", h), "w_in_2", at + P * h, P)
    at += GLA_HEADS * GLA_K
    for h in range(GLA_HEADS):
        p.project(("gla_k", h), "w_in_2", at + P * h, P)
    at += GLA_HEADS * GLA_K
    for n in range(2):
        p.project(("gla_v", n), "w_in_2", at + 512 * n, 512)
    at += GLA_HEADS * GLA_V + GATE_RANK
    for n in range(2):
        p.project(("gla_r", n), "w_in_2", at + 512 * n, 512)
    p.project("q_rope", "w_uq_rope", 0, MLA_HEADS * ROPE, 0, Q_RANK // P)
    for h in range(MLA_HEADS):
        p.project(("q_nope", h), "w_uq_nope", P * h, P, 0, Q_RANK // P)
    for h in range(MLA_HEADS):
        p.project(("k_nope", h), "w_uk", P * h, P, 0, KV_RANK // P)
    for n in range(2):
        p.project(("mla_v", n), "w_uv", 512 * n, 512, 0, KV_RANK // P)
    for n in range(4):
        p.project(("out2", n), "w_out_2", 512 * n, 512, order=MIX_ORDER)
        p.ada_until(2 * KD, 1.0)
    p.finish_ada()
    p.ada_until(0, 0.2)
    for half in range(2):
        for j in range(FF_HALF * half, FF_HALF * (half + 1)):
            p.project(("gate", j), "w_ffn_gate", P * j, P)
            p.project(("up", j), "w_ffn_up", P * j, P)
        for n in range(4):
            p.project(("down2", half, n), "w_ffn_down", 512 * n, 512, FF_HALF * half, FF_HALF)
    return p


def chunk_widths(plan):
    return [sum(x[3] for x in c) for c in plan.chunks]



def fields(sizes):
    at, out = 0, {}
    for name, n in sizes:
        out[name] = (at, at + n)
        at += n
    out["_width"] = at
    return out


LASTING = fields([
    ("identity", P), ("ones", P), ("causal", 2 * P), ("mix_norm_g", KD), ("ffn_norm_g", KD),
    ("final_norm_g", KD), ("g_pre_mix", KD), ("g_post_mix", KD), ("g_pre_ffn", KD),
    ("g_post_ffn", KD), ("b_ada", 6 * KD), ("c", KD), ("ffn_conv_w", 3 * 2 * FF_TILES),
    ("ffn_conv_b", 2 * FF_TILES), ("g_q", Q_RANK // P), ("g_kv", KV_RANK // P),
    ("b_gate", GLA_HEADS), ("g_gla", GLA_V // P),
])
N_DIST = 2 * T
DIST0 = 2 * P - 1
ROW = 3 * P
PHASE1 = fields([
    ("one_hot", N_DIST), ("one_hot_down", ROW), ("rel_bias", HEADS), ("cmp_w2", 2 * DH), ("cmp_pos", 2 * CMP_LEN),
    ("conv_w", CONV_TILES * CONV_TAPS), ("conv_b", CONV_TILES), ("conv_ln_g", CONV_TILES),
    ("conv_ln_b", CONV_TILES), ("any_block", TT),
])
PHASE2 = fields([
    ("w_gate_up", GLA_HEADS * GLA_K), ("chunk_restart", T), ("inv_freq", ROPE2),
    ("chunk_causal", P),
])



class Line:

    def __init__(self, sem, name):
        self.sem, self.name, self.count, self.seen, self.steps = sem, name, 0, {}, []

    def wait(self, *tokens):
        for t in tokens:
            if t is None:
                continue
            if isinstance(t, list):
                self.wait(*t)
                continue
            name, sem, value = t
            if self.seen.get(name, 0) < value:
                self.seen[name] = value
                self.steps.append(lambda e, s=sem, v=value: e.wait_ge(s, v))

    def do(self, step, *after, signal=True):
        self.wait(*after)
        if not signal:
            self.steps.append(step)
            return None
        self.count += 1
        self.steps.append(lambda e: step(e).then_inc(self.sem, 1))
        return self.name, self.sem, self.count

    def play(self, engine):
        for step in self.steps:
            step(engine)


def two_blocks(nc, WEIGHTS, X, PARAMS, PARAMS1, PARAMS2, POSITIONS, OUT):
    plan = make_plan()
    widths = chunk_widths(plan)
    starts = [P * s for s in np.concatenate([[0], np.cumsum(widths)]).tolist()]

    ctx = ExitStack()
    with ctx:
        base = -(-nc.sbuf_base // 64) * 64
        at = {}
        cursor = base
        LAST_BYTES = -(-LASTING["_width"] * 4 // 64) * 64
        PHASE_BYTES = -(-max(PHASE1["_width"], PHASE2["_width"]) * 4 // 64) * 64
        for name, size in (
            ("raw", RAW_SLOTS * CHUNK * 4), ("hi", PART_SLOTS * CHUNK * 4), ("lo", PART_SLOTS * CHUNK * 4),
            ("h", 2 * KD * T * 4), ("mid", 2 * FF_HALF * T * 4), ("x", TT * D * 4), ("wide", TT * D * 4),
            ("acc", 2 * HALF * 4), ("last", LAST_BYTES), ("phase", PHASE_BYTES), ("stat", 2048),
        ):
            at[name] = cursor
            cursor += size
        at["free"] = cursor
        assert nc.sbuf_usable_end - cursor >= 19 * 1024, nc.sbuf_usable_end - cursor

        def place(name, region, offset, shape, dt=F32):
            return nc.alloc_sbuf_tensor_at(name, shape, dt, offset=at[region] + offset)

        raw = place("raw", "raw", 0, [P, RAW_SLOTS, CHUNK])
        w_hi = place("w_hi", "hi", 0, [P, PART_SLOTS, CHUNK], F32R)
        w_lo = place("w_lo", "lo", 0, [P, PART_SLOTS, CHUNK], F32R)
        h_hi = place("h_hi", "h", 0, [P, KD, T], F32R)
        h_lo = place("h_lo", "h", KD * T * 4, [P, KD, T], F32R)
        mix_hi = place("mix_hi", "mid", 0, [P, KD, T], F32R)
        mix_lo = place("mix_lo", "mid", KD * T * 4, [P, KD, T], F32R)
        ff_hi = place("ff_hi", "mid", 0, [P, FF_HALF, T], F32R)
        ff_lo = place("ff_lo", "mid", FF_HALF * T * 4, [P, FF_HALF, T], F32R)
        mid_tail = 2 * KD * T * 4
        x = place("x", "x", 0, [P, TT, D])
        wide = place("wide", "wide", 0, [P, TT, D])
        ada_acc = place("ada_acc", "acc", 0, [P, 2, HALF])
        lasting = place("lasting", "last", 0, [P, LASTING["_width"]])
        stat = place("stat", "stat", 0, [P, 512])

        def param(name):
            a, b = LASTING[name]
            return lasting[:, a:b]

        identity, ones, causal = param("identity"), param("ones"), param("causal")

        stat_used = [0]

        def stats(n):
            a = stat_used[0]
            stat_used[0] += n
            assert stat_used[0] <= 512
            return stat[:, a:a + n]

        banks = [ctx.enter_context(nc.psum_tensor(f"bank{b}", [P, 512], F32)) for b in range(8)]
        bank_read = [None] * 8
        ODD_BANKS = (6, 7)

        def sem(name):
            return ctx.enter_context(nc.semaphore(name))

        PE = Line(sem("pe_done"), "pe")
        DVE = Line(sem("dve_done"), "dve")
        ACTE = Line(sem("act_done"), "act")
        POOL = Line(sem("pool_done"), "pool")
        SP = Line(sem("sp_done"), "sp")
        raw_sems = [sem(f"raw_landed{i}") for i in range(RAW_SLOTS)]

        def load(name, dst, src, *after, line=None):
            s = sem(name)
            (line or SP).wait(*after)
            (line or SP).steps.append(lambda e: e.dma_start(dst, src).then_inc(s, 16))
            return name, s, 16

        minus_half = stats(1)
        minus_half_done = POOL.do(lambda e: e.memset(minus_half, -0.5))

        released = [None] * len(widths)
        part_of = {}
        part_used = []
        pieces_left = [len(c) for c in plan.chunks]
        state = {"loaded": 0, "prepared": 0, "ada": None, "ada_slot": [None, None]}
        deferred = []

        def arrived(i):
            return f"raw{i % RAW_SLOTS}", raw_sems[i % RAW_SLOTS], 16 * (i // RAW_SLOTS + 1)

        def load_chunks():
            while state["loaded"] < len(widths):
                i = state["loaded"]
                if i >= RAW_SLOTS:
                    if released[i - RAW_SLOTS] is None:
                        return
                    SP.wait(released[i - RAW_SLOTS])
                src = WEIGHTS[starts[i]:starts[i + 1]].rearrange("(p w) -> p w", p=P)
                dst = raw[:, i % RAW_SLOTS, 0:widths[i]]
                SP.steps.append(lambda e, d=dst, s=src, k=i % RAW_SLOTS: e.dma_start(d, s).then_inc(raw_sems[k], 16))
                state["loaded"] += 1

        def split(dst_hi, dst_lo, src, *after):
            hi = ACTE.do(lambda e: e.activation(dst_hi, src, ACT.Copy), *after)
            return DVE.do(lambda e: e.tensor_tensor(dst_lo, src, dst_hi.bitcast(F32), ALU.subtract), hi)

        def prepare(upto):
            while state["prepared"] <= min(upto, len(widths) - 1):
                i = state["prepared"]
                src = raw[:, i % RAW_SLOTS, 0:widths[i]]
                if plan.kinds[i] == "split":
                    n = len(part_of)
                    slot_free = part_used[n - PART_SLOTS] if n >= PART_SLOTS else None
                    slot = n % PART_SLOTS
                    token = split(w_hi[:, slot, 0:widths[i]], w_lo[:, slot, 0:widths[i]], src, arrived(i), slot_free)
                    part_of[i] = slot, token
                    released[i] = token
                elif plan.kinds[i] == "ada":
                    released[i] = ada_step(i, src)
                state["prepared"] += 1
                load_chunks()

        vectors = {}

        def ada_step(i, src):
            _, kt, col, _ = plan.chunks[i][0]
            v, half = col // D, (col % D) // HALF
            slot = (2 * v + half) % 2
            acc, s = ada_acc[:, slot, :], silu_c[:, kt:kt + 1]
            if kt == 0:
                t = DVE.do(lambda e: e.tensor_scalar(acc, src, s, None, ALU.mult), arrived(i),
                           state["ada_slot"][slot], silu_c_done)
            else:
                t = DVE.do(lambda e: e.scalar_tensor_tensor(acc, src, s, acc, ALU.mult, ALU.add),
                           arrived(i), state["ada"])
            state["ada"] = t
            if kt == KD - 1:
                deferred.append([AHEAD + 1, v, half, slot, t])
                state["ada_slot"][slot] = "pending"
            return t

        def ada_reduce(v, half, slot, acc_done):
            b = ODD_BANKS[0]
            n = HALF // P
            for k in range(n):
                t = PE.do(lambda e, k=k: e.matmul(banks[b][:, k:k + 1], ada_acc[:, slot, k * P:(k + 1) * P],
                                                  ones[:, 0:1], start=True, stop=True),
                          acc_done, bank_read[b], signal=k == n - 1)
            state["ada_slot"][slot] = t
            lo, hi = LASTING["b_ada"][0] + v * KD + half * n, LASTING["b_ada"][0] + v * KD + (half + 1) * n
            t = DVE.do(lambda e: e.tensor_tensor(lasting[:, lo:hi], banks[b][:, 0:n], lasting[:, lo:hi], ALU.add), t)
            bank_read[b] = t
            vectors[v, half] = t

        def run_deferred(now=False):
            while deferred and (now or deferred[0][0] <= 0):
                ada_reduce(*deferred.pop(0)[1:])
            for d in deferred:
                d[0] -= 1

        def piece_used(i, token):
            pieces_left[i] -= 1
            if pieces_left[i] == 0:
                part_used.append(token)
                run_deferred()

        def parts(i, off, n):
            slot, _ = part_of[i]
            return w_hi[:, slot, off:off + n], w_lo[:, slot, off:off + n]

        def projection(key, n, out_of, outs, act_hi, act_lo, after, tile):
            got = plan.groups[key]
            base_k = min(kt for _, _, kt in got)
            last = None
            for at_piece, (i, off, kt) in enumerate(got):
                prepare(i)
                k = kt - base_k
                hi, lo = parts(i, off, n)
                ends = pieces_left[i] == 1
                first_k, last_k = at_piece == 0, at_piece == len(got) - 1
                need = after(k) if callable(after) else after
                for o, out in enumerate(outs):
                    if tile:
                        a_hi, a_lo = act_hi[:, k, :], act_lo[:, k, :]
                        trio = ((hi, a_hi), (hi, a_lo), (lo, a_hi))
                    else:
                        a_hi, a_lo = act_hi[:, k, o * P:(o + 1) * P], act_lo[:, k, o * P:(o + 1) * P]
                        trio = ((a_hi, hi), (a_hi, lo), (a_lo, hi))
                    for q, (s, m) in enumerate(trio):
                        final = o == len(outs) - 1 and q == 2
                        last = PE.do(lambda e, s=s, m=m, out=out, st=first_k and q == 0, en=last_k and q == 2:
                                     e.matmul(out, s, m, start=st, stop=en),
                                     part_of[i][1], need, [bank_read[b] for b in out_of] if first_k else None,
                                     signal=final and (ends or last_k))
                if ends:
                    piece_used(i, last)
                    prepare(i + AHEAD)
                    if not last_k:
                        yield
                else:
                    pieces_left[i] -= 1
            return last

        turn = {"tile": 0, "group": 0, "odd": 0}
        use = {"tile": (4, 5, 2, 3), "group": ((0, 1), (2, 3))}

        def tile_steps(key, act_hi, act_lo, after):
            b = use["tile"][turn["tile"] % len(use["tile"])]
            turn["tile"] += 1
            out = banks[b][:, 0:T]
            return out, b, (yield from projection(key, P, [b], [out], act_hi, act_lo, after, True))

        def group_steps(key, n, act_hi, act_lo, after):
            pair = use["group"][turn["group"] % len(use["group"])]
            turn["group"] += 1
            outs = [banks[b][:, 0:n] for b in pair]
            return outs, pair, (yield from projection(key, n, list(pair), outs, act_hi, act_lo, after, False))

        def finish(steps):
            while True:
                try:
                    next(steps)
                except StopIteration as end:
                    return end.value

        def tile(*args):
            return finish(tile_steps(*args))

        def group(*args):
            return finish(group_steps(*args))

        class Beside:

            def __init__(self, *stages):
                self.stages = list(stages)

            def step(self, n=1):
                while n > 0 and self.stages:
                    try:
                        next(self.stages[0])
                        n -= 1
                    except StopIteration:
                        self.stages.pop(0)

            def finish(self):
                while self.stages:
                    self.step()

        def odd_bank():
            b = ODD_BANKS[turn["odd"] % 2]
            turn["odd"] += 1
            return b

        def rms_power(out, squares, n, after):
            t = POOL.do(lambda e: e.tensor_scalar(out, squares, 1.0 / n, EPS, ALU.mult, ALU.add), after)
            return POOL.do(lambda e: e.tensor_tensor(out, out, minus_half, ALU.pow), t, minus_half_done)

        def rms_factors(src, n, junk, after):
            out, tokens, sq = stats(TT), [], stats(TT)
            t_act = None
            for tt in range(TT):
                t = t_act = ACTE.do(lambda e, tt=tt: e.activation(junk(tt), src(tt), ACT.Square, accum_out=sq[:, tt:tt + 1]),
                                    after(tt), t_act)
                tokens.append(rms_power(out[:, tt:tt + 1], sq[:, tt:tt + 1], n, t))
            return out, tokens

        class RowSquares:

            def __init__(self, junk, junk_free):
                self.parts, self.sum, self.out = stats(TT * 4), stats(TT), stats(TT)
                self.junk, self.junk_free, self.last = junk, junk_free, [None] * TT

            def add(self, tt, n, src, after):
                col = self.parts[:, tt * 4 + n:tt * 4 + n + 1]
                self.junk_free = self.last[tt] = ACTE.do(
                    lambda e: e.activation(self.junk, src, ACT.Square, accum_out=col), after, self.junk_free)

            def factors(self):
                tokens = []
                for tt in range(TT):
                    s, out = self.sum[:, tt:tt + 1], self.out[:, tt:tt + 1]
                    t = DVE.do(lambda e, tt=tt, s=s: e.tensor_reduce(s, self.parts[:, tt * 4:tt * 4 + 4], AX.X, ALU.add), self.last[tt])
                    tokens.append(rms_power(out, s, D, t))
                return self.out, tokens

        def transpose_split(src, nk, gain, shift, dst_hi, dst_lo, work, work_free, after, dst_free=None):
            done = []
            for k in range(nk):
                b = odd_bank()
                for tt in range(TT):
                    t = PE.do(lambda e, tt=tt, k=k, b=b: e.transpose(banks[b][:, tt * P:(tt + 1) * P], src(tt, k), identity),
                              after(tt, k), bank_read[b], signal=tt == TT - 1)
                g, hi, lo = gain(k), dst_hi(k), dst_lo(k)
                if shift is None:
                    t = ACTE.do(lambda e, b=b, hi=hi, g=g: e.activation(hi, banks[b][:, 0:T], ACT.Copy, scale=g), t, dst_free)
                    t = DVE.do(lambda e, b=b, hi=hi, lo=lo, g=g: e.scalar_tensor_tensor(lo, banks[b][:, 0:T], g, hi.bitcast(F32), ALU.mult, ALU.subtract), t)
                    bank_read[b] = t
                else:
                    tmp, free = work[:, k % 2, :], work_free[k % 2]
                    t = ACTE.do(lambda e, b=b, tmp=tmp, g=g, s=shift(k): e.activation(tmp, banks[b][:, 0:T], ACT.Identity, scale=g, bias=s), t, free)
                    bank_read[b] = t
                    if k % 2:
                        t = split(hi, lo, tmp, t, dst_free)
                    else:
                        t = DVE.do(lambda e, hi=hi, tmp=tmp: e.tensor_copy(hi, tmp), t, dst_free)
                        t = DVE.do(lambda e, hi=hi, lo=lo, tmp=tmp: e.tensor_tensor(lo, tmp, hi.bitcast(F32), ALU.subtract), t)
                    work_free[k % 2] = t
                done.append(t)
            return done

        def norm_to_h(rs, rs_done, after, gain, shift, work, work_free, wide_free, extra=None):
            scaled = {}
            for n in range(4):
                for tt in range(TT):
                    cols = slice(n * 512, (n + 1) * 512)
                    scaled[tt, n] = DVE.do(lambda e, tt=tt, cols=cols: e.tensor_scalar(wide[:, tt, cols], x[:, tt, cols], rs[:, tt:tt + 1], None, ALU.mult),
                                           rs_done[tt], after[tt], wide_free)
            ACTE.wait(extra)
            return transpose_split(lambda tt, k: wide[:, tt, k * P:(k + 1) * P], KD, gain, shift,
                                   lambda k: h_hi[:, k, :], lambda k: h_lo[:, k, :], work, work_free,
                                   lambda tt, k: scaled[tt, k // 4])

        x_landed = [load(f"x_landed{tt}", x[:, tt, :], X[tt * P:(tt + 1) * P, :]) for tt in range(TT)]
        params_landed = load("params_landed", lasting[:, :], PARAMS)
        phase1 = place("phase1", "phase", 0, [P, PHASE1["_width"]])
        params1_landed = load("params1_landed", phase1[:, :], PARAMS1)
        load_chunks()

        def param1(name):
            a, b = PHASE1[name]
            return phase1[:, a:b]

        work1 = place("work1", "free", 0, [P, 2, T])
        work1_free = [None, None]
        silu_c = stats(KD)
        silu_c_done = ACTE.do(lambda e: e.activation(silu_c, param("c"), ACT.Silu), params_landed)
        g1 = param("mix_norm_g")
        rs, rs_done = rms_factors(lambda tt: x[:, tt, :], D, lambda tt: wide[:, tt, :], lambda tt: x_landed[tt])
        h_ready = norm_to_h(rs, rs_done, x_landed, lambda k: g1[:, k:k + 1], None, work1, work1_free, rs_done, params_landed)
        h_of = lambda k: h_ready[k]

        FR = "free"
        bias = place("bias", "wide", 0, [P, HEADS, T])
        cmp_bias = place("cmp_bias", FR, 16640, [P, TT * HEADS * NCMP])
        table = place("table", FR, 10240, [HEADS, ROW])
        rows_dram = nc.dram_tensor("bias_rows", (HEADS, P * ROW), F32, kind="Internal").ap()
        one_hot, rel = param1("one_hot"), param1("rel_bias")
        K1 = BUCKETS + 1
        t = PE.do(lambda e: e.matmul(banks[0][0:HEADS, 0:ROW], rel[0:K1, :], param1("one_hot_down")[0:K1, :], start=True, stop=True), params1_landed)
        t = bank_read[0] = DVE.do(lambda e: e.tensor_copy(table[:, :], banks[0][0:HEADS, 0:ROW]), t)
        rows_written = sem("bias_rows_written")
        POOL.wait(t)
        POOL.steps.append(lambda e: e.dma_start(rows_dram.rearrange("h (p w) -> h p w", p=P),
                                              table[:, :].unsqueeze(1).to_broadcast([HEADS, P, ROW])).then_inc(rows_written, 16))
        along = rows_dram[:, P - 1:P - 1 + P * (ROW - 1)].rearrange("h (p w) -> p h w", w=ROW - 1)[:, :, 0:T]
        bias_landed = ("bias_landed", sem("bias_landed"), 16)
        POOL.wait(("bias_rows", rows_written, 16), h_ready[-1])
        POOL.steps.append(lambda e: e.dma_start(bias[:, :, :], along).then_inc(bias_landed[1], 16))
        bias_done = [bias_landed]
        b = 0
        for tt in range(TT):
            for n in range(NCMP):
                a = DIST0 + tt * P - (n * CMP_STRIDE + CMP_LEN - 1)
                lo = tt * HEADS * NCMP + n
                t = PE.do(lambda e, a=a, lo=lo: e.matmul(banks[0][:, lo:lo + HEADS * NCMP - NCMP + 1:NCMP],
                                                         one_hot[0:K1, a:a + P], rel[0:K1, :], start=True, stop=True),
                          bank_read[0], signal=n == NCMP - 1)
        cmp_bias_done = bank_read[0] = DVE.do(lambda e: e.tensor_copy(cmp_bias[:, :], banks[0][:, 0:TT * HEADS * NCMP]), t)

        tokens = place("tokens", FR, 2048, [P, 2, 2, 2, T])
        pos = param1("cmp_pos").rearrange("p (s l) -> p s l", s=2)
        tokens_done = []
        for s in range(2):
            for j in range(2):
                out, b, t = tile(("cmp", s, j), h_hi, h_lo, h_of)
                for half in range(2):
                    add = pos[:, s, half * CMP_STRIDE:(half + 1) * CMP_STRIDE].unsqueeze(1).to_broadcast([P, T // CMP_STRIDE, CMP_STRIDE])
                    u = DVE.do(lambda e, s=s, j=j, half=half, out=out, add=add: e.tensor_tensor(
                        tokens[:, s, half, j, :].rearrange("p (n l) -> p n l", l=CMP_STRIDE),
                        out.rearrange("p (n l) -> p n l", l=CMP_STRIDE), add, ALU.add), t, params1_landed)
                bank_read[b] = u
                tokens_done.append(u)
        hidden = place("hidden", FR, 16640 + 1920, [P, 2, 2 * NCMP])
        kcmp = place("kcmp", FR, 16640 + 1920 + 256, [P, 2 * NCMP])
        vcmp = place("vcmp", FR, 16640 + 1920 + 384, [NCMP, KV_HEADS, DH])
        w2 = param1("cmp_w2").rearrange("p (s e) -> p s e", s=2)
        chunks_w1 = plan.groups["cmp_w1"]
        per = CHUNK // DH
        for s in range(2):
            b = odd_bank()
            for l in range(CMP_LEN):
                i = chunks_w1[(s * CMP_LEN + l) // per]
                for base_p in (0, DH):
                    rows = slice(base_p, base_p + DH)
                    w1_ap = raw[rows, i % RAW_SLOTS, (l % per) * DH:(l % per + 1) * DH]
                    half, within = divmod(l, CMP_STRIDE)
                    first = half * CMP_STRIDE + within
                    moving = tokens[rows, s, half, :, first:first + CMP_STRIDE * (NCMP - 1) + 1:CMP_STRIDE]
                    t = PE.do(lambda e, b=b, rows=rows, w1_ap=w1_ap, moving=moving, l=l: e.matmul(
                        banks[b][rows, 0:2 * NCMP].rearrange("p (j n) -> p j n", j=2), w1_ap, moving, start=l == 0, stop=l == CMP_LEN - 1),
                        arrived(i), tokens_done[2 * s + 1], bank_read[b],
                        signal=base_p == DH and l % per == per - 1)
                if l % per == per - 1:
                    released[i] = t
            prepare(chunks_w1[2 * s + 1])
            load_chunks()
            t = ACTE.do(lambda e, s=s, b=b: e.activation(hidden[:, s, :], banks[b][:, 0:2 * NCMP], ACT.Silu), t)
            bank_read[b] = t
            b2 = odd_bank()
            if s == 0:
                for base_p in (0, DH):
                    rows = slice(base_p, base_p + DH)
                    u = PE.do(lambda e, b=b2, rows=rows: e.matmul(banks[b][rows, 0:2 * NCMP], w2[rows, 0, :], hidden[rows, 0, :], start=True, stop=True),
                              t, bank_read[b2])
                kcmp_done = bank_read[b2] = DVE.do(lambda e, b=b2: e.tensor_copy(kcmp[:, :], banks[b][:, 0:2 * NCMP]), u)
            else:
                u = None
                for hk in (0, 2, 1, 3):
                    base_p = DH * (hk % 2)
                    rows = slice(base_p, base_p + DH)
                    j = hk // 2
                    u = PE.do(lambda e, b=b2, rows=rows, hk=hk, j=j: e.matmul(banks[b][0:NCMP, hk * DH:(hk + 1) * DH], hidden[rows, 1, j * NCMP:(j + 1) * NCMP],
                                                                             w2[rows, 1, :], start=True, stop=True), t, u, bank_read[b2])
                vcmp_done = bank_read[b2] = DVE.do(lambda e, b=b2: e.tensor_copy(vcmp[:, :, :].rearrange("p h d -> p (h d)"), banks[b][0:NCMP, 0:KV_HEADS * DH]), u)
        w1_used = t

        keys = place("keys", "mid", mid_tail + 8192, [P, 2, 2, T])
        queries = place("queries", "mid", mid_tail, [P, 8, T])
        values = place("values", FR, 10240, [P, TT, 2, KV_HEADS * DH])
        gates = place("gates", FR, 14336, [P, TT, HEADS, N_BRANCH])
        for br in range(2):
            for j in range(2):
                out, b, t = tile(("key", br + 1, j), h_hi, h_lo, h_of)
                keys_done = bank_read[b] = ACTE.do(lambda e, br=br, j=j, out=out: e.activation(keys[:, br, j, :], out, ACT.Copy), t)
        for j in range(8):
            out, b, t = tile(("query", j), h_hi, h_lo, h_of)
            queries_done = bank_read[b] = ACTE.do(lambda e, j=j, out=out: e.activation(queries[:, j, :], out, ACT.Copy, scale=DH ** -0.5), t)
        outs, pair, t = group("value", 512, h_hi, h_lo, h_of)
        for tt in range(TT):
            values_done = bank_read[pair[tt]] = ACTE.do(
                lambda e, tt=tt, out=outs[tt]: e.activation(values[:, tt, :, :].rearrange("p b c -> p (b c)"), out, ACT.Copy), t, ("bias_rows", rows_written, 16))
        outs, pair, t = group("gates", N_BRANCH * HEADS, h_hi, h_lo, h_of)
        for tt in range(TT):
            gates_done = bank_read[pair[tt]] = ACTE.do(
                lambda e, tt=tt, out=outs[tt]: e.activation(gates[:, tt, :, :].rearrange("p h b -> p (h b)"), out, ACT.Sigmoid), t)

        NU = TT * HEADS
        cmp_p = place("cmp_p", FR, 14336 + 384, [P, NU, NCMP])
        b = ODD_BANKS[0]
        t = None
        by_rows = sorted((query_place(h)[1], h, tt) for h in range(HEADS) for tt in range(TT))
        for at_h, (base_p, h, tt) in enumerate(by_rows):
                j = query_place(h)[0]
                rows = slice(base_p, base_p + DH)
                u = tt * HEADS + h
                pair_j = h // GQA // 2
                half_done = t if at_h == NU // 2 else None
                t = PE.do(lambda e, b=b, j=j, rows=rows, u=u, tt=tt, pair_j=pair_j: e.matmul(
                    banks[b][:, u * NCMP:(u + 1) * NCMP], queries[rows, j, tt * P:(tt + 1) * P],
                    kcmp[rows, pair_j * NCMP:(pair_j + 1) * NCMP], start=True, stop=True),
                    queries_done, kcmp_done, half_done, bank_read[b], signal=at_h in (NU // 2 - 1, NU - 1))
        flat = cmp_p[:, :, :].rearrange("p u n -> p (u n)")
        t = DVE.do(lambda e: e.tensor_tensor(flat, banks[6][:, 0:NU * NCMP], cmp_bias[:, :], ALU.add), t, cmp_bias_done)
        bank_read[b] = t
        cmp_max, cmp_sum, cmp_coef = stats(NU), stats(NU), stats(NU)
        t = DVE.do(lambda e: e.tensor_reduce(cmp_max, cmp_p[:, :, :], AX.X, ALU.max), t)
        t = DVE.do(lambda e: e.tensor_tensor(cmp_p[:, :, :], cmp_p[:, :, :], cmp_max.unsqueeze(2).to_broadcast([P, NU, NCMP]), ALU.subtract), t)
        t = ACTE.do(lambda e: e.activation(flat, flat, ACT.Exp), t)
        t = DVE.do(lambda e: e.tensor_reduce(cmp_sum, cmp_p[:, :, :], AX.X, ALU.add), t)
        t = DVE.do(lambda e: e.reciprocal(cmp_coef, cmp_sum), t)
        t = DVE.do(lambda e: e.tensor_tensor(cmp_coef.rearrange("p (t h) -> p t h", t=TT), cmp_coef.rearrange("p (t h) -> p t h", t=TT),
                                             gates[:, :, :, 0], ALU.mult), t, gates_done)
        some = param1("any_block").unsqueeze(2).to_broadcast([P, TT, HEADS])
        t = DVE.do(lambda e: e.tensor_tensor(cmp_coef.rearrange("p (t h) -> p t h", t=TT), cmp_coef.rearrange("p (t h) -> p t h", t=TT), some, ALU.mult), t)
        cmp_p_done = DVE.do(lambda e: e.tensor_tensor(cmp_p[:, :, :], cmp_p[:, :, :], cmp_coef.unsqueeze(2).to_broadcast([P, NU, NCMP]), ALU.mult), t)

        scores = place("scores", FR, 0, [P, 2, 2, T])
        weights_T = place("weights_T", FR, 4096, [P, 4, P])
        cmp_T = place("cmp_T", FR, 6144, [NCMP, P])
        conv_u = place("conv_u", FR, 6656, [P, 2, T + CONV_TAPS - 1 + 2])
        PAD = CONV_TAPS - 1
        conv_y = place("conv_y", "acc", 0, [P, CONV_TILES, T])
        sig = place("sig", FR, 8960, [P, T])
        neg_max, row_sum, coef = stats(2 * NU), stats(2 * NU), stats(2 * NU)
        unit_free = {"scores": [w1_used, w1_used], "T": w1_used, "cmp_T": w1_used}
        units = [(h, tt) for h in range(HEADS) for tt in range(TT)]
        mix_ready = [None] * KD

        def unit_scores(u):
            h, tt = units[u]
            n = P * (tt + 1)
            j, base_p = query_place(h)
            rows = slice(base_p, base_p + DH)
            hk = h // GQA
            b = u % 2
            for br in range(2):
                t = PE.do(lambda e, br=br: e.matmul(banks[b][:, br * n:(br + 1) * n], queries[rows, j, tt * P:(tt + 1) * P],
                                                    keys[rows, br, hk // 2, 0:n], start=True, stop=True),
                          queries_done, keys_done, bank_read[b], signal=br == 1)
            s = scores[:, u % 2, :, 0:n]
            add = bias[:, h, T - n:T].unsqueeze(1).to_broadcast([P, 2, n])
            t = DVE.do(lambda e: e.tensor_tensor(s, banks[b][:, 0:2 * n].rearrange("p (b c) -> p b c", b=2), add, ALU.add),
                       t, unit_free["scores"][u % 2], bias_done[-1])
            bank_read[b] = t
            m = neg_max[:, 2 * u:2 * u + 2]
            t = DVE.do(lambda e: e.tensor_reduce(m, s, AX.X, ALU.max, negate=True), t)
            for br in range(2):
                t = ACTE.do(lambda e, br=br: e.activation(s[:, br, :], s[:, br, :], ACT.Exp, bias=m[:, br:br + 1],
                                                          accum_out=row_sum[:, 2 * u + br:2 * u + br + 1]), t)
            return t

        def unit_weights(u, t):
            h, tt = units[u]
            n = P * (tt + 1)
            s = scores[:, u % 2, :, 0:n]
            c = coef[:, 2 * u:2 * u + 2]
            t = DVE.do(lambda e: e.reciprocal(c, row_sum[:, 2 * u:2 * u + 2]), t)
            t = DVE.do(lambda e: e.tensor_tensor(c, c, gates[:, tt, h, 1:3], ALU.mult), t, gates_done)
            v = DVE.do(lambda e: e.tensor_scalar(s[:, 0, :], s[:, 0, :], c[:, 0:1], None, ALU.mult), t)
            w = ACTE.do(lambda e: e.activation(s[:, 1, :], s[:, 1, :], ACT.Copy, scale=c[:, 1:2]), t)
            return [v, w]

        def unit_transpose(u, p_done):
            h, tt = units[u]
            nb = tt + 1
            t = PE.do(lambda e: e.transpose(banks[2][0:NCMP, 2 * P:3 * P], cmp_p[:, tt * HEADS + h, :], identity), cmp_p_done, bank_read[2])
            ct = ACTE.do(lambda e: e.activation(cmp_T[:, :], banks[2][0:NCMP, 2 * P:3 * P], ACT.Copy), t, unit_free["cmp_T"])
            for br in range(2):
                for sb in range(nb):
                    t = PE.do(lambda e, br=br, sb=sb: e.transpose(banks[3][:, (br * nb + sb) * P:(br * nb + sb + 1) * P],
                                                                  scores[:, u % 2, br, sb * P:(sb + 1) * P], identity),
                              p_done, bank_read[3], signal=br == 1 and sb == nb - 1)
            unit_free["scores"][u % 2] = t
            wt = ACTE.do(lambda e: e.activation(weights_T[:, 0:2 * nb, :].rearrange("p a c -> p (a c)"), banks[3][:, 0:2 * nb * P], ACT.Copy), t, unit_free["T"])
            bank_read[3] = wt
            return ct, wt

        def unit_output(u, ct, wt):
            h, tt = units[u]
            hk = h // GQA
            nb = tt + 1
            base_p = DH * (h % 2)
            rows = slice(base_p, base_p + DH)
            out = banks[2][rows, 0:P]
            PE.do(lambda e: e.matmul(out, vcmp[:, hk, :], cmp_T[:, :], start=True, stop=False), ct, vcmp_done, signal=False)
            for br in range(2):
                for sb in range(nb):
                    end = br == 1 and sb == nb - 1
                    t = PE.do(lambda e, br=br, sb=sb, end=end: e.matmul(out, values[:, sb, br, hk * DH:(hk + 1) * DH],
                                                                        weights_T[:, br * nb + sb, :], start=False, stop=end),
                              wt, values_done, signal=end)
            unit_free["T"] = unit_free["cmp_T"] = t
            cols = slice(tt * P, (tt + 1) * P)
            t = split(mix_hi[rows, h // 2, cols], mix_lo[rows, h // 2, cols], out, t)
            bank_read[2] = mix_ready[h // 2] = t

        pad_done = [DVE.do(lambda e, s=s: e.memset(conv_u[:, s, 0:PAD], 0.0), w1_used) for s in range(2)]
        conv_w = param1("conv_w").rearrange("p (j t) -> p j t", j=CONV_TILES)
        conv_b = param1("conv_b")
        y_done = [None] * CONV_TILES
        u_ready = [None] * CONV_TILES
        ln_mean = place("ln_mean", FR, 9984, [P, T])
        ln_sq = place("ln_sq", FR, 6656, [P, 2, T])
        ln_rs = place("ln_rs", FR, 8960, [P, 2, T])

        def conv_project():
            for j in range(CONV_TILES):
                out_a, ba, ta = yield from tile_steps(("conv_a", j), h_hi, h_lo, h_of)
                yield
                out_g, bg, tg = yield from tile_steps(("conv_g", j), h_hi, h_lo, h_of)
                s = ACTE.do(lambda e, out_g=out_g: e.activation(sig[:, :], out_g, ACT.Sigmoid), tg, u_ready[j - 1], w1_used)
                bank_read[bg] = s
                u = conv_u[:, j % 2, PAD:PAD + T]
                u_ready[j] = bank_read[ba] = DVE.do(lambda e, u=u, out_a=out_a: e.tensor_tensor(u, out_a, sig[:, :], ALU.mult),
                                                    s, ta, y_done[j - 2], pad_done[1])
                yield

        def conv_taps():
            for j in range(CONV_TILES):
                while u_ready[j] is None:
                    yield
                u, y = conv_u[:, j % 2, :], conv_y[:, j, :]
                t = DVE.do(lambda e, u=u, y=y, j=j: e.tensor_scalar(y, u[:, PAD:PAD + T], conv_w[:, j, PAD:PAD + 1], conv_b[:, j:j + 1], ALU.mult, ALU.add), u_ready[j])
                for tap in range(PAD):
                    t = DVE.do(lambda e, u=u, y=y, j=j, tap=tap: e.scalar_tensor_tensor(y, u[:, tap:tap + T], conv_w[:, j, tap:tap + 1], y, ALU.mult, ALU.add), t)
                    yield
                y_done[j] = t

        def conv_norm():
            for j in range(CONV_TILES):
                t = PE.do(lambda e, j=j: e.matmul(banks[6][:, 0:T], ones, conv_y[:, j, :], start=j == 0, stop=j == CONV_TILES - 1),
                          y_done[j], bank_read[6])
            t = ACTE.do(lambda e: e.activation(ln_mean[:, :], banks[6][:, 0:T], ACT.Copy, scale=1.0 / CONV_CH), t, h_landed)
            bank_read[6] = t
            yield
            sq_free = [y_done[-1], y_done[-1]]
            centred = [DVE.do(lambda e, j=j: e.tensor_tensor(conv_y[:, j, :], conv_y[:, j, :], ln_mean[:, :], ALU.subtract), t) for j in range(CONV_TILES)]
            yield
            for j in range(CONV_TILES):
                t = ACTE.do(lambda e, j=j: e.activation(ln_sq[:, j % 2, :], conv_y[:, j, :], ACT.Square), centred[j], sq_free[j % 2])
                t = sq_free[j % 2] = PE.do(lambda e, j=j: e.matmul(banks[7][:, 0:T], ones, ln_sq[:, j % 2, :], start=j == 0, stop=j == CONV_TILES - 1),
                                           t, bank_read[7])
                if j % 3 == 2:
                    yield
            v, r, q = ln_mean[:, :], ln_rs[:, 0, :], ln_rs[:, 1, :]
            t = DVE.do(lambda e: e.tensor_scalar(v, banks[7][:, 0:T], 1.0 / CONV_CH, EPS, ALU.mult, ALU.add), t, centred[-1], u_ready[-1])
            bank_read[7] = t
            yield
            t = ACTE.do(lambda e: e.activation(r, v, ACT.Sqrt), t)
            t = DVE.do(lambda e: e.reciprocal(r, r), t)
            yield
            t = DVE.do(lambda e: e.scalar_tensor_tensor(q, v, -0.5, r, ALU.mult, ALU.mult), t)
            t = DVE.do(lambda e: e.tensor_tensor(q, q, r, ALU.mult), t)
            t = DVE.do(lambda e: e.scalar_tensor_tensor(r, q, 1.5, r, ALU.add, ALU.mult), t)
            ln_g, ln_b = param1("conv_ln_g"), param1("conv_ln_b")
            yield
            scaled = [DVE.do(lambda e, j=j: e.tensor_tensor(conv_y[:, j, :], conv_y[:, j, :], r, ALU.mult), t) for j in range(CONV_TILES)]
            yield
            swished = [ACTE.do(lambda e, j=j: e.activation(conv_y[:, j, :], conv_y[:, j, :], ACT.Silu, scale=ln_g[:, j:j + 1], bias=ln_b[:, j:j + 1]), scaled[j])
                       for j in range(CONV_TILES)]
            yield
            for j in range(CONV_TILES):
                mix_ready[KD // 2 + j] = split(mix_hi[:, KD // 2 + j, :], mix_lo[:, KD // 2 + j, :], conv_y[:, j, :], swished[j])
                if j % 3 == 2:
                    yield

        h_landed = w1_used
        projecting, tapping = Beside(conv_project()), Beside(conv_taps(), conv_norm())
        use["tile"] = (4, 5)
        scored, weighted, turned = None, None, None
        for u in range(NU + 2):
            if u < NU:
                exp_done = unit_scores(u)
            projecting.step(1)
            tapping.step(6)
            if turned is not None:
                unit_output(*turned)
                turned = None
            if weighted is not None:
                turned = (weighted[0], *unit_transpose(*weighted))
                weighted = None
            if u % 4 != 3:
                projecting.step(1)
            tapping.step(5)
            if u < NU:
                weighted = (u, unit_weights(u, exp_done))
        if turned is not None:
            unit_output(*turned)
        projecting.finish()
        tapping.finish()
        conv_done = mix_ready[KD - 1]
        attention_done = mix_ready[KD // 2 - 1]
        state["ada_slot"] = [conv_done, conv_done]
        use["tile"] = (4, 5, 2, 3)

        def residual_groups(name, act_hi, act_lo, after, add_to, squares=None):
            done = [None, None]
            for n in range(4):
                outs, pair, t = group((*name, n), 512, act_hi, act_lo, after)
                for tt in range(TT):
                    dst = add_to[:, tt, n * 512:(n + 1) * 512]
                    done[tt] = bank_read[pair[tt]] = DVE.do(
                        lambda e, dst=dst, out=outs[tt]: e.tensor_tensor(dst, out, dst, ALU.add), t)
                    if squares is not None:
                        squares.add(tt, n, dst, done[tt])
            return done

        def fresh_groups(name, act_hi, act_lo, after, dst_of, dst_free, squares=None):
            done = [None, None]
            for n in range(4):
                outs, pair, t = group((*name, n), 512, act_hi, act_lo, after)
                for tt in range(TT):
                    dst = dst_of[:, tt, n * 512:(n + 1) * 512]
                    done[tt] = bank_read[pair[tt]] = ACTE.do(
                        lambda e, dst=dst, out=outs[tt]: e.activation(dst, out, ACT.Copy), t, dst_free)
                    if squares is not None:
                        squares.add(tt, n, dst, done[tt])
            return done

        junk = place("junk", FR, 10240, [P, 512])
        squares = RowSquares(junk[:, :], [attention_done, conv_done])
        x_done = residual_groups(("out1",), mix_hi, mix_lo, lambda k: mix_ready[k], x, squares)

        work2 = place("work2", FR, 0, [P, 2, T])
        work2_free = [conv_done, conv_done]
        g2 = param("ffn_norm_g")
        h_ready = norm_to_h(*squares.factors(), x_done, lambda k: g2[:, k:k + 1], None, work2, work2_free, None)
        ff_w = param("ffn_conv_w").rearrange("p (j t) -> p j t", t=3)
        ff_b = param("ffn_conv_b")
        ffn_a = place("ffn_a", FR, 2048, [P, 2, T])
        ffn_g = place("ffn_g", FR, 4096, [P, 2, T])
        ff_free = [conv_done, conv_done]

        def conv3(out, b, t, y, j, free):
            t = ACTE.do(lambda e: e.activation(y, out, ACT.Identity, scale=ff_w[:, j, 2:3], bias=ff_b[:, j:j + 1]), t, free)
            t = DVE.do(lambda e: e.scalar_tensor_tensor(y[:, 1:T], out[:, 0:T - 1], ff_w[:, j, 1:2], y[:, 1:T], ALU.mult, ALU.add), t)
            t = DVE.do(lambda e: e.scalar_tensor_tensor(y[:, 2:T], out[:, 0:T - 2], ff_w[:, j, 0:1], y[:, 2:T], ALU.mult, ALU.add), t)
            bank_read[b] = t
            return t

        mid_free = PE_last = None
        for half in range(2):
            ff_done = []
            for j in range(FF_HALF * half, FF_HALF * (half + 1)):
                s = j % 2
                out, b, t = tile(("up_a", j), h_hi, h_lo, h_of)
                ya = conv3(out, b, t, ffn_a[:, s, :], j, ff_free[s])
                out, b, t = tile(("up_g", j), h_hi, h_lo, h_of)
                yg = conv3(out, b, t, ffn_g[:, s, :], FF_TILES + j, ff_free[s])
                t = ACTE.do(lambda e, s=s: e.activation(ffn_g[:, s, :], ffn_g[:, s, :], ACT.Silu), yg)
                t = DVE.do(lambda e, s=s: e.tensor_tensor(ffn_a[:, s, :], ffn_a[:, s, :], ffn_g[:, s, :], ALU.mult), t, ya)
                jj = j - FF_HALF * half
                t = ff_free[s] = split(ff_hi[:, jj, :], ff_lo[:, jj, :], ffn_a[:, s, :], t)
                ff_done.append(t)
            squares = RowSquares(junk[:, :], squares.last[1]) if half else squares
            x_done = residual_groups(("down1", half), ff_hi, ff_lo, lambda k, d=ff_done: d[k], x, squares if half else None)
        prepare(plan.groups["c_q"][0][0] - 1)
        run_deferred(True)
        phase2 = place("phase2", "phase", 0, [P, PHASE2["_width"]])
        params2_landed = load("params2_landed", phase2[:, :], PARAMS2, conv_done)
        positions = place("positions", "phase", -(-PHASE2["_width"] * 4 // 64) * 64, [P, TT], I32)
        positions_landed = load("positions_landed", positions[:, :], POSITIONS, conv_done)

        def param2(name):
            a, b = PHASE2[name]
            return phase2[:, a:b]

        def broadcast_row(vec, diag, diag_free, vec_done):
            done = []
            for q in range(4):
                for k in range(4):
                    t = DVE.do(lambda e, q=q, k=k: e.tensor_scalar(diag[:, q % 2, k * P:(k + 1) * P], identity, vec(4 * q + k), None, ALU.mult),
                               diag_free[q % 2], vec_done)
                diag_free[q % 2] = t = PE.do(lambda e, q=q: e.matmul(banks[q][:, :], ones, diag[:, q % 2, :], start=True, stop=True), t, bank_read[q])
                done.append(t)
            return done

        diag = place("diag", FR, 6144, [P, 2, 512])
        diag_free = [conv_done, conv_done]
        rs, rs_done = squares.factors()
        gf = param("final_norm_g")
        row_done = broadcast_row(lambda k: gf[:, k:k + 1], diag, diag_free, params_landed)
        x_done = [None, None]
        squares = RowSquares(junk[:, :], squares.last[1])
        for q in range(4):
            for tt in range(TT):
                x_q = x[:, tt, q * 512:(q + 1) * 512]
                x_done[tt] = bank_read[q] = DVE.do(lambda e, tt=tt, q=q, x_q=x_q, rs=rs: e.scalar_tensor_tensor(
                    x_q, x_q, rs[:, tt:tt + 1], banks[q][:, :], ALU.mult, ALU.mult), rs_done[tt], row_done[q])
                squares.add(tt, q, x_q, x_done[tt])

        def ada(v):
            a = LASTING["b_ada"][0] + v * KD
            return lasting[:, a:a + KD]

        def ada_done(v):
            return [vectors[v, 0], vectors[v, 1]]

        def fold(gain, scale_v):
            return DVE.do(lambda e: e.scalar_tensor_tensor(ada(scale_v), ada(scale_v), 1.0, param(gain), ALU.add, ALU.mult), ada_done(scale_v))

        def fold_gate(gain, gate_v):
            return DVE.do(lambda e: e.tensor_tensor(ada(gate_v), ada(gate_v), param(gain), ALU.mult), ada_done(gate_v))

        folded = fold("g_pre_mix", 1)
        folded_gate = fold_gate("g_post_mix", 2)
        h_ready = norm_to_h(*squares.factors(), x_done, lambda k: ada(1)[:, k:k + 1], lambda k: ada(0)[:, k:k + 1],
                            work2, work2_free, None, [folded, ada_done(0)])
        wide_free = h_ready[-1]
        ffn1_done = ff_free[:]
        acc_free = ada_done(3)

        c_q = place("c_q", "acc", 0, [P, TT, Q_RANK])
        c_kv = place("c_kv", "acc", TT * Q_RANK * 4, [P, TT, KV_RANK + ROPE + GATE_RANK])
        outs, pair, t = group("c_q", Q_RANK, h_hi, h_lo, h_of)
        c_q_done, c_kv_done = [None] * TT, [None] * TT
        for tt in range(TT):
            c_q_done[tt] = bank_read[pair[tt]] = ACTE.do(lambda e, tt=tt, out=outs[tt]: e.activation(c_q[:, tt, :], out, ACT.Copy), t, acc_free)
        outs, pair, t = group("c_kv", KV_RANK + ROPE + GATE_RANK, h_hi, h_lo, h_of)
        for tt in range(TT):
            c_kv_done[tt] = bank_read[pair[tt]] = ACTE.do(lambda e, tt=tt, out=outs[tt]: e.activation(c_kv[:, tt, :], out, ACT.Copy), t, acc_free)
        small_junk = place("small_junk", FR, 4096, [P, Q_RANK])
        rs_q, rs_q_done = rms_factors(lambda tt: c_q[:, tt, :], Q_RANK, lambda tt: small_junk[:, :], lambda tt: [c_q_done[tt], ffn1_done])
        rs_kv, rs_kv_done = rms_factors(lambda tt: c_kv[:, tt, 0:KV_RANK], KV_RANK, lambda tt: small_junk[:, 0:KV_RANK], lambda tt: [c_kv_done[tt], rs_q_done])
        c_q_ok = [DVE.do(lambda e, tt=tt: e.tensor_scalar(c_q[:, tt, :], c_q[:, tt, :], rs_q[:, tt:tt + 1], None, ALU.mult), rs_q_done[tt]) for tt in range(TT)]
        c_kv_ok = [DVE.do(lambda e, tt=tt: e.tensor_scalar(c_kv[:, tt, 0:KV_RANK], c_kv[:, tt, 0:KV_RANK], rs_kv[:, tt:tt + 1], None, ALU.mult), rs_kv_done[tt]) for tt in range(TT)]

        rope_w = place("rope_w", FR, 6144, [P, 8, TT, ROPE2])
        pos_f = stats(TT)
        angle, turns_, cosine, sine = (rope_w[:, i, :, :] for i in range(4))
        r_t = DVE.do(lambda e: e.tensor_copy(pos_f, positions[:, :]), positions_landed)
        for tt in range(TT):
            r_u = DVE.do(lambda e, tt=tt: e.tensor_scalar(angle[:, tt, :], param2("inv_freq"), pos_f[:, tt:tt + 1], None, ALU.mult), r_t, params2_landed, diag_free, ffn1_done)
        MAGIC = 12582912.0
        r_t = DVE.do(lambda e: e.tensor_scalar(turns_, angle, float(np.float32(1 / (2 * np.pi))), MAGIC, ALU.mult, ALU.add), r_u)
        r_t = DVE.do(lambda e: e.tensor_scalar(turns_, turns_, -MAGIC, None, ALU.add), r_t)
        rest = 2 * np.pi
        for bits in (7, 8, 8, 24):
            m, ex = np.frexp(rest)
            part = float(np.ldexp(np.round(m * 2 ** bits), int(ex) - bits))
            rest -= part
            r_t = DVE.do(lambda e, part=part: e.scalar_tensor_tensor(angle, turns_, -part, angle, ALU.mult, ALU.add), r_t)
        PI = float(np.float32(np.pi))
        PI_IN = float(np.nextafter(np.float32(np.pi), np.float32(0)))
        r_t = DVE.do(lambda e: e.tensor_scalar(angle, angle, PI_IN, -PI_IN, ALU.min, ALU.max), r_t)
        r_c = DVE.do(lambda e: e.tensor_scalar(cosine, angle, -1.0, None, ALU.mult), r_t)
        r_c = DVE.do(lambda e: e.tensor_tensor(cosine, cosine, angle, ALU.min), r_c)
        r_c = DVE.do(lambda e: e.tensor_scalar(cosine, cosine, PI / 2, None, ALU.add), r_c)
        ACTE.do(lambda e: e.activation(cosine, cosine, ACT.Sin), r_c)
        rope_done = ACTE.do(lambda e: e.activation(sine, angle, ACT.Sin), r_t)

        gla_q = place("gla_q", "mid", mid_tail, [P, GLA_HEADS, T])
        gla_k = place("gla_k", "mid", mid_tail + 4096, [P, GLA_HEADS, T])
        gla_kd = place("gla_kd", "mid", mid_tail + 8192, [P, GLA_HEADS, T])
        down_done = x_done[1]
        for h in range(GLA_HEADS):
            out, b, t = tile(("gla_q", h), h_hi, h_lo, h_of)
            gla_q_done = bank_read[b] = ACTE.do(lambda e, h=h, out=out: e.activation(gla_q[:, h, :], out, ACT.Copy, scale=float(np.float32(GLA_K ** -0.5))), t, down_done)
        for h in range(GLA_HEADS):
            out, b, t = tile(("gla_k", h), h_hi, h_lo, h_of)
            gla_k_done = bank_read[b] = ACTE.do(lambda e, h=h, out=out: e.activation(gla_k[:, h, :], out, ACT.Copy), t, down_done)

        KQ, KKV = Q_RANK // P, KV_RANK // P
        cq_hi = place("cq_hi", FR, 8192, [P, KQ, T], F32R)
        cq_lo = place("cq_lo", FR, 12288, [P, KQ, T], F32R)
        ckv_hi = place("ckv_hi", FR, 16384, [P, KKV, T], F32R)
        ckv_lo = place("ckv_lo", FR, 18432, [P, KKV, T], F32R)
        g_q, g_kv = param("g_q"), param("g_kv")
        c_free = [diag_free, squares.last]
        cq_ready = transpose_split(lambda tt, k: c_q[:, tt, k * P:(k + 1) * P], KQ, lambda k: g_q[:, k:k + 1], None,
                                   lambda k: cq_hi[:, k, :], lambda k: cq_lo[:, k, :], work2, work2_free, lambda tt, k: c_q_ok[tt], c_free)
        ckv_ready = transpose_split(lambda tt, k: c_kv[:, tt, k * P:(k + 1) * P], KKV, lambda k: g_kv[:, k:k + 1], None,
                                    lambda k: ckv_hi[:, k, :], lambda k: ckv_lo[:, k, :], work2, work2_free, lambda tt, k: c_kv_ok[tt], c_free)
        a_lr = place("a_lr", FR, 2048, [GATE_RANK, T])
        b = odd_bank()
        for tt in range(TT):
            t = PE.do(lambda e, tt=tt, b=b: e.transpose(banks[b][0:GATE_RANK, tt * P:(tt + 1) * P], c_kv[:, tt, KV_RANK + ROPE:], identity),
                      c_kv_ok, bank_read[b])
        a_lr_done = bank_read[b] = DVE.do(lambda e, b=b: e.tensor_copy(a_lr[:, :], banks[b][0:GATE_RANK, 0:T]), t, ffn1_done)

        rope_last = [None]

        def rope(src1, src2, dst1, dst2, heads, tt, after, temps):
            cos_b = cosine[:, tt, :].unsqueeze(1).to_broadcast([P, heads, ROPE2])
            sin_b = sine[:, tt, :].unsqueeze(1).to_broadcast([P, heads, ROPE2])
            ta, tb = temps
            a = DVE.do(lambda e: e.tensor_tensor(ta, src1, cos_b, ALU.mult), after, rope_done, rope_last[0])
            b_ = DVE.do(lambda e: e.tensor_tensor(tb, src2, sin_b, ALU.mult), after)
            o1 = DVE.do(lambda e: e.tensor_tensor(dst1, ta, tb, ALU.subtract), a, b_)
            a = DVE.do(lambda e: e.tensor_tensor(ta, src2, cos_b, ALU.mult), o1)
            b_ = DVE.do(lambda e: e.tensor_tensor(tb, src1, sin_b, ALU.mult), o1)
            rope_last[0] = DVE.do(lambda e: e.tensor_tensor(dst2, ta, tb, ALU.add), a, b_)
            return rope_last[0]

        k_rot = place("k_rot", FR, 3072, [P, TT, 2, ROPE])
        tmp_k = rope_w[:, 4, :, :]
        b = odd_bank()
        for tt in range(TT):
            k1 = c_kv[:, tt, KV_RANK:KV_RANK + ROPE2].unsqueeze(1)
            k2 = c_kv[:, tt, KV_RANK + ROPE2:KV_RANK + ROPE].unsqueeze(1)
            t = rope(k1, k2, k_rot[:, tt, 0:1, 0:ROPE2], k_rot[:, tt, 0:1, ROPE2:ROPE], 1, tt, [c_kv_done[tt], ffn1_done],
                     (tmp_k[:, 0:1, :], tmp_k[:, 1:2, :]))
            t = DVE.do(lambda e, tt=tt: e.tensor_copy(k_rot[:, tt, 1, :], k_rot[:, tt, 0, :]), t)
            t = PE.do(lambda e, tt=tt, b=b: e.transpose(banks[b][:, tt * P:(tt + 1) * P], k_rot[:, tt, :, :].rearrange("p a c -> p (a c)"), identity), t, bank_read[b])
        k_rope_x = place("k_rope_x", FR, 5120, [P, T])
        k_rope_done = bank_read[b] = DVE.do(lambda e, b=b: e.tensor_copy(k_rope_x[:, :], banks[b][:, 0:T]), t, rs_kv_done)

        gv = place("decay_work", "mid", 0, [P, 2, 3, T])
        b_last, decay = stats(GLA_HEADS * N_CHUNKS), stats(GLA_HEADS * N_CHUNKS)
        keep = param2("chunk_causal").bitcast(I32)
        restart = param2("chunk_restart")
        wgu, b_gate = param2("w_gate_up"), param("b_gate")
        C = GLA_CHUNK
        decayed = [None] * GLA_HEADS
        decay_work_free = [down_done, down_done]

        def decays():
            for h in range(GLA_HEADS):
                g_a, g_b, g_sum = (gv[:, h % 2, i, :] for i in range(3))
                bl, dc = b_last[:, h * N_CHUNKS:(h + 1) * N_CHUNKS], decay[:, h * N_CHUNKS:(h + 1) * N_CHUNKS]
                free = decay_work_free[h % 2]
                b = odd_bank()
                t = PE.do(lambda e, h=h, b=b: e.matmul(banks[b][:, 0:T], wgu[0:GATE_RANK, h * P:(h + 1) * P], a_lr[:, :], start=True, stop=True),
                          a_lr_done, params2_landed, bank_read[b])
                bg = b_gate[:, h:h + 1]
                t1 = DVE.do(lambda e, b=b, bg=bg, o=g_sum: e.tensor_scalar(o, banks[b][:, 0:T], bg, 0.0, ALU.add, ALU.min), t, free)
                t2 = DVE.do(lambda e, b=b, bg=bg, o=g_b: e.tensor_scalar(o, banks[b][:, 0:T], bg, 0.0, ALU.add, ALU.max), t, free)
                bank_read[b] = t2
                t = DVE.do(lambda e, a=g_a, s=g_sum, b=g_b: e.tensor_tensor(a, s, b, ALU.subtract), t1, t2)
                yield
                t = ACTE.do(lambda e, a=g_a: e.activation(a, a, ACT.Exp), t)
                t = DVE.do(lambda e, a=g_a: e.tensor_scalar(a, a, 1.0, None, ALU.add), t)
                yield
                t = ACTE.do(lambda e, a=g_a: e.activation(a, a, ACT.Ln), t)
                t = DVE.do(lambda e, a=g_a, s=g_sum: e.tensor_tensor(a, s, a, ALU.subtract), t)
                sums = DVE.do(lambda e, a=g_a, s=g_sum: e.tensor_tensor_scan(s, restart, a, 0.0, ALU.mult, ALU.add), t)
                t = DVE.do(lambda e, s=g_sum, bl=bl: e.tensor_scalar(bl, s[:, C - 1::C], 1.0 / GLA_TAU, None, ALU.mult), sums)
                yield
                dec = ACTE.do(lambda e, bl=bl, dc=dc: e.activation(dc, bl, ACT.Exp), t)
                for n in range(N_CHUNKS):
                    cs = slice(n * C, (n + 1) * C)
                    u = ACTE.do(lambda e, n=n, cs=cs, a=g_a, s=g_sum, bl=bl: e.activation(a[:, cs], s[:, cs], ACT.Exp, scale=-1.0 / GLA_TAU, bias=bl[:, n:n + 1]), t)
                v = ACTE.do(lambda e, s=g_sum, b=g_b: e.activation(b, s, ACT.Exp, scale=1.0 / GLA_TAU), sums)
                yield
                kd = DVE.do(lambda e, h=h, a=g_a: e.tensor_tensor(gla_kd[:, h, :], gla_k[:, h, :], a, ALU.mult), u, gla_k_done)
                qd = DVE.do(lambda e, h=h, b=g_b: e.tensor_tensor(gla_q[:, h, :], gla_q[:, h, :], b, ALU.mult), v, gla_q_done)
                u = ACTE.do(lambda e, s=g_sum, a=g_a: e.activation(a, s, ACT.Exp, scale=-1.0 / GLA_TAU), kd)
                yield
                ki = DVE.do(lambda e, h=h, a=g_a: e.tensor_tensor(gla_k[:, h, :], gla_k[:, h, :], a, ALU.mult), u)
                decayed[h] = [kd, qd, ki, dec]
                decay_work_free[h % 2] = [ki, qd]
                yield

        decaying = Beside(decays())

        gla_v = place("gla_v", "wide", 0, [P, TT, GLA_HEADS * GLA_V])
        gla_o = place("gla_o", "wide", TT * GLA_HEADS * GLA_V * 4, [P, TT, GLA_HEADS * GLA_V])
        ready = {}
        for name, dst, func in (("gla_v", gla_v, ACT.Copy), ("gla_r", gla_o, ACT.Silu)):
            for n in range(2):
                steps = group_steps((name, n), 512, h_hi, h_lo, h_of)
                while True:
                    try:
                        next(steps)
                    except StopIteration as end:
                        outs, pair, t = end.value
                        break
                    if name == "gla_v" or n == 0:
                        decaying.step(1)
                h_used = t
                if name == "gla_r" and n == 0:
                    decaying.finish()
                for tt in range(TT):
                    ready[name] = bank_read[pair[tt]] = ACTE.do(lambda e, tt=tt, n=n, out=outs[tt], dst=dst, func=func: e.activation(
                        dst[:, tt, n * 512:(n + 1) * 512], out, func), t, wide_free)
        gla_v_done, gla_r_done = ready["gla_v"], ready["gla_r"]

        gla_ss, gla_rs = stats(GLA_HEADS * TT), stats(GLA_HEADS * TT)
        gw = []
        for i, off in enumerate((8192, 24576)):
            gw.append((place(f"g_kdn{i}", "mid", off, [P, TT, P]), place(f"g_at{i}", "mid", off + 1024, [P, TT, P]),
                       place(f"g_state{i}", "mid", off + 2048, [P, N_CHUNKS - 1, GLA_V]), place(f"g_junk{i}", "mid", off + 5120, [P, GLA_V])))
        at_zero = [DVE.do(lambda e, i=i: e.memset(gw[i][1][:, :, :], 0.0), down_done) for i in range(2)]
        gla_out = [None] * GLA_HEADS
        gla_read = [None] * GLA_HEADS

        def gla():
            for h in range(GLA_HEADS):
                kdn, at_, state_, junk_ = gw[h % 2]
                before = [gla_out[h - 2], gla_read[h - 2], down_done] if h >= 2 else [down_done]
                kd, qd, ki, dec = decayed[h]
                v_h = slice(h * GLA_V, (h + 1) * GLA_V)
                for tt in range(TT):
                    t = PE.do(lambda e, h=h, tt=tt: e.transpose(banks[6][:, tt * P:(tt + 1) * P], gla_kd[:, h, tt * P:(tt + 1) * P], identity), kd, bank_read[6])
                kdn_done = bank_read[6] = ACTE.do(lambda e, kdn=kdn: e.activation(kdn[:, :, :].rearrange("p t c -> p (t c)"), banks[6][:, 0:T], ACT.Copy), t, before)
                for tt in range(TT):
                    t = PE.do(lambda e, h=h, tt=tt: e.matmul(banks[7][:, tt * P:(tt + 1) * P], gla_k[:, h, tt * P:(tt + 1) * P],
                                                             gla_q[:, h, tt * P:(tt + 1) * P], start=True, stop=True), ki, qd, bank_read[7])
                for tt in range(TT):
                    a_done = DVE.do(lambda e, tt=tt, at_=at_: e.copy_predicated(at_[:, tt, :], keep, banks[7][:, tt * P:(tt + 1) * P]), t, before, at_zero)
                bank_read[7] = a_done
                yield
                s_prev = None
                for n in range(N_CHUNKS - 1):
                    b = 6 + n % 2
                    rows = slice(C * (n % 2), C * (n % 2) + C)
                    t = PE.do(lambda e, n=n, b=b, rows=rows, v_h=v_h, kdn=kdn: e.matmul(banks[b][:, 0:GLA_V], kdn[rows, n // 2, :], gla_v[rows, n // 2, v_h], start=True, stop=True),
                              kdn_done, gla_v_done, bank_read[b])
                    if n == 0:
                        s_prev = DVE.do(lambda e, b=b, s=state_: e.tensor_copy(s[:, 0, :], banks[b][:, 0:GLA_V]), t, before)
                    else:
                        dn = decay[:, h * N_CHUNKS + n:h * N_CHUNKS + n + 1]
                        s_prev = DVE.do(lambda e, b=b, n=n, s=state_, dn=dn: e.scalar_tensor_tensor(s[:, n, :], s[:, n - 1, :], dn, banks[b][:, 0:GLA_V], ALU.mult, ALU.add),
                                        t, s_prev, dec)
                    bank_read[b] = s_prev
                yield
                for tt in range(TT):
                    b = 2 + tt
                    out = banks[b][:, 0:GLA_V]
                    t = PE.do(lambda e, tt=tt, out=out, v_h=v_h, at_=at_: e.matmul(out, at_[:, tt, :], gla_v[:, tt, v_h], start=True, stop=False, skip_group_check=True),
                              a_done, gla_v_done, bank_read[b])
                    for n in (2 * tt, 2 * tt + 1):
                        if n == 0:
                            continue
                        rows = slice(C * (n % 2), C * (n % 2) + C)
                        t = PE.do(lambda e, n=n, h=h, b=b, rows=rows, s=state_: e.matmul(banks[b][rows, 0:GLA_V], gla_q[:, h, n * C:(n + 1) * C], s[:, n - 1, :],
                                                                                        start=False, stop=n % 2 == 1, skip_group_check=True), s_prev)
                    i = h * TT + tt
                    u = ACTE.do(lambda e, out=out, i=i, j=junk_: e.activation(j[:, :], out, ACT.Square, accum_out=gla_ss[:, i:i + 1]), t, before, gla_out[h] and gla_out[h][1])
                    w = rms_power(gla_rs[:, i:i + 1], gla_ss[:, i:i + 1], GLA_V, u)
                    bank_read[b] = DVE.do(lambda e, out=out, i=i, tt=tt, v_h=v_h: e.scalar_tensor_tensor(
                        gla_o[:, tt, v_h], out, gla_rs[:, i:i + 1], gla_o[:, tt, v_h], ALU.mult, ALU.mult), w, gla_r_done)
                    gla_out[h] = [t, u, bank_read[b]]
                gla_read[h] = [bank_read[2], bank_read[3], s_prev]
                yield

        g_gla = param("g_gla")
        gla_ready = [None] * (KD // 2)

        def gla_transpose():
            for h in range(GLA_HEADS):
                for q in range(2):
                    k = 2 * h + q
                    gla_ready[k] = transpose_split(lambda tt, _, k=k: gla_o[:, tt, k * P:(k + 1) * P], 1, lambda _, q=q: g_gla[:, q:q + 1], None,
                                                   lambda _, k=k: mix_hi[:, KD // 2 + k, :], lambda _, k=k: mix_lo[:, KD // 2 + k, :], None, None,
                                                   lambda tt, _, h=h: gla_read[h], [gla_out[GLA_HEADS - 1], gla_read[GLA_HEADS - 1], gla_out[GLA_HEADS - 2], gla_read[GLA_HEADS - 2]])[0]
                    yield

        linear = Beside(gla(), gla_transpose())

        q_nope = place("q_nope", "h", 0, [P, MLA_HEADS, T])
        k_nope = place("k_nope", "h", 8192, [P, MLA_HEADS, T])
        mla_v = place("mla_v", "h", 16384, [P, TT, MLA_HEADS * NOPE])
        q_rope_T = place("q_rope_T", "h", 24576, [P, 4, T])
        q_rot = place("q_rot", "acc", 0, [P, TT, MLA_HEADS * ROPE])
        rope_tmp = place("rope_tmp", "h", 29696, [P, 2, MLA_HEADS, ROPE2])
        use["tile"], use["group"] = (4, 5), ((0, 1),)
        outs, pair, t = group("q_rope", MLA_HEADS * ROPE, cq_hi, cq_lo, lambda k: cq_ready[k])
        linear.step(1)
        for tt in range(TT):
            src = outs[tt].rearrange("p (h c) -> p h c", h=MLA_HEADS)
            dst = q_rot[:, tt, :].rearrange("p (h c) -> p h c", h=MLA_HEADS)
            u = rope(src[:, :, 0:ROPE2], src[:, :, ROPE2:ROPE], dst[:, :, 0:ROPE2], dst[:, :, ROPE2:ROPE], MLA_HEADS, tt,
                     [t, h_used, cq_ready], (rope_tmp[:, 0, :, :], rope_tmp[:, 1, :, :]))
            bank_read[pair[tt]] = u
        q_rot_done = u
        for h in range(MLA_HEADS):
            out, b, t = tile(("q_nope", h), cq_hi, cq_lo, lambda k: cq_ready[k])
            q_nope_done = bank_read[b] = ACTE.do(lambda e, h=h, out=out: e.activation(q_nope[:, h, :], out, ACT.Copy, scale=MLA_SCALE), t, h_used)
            if h % 2:
                linear.step(1)
        for h in range(MLA_HEADS):
            out, b, t = tile(("k_nope", h), ckv_hi, ckv_lo, lambda k: ckv_ready[k])
            k_nope_done = bank_read[b] = ACTE.do(lambda e, h=h, out=out: e.activation(k_nope[:, h, :], out, ACT.Copy), t, h_used)
            if h % 4 == 3:
                linear.step(1)
        for j in range(4):
            b = use["tile"][j % 2]
            for tt in range(TT):
                t = PE.do(lambda e, j=j, tt=tt, b=b: e.transpose(banks[b][:, tt * P:(tt + 1) * P], q_rot[:, tt, j * P:(j + 1) * P], identity), q_rot_done, bank_read[b])
            q_rope_done = bank_read[b] = ACTE.do(lambda e, j=j, b=b: e.activation(q_rope_T[:, j, :], banks[b][:, 0:T], ACT.Copy, scale=MLA_SCALE), t, h_used)
        state["ada_slot"] = [[q_rope_done, cq_ready, ckv_ready, k_rope_done, a_lr_done]] * 2
        for n in range(2):
            outs, pair, t = group(("mla_v", n), 512, ckv_hi, ckv_lo, lambda k: ckv_ready[k])
            for tt in range(TT):
                mla_v_done = bank_read[pair[tt]] = ACTE.do(lambda e, tt=tt, n=n, out=outs[tt]: e.activation(
                    mla_v[:, tt, n * 512:(n + 1) * 512], out, ACT.Copy), t, h_used)
            linear.step(1)
        latents_used = t

        m_scores = place("m_scores", FR, 8192, [P, 3, T])
        m_T = place("m_T", FR, 8192 + 3072, [P, 2, TT, P])
        NM = MLA_HEADS * TT
        m_max, m_sum = stats(NM), stats(NM)
        m_units = [(h, tt) for h in range(MLA_HEADS) for tt in range(TT)]
        m_free = {"s": [latents_used] * 3, "T": [latents_used] * 2}
        mla_ready = [None] * MLA_HEADS

        def latent_scores(u):
            h, tt = m_units[u]
            n = P * (tt + 1)
            b = u % 2
            rows = slice(ROPE * (h % 2), ROPE * (h % 2) + ROPE)
            toks = slice(tt * P, (tt + 1) * P)
            PE.do(lambda e: e.matmul(banks[b][:, 0:n], q_nope[:, h, toks], k_nope[:, h, 0:n], start=True, stop=False),
                  q_nope_done, k_nope_done, bank_read[b], signal=False)
            t = PE.do(lambda e: e.matmul(banks[b][:, 0:n], q_rope_T[rows, h // 2, toks], k_rope_x[rows, 0:n], start=False, stop=True),
                      q_rope_done, k_rope_done)
            s = m_scores[:, u % 3, 0:n]
            t = DVE.do(lambda e: e.tensor_tensor(s, banks[b][:, 0:n], causal[:, T - n:T], ALU.add), t, m_free["s"][u % 3])
            bank_read[b] = t
            t = DVE.do(lambda e: e.tensor_reduce(m_max[:, u:u + 1], s, AX.X, ALU.max, negate=True), t)
            return ACTE.do(lambda e: e.activation(s, s, ACT.Exp, bias=m_max[:, u:u + 1], accum_out=m_sum[:, u:u + 1]), t)

        def latent_weights(u, t):
            h, tt = m_units[u]
            s = m_scores[:, u % 3, 0:P * (tt + 1)]
            t = DVE.do(lambda e: e.reciprocal(m_sum[:, u:u + 1], m_sum[:, u:u + 1]), t)
            return DVE.do(lambda e: e.tensor_scalar(s, s, m_sum[:, u:u + 1], None, ALU.mult), t)

        def latent_transpose(u, p_done):
            h, tt = m_units[u]
            for sb in range(tt + 1):
                t = PE.do(lambda e, sb=sb: e.transpose(banks[4][:, sb * P:(sb + 1) * P], m_scores[:, u % 3, sb * P:(sb + 1) * P], identity),
                          p_done, bank_read[4])
            m_free["s"][u % 3] = t
            wt = bank_read[4] = ACTE.do(lambda e: e.activation(m_T[:, u % 2, 0:tt + 1, :].rearrange("p a c -> p (a c)"), banks[4][:, 0:(tt + 1) * P], ACT.Copy), t, m_free["T"][u % 2])
            return wt

        def latent_output(u, wt):
            h, tt = m_units[u]
            for sb in range(tt + 1):
                t = PE.do(lambda e, sb=sb: e.matmul(banks[5][:, 0:P], mla_v[:, sb, h * NOPE:(h + 1) * NOPE], m_T[:, u % 2, sb, :], start=sb == 0, stop=sb == tt),
                          wt, mla_v_done, bank_read[5])
            m_free["T"][u % 2] = t
            toks = slice(tt * P, (tt + 1) * P)
            mla_ready[h] = bank_read[5] = split(mix_hi[:, h, toks], mix_lo[:, h, toks], banks[5][:, 0:P], t, decay_work_free)

        exped, weighted, turned = None, None, None
        for u in range(NM + 3):
            if weighted is not None:
                turned_next = (weighted[0], latent_transpose(*weighted))
            else:
                turned_next = None
            now = (u, latent_scores(u)) if u < NM else None
            if turned is not None:
                latent_output(*turned)
            linear.step(1)
            turned = turned_next
            weighted = (exped[0], latent_weights(*exped)) if exped is not None else None
            exped = now
        linear.finish()
        assert turned is None and weighted is None
        use["tile"], use["group"] = (4, 5, 2, 3), ((0, 1), (2, 3))
        mix_ready = mla_ready + gla_ready
        attn_free = mla_ready[-1]

        def gated_residual(gate_v, squares, folded_token, diag_free):
            rs, rs_done = squares.factors()
            row_done = broadcast_row(lambda k: ada(gate_v)[:, k:k + 1], diag, diag_free, folded_token)
            done = [None, None]
            after = RowSquares(junk[:, :], squares.last[1])
            for q in range(4):
                for tt in range(TT):
                    w_q, x_q = wide[:, tt, q * 512:(q + 1) * 512], x[:, tt, q * 512:(q + 1) * 512]
                    u = bank_read[q] = DVE.do(lambda e, tt=tt, q=q, w_q=w_q: e.scalar_tensor_tensor(w_q, w_q, rs[:, tt:tt + 1], banks[q][:, :], ALU.mult, ALU.mult), rs_done[tt], row_done[q])
                    done[tt] = DVE.do(lambda e, w_q=w_q, x_q=x_q: e.tensor_tensor(x_q, x_q, w_q, ALU.add), u)
                    if gate_v == 2:
                        after.add(tt, q, x_q, done[tt])
            return done, after

        squares = RowSquares(junk[:, :], attn_free)
        o_done = fresh_groups(("out2",), mix_hi, mix_lo, lambda k: mix_ready[k], wide, gla_ready[-1], squares)
        prepare(plan.groups["gate", 0][0][0] - 1)
        run_deferred(True)
        x_done, squares = gated_residual(2, squares, folded_gate, [attn_free, attn_free])
        folded_ffn = fold("g_pre_ffn", 4)
        h_ready = norm_to_h(*squares.factors(), x_done, lambda k: ada(4)[:, k:k + 1], lambda k: ada(3)[:, k:k + 1], work2, work2_free,
                            x_done, [folded_ffn, ada_done(3), attn_free])

        sw_g = place("sw_g", FR, 2048, [P, 2, T])
        sw_free = [h_ready[-1], h_ready[-1]]
        for half in range(2):
            ff_done = []
            for j in range(FF_HALF * half, FF_HALF * (half + 1)):
                s = j % 2
                out_g, bg, t = tile(("gate", j), h_hi, h_lo, h_of)
                t = bank_read[bg] = ACTE.do(lambda e, s=s, out=out_g: e.activation(sw_g[:, s, :], out, ACT.Silu), t, sw_free[s])
                out_u, bu, tu = tile(("up", j), h_hi, h_lo, h_of)
                t = bank_read[bu] = DVE.do(lambda e, s=s, out=out_u: e.tensor_tensor(sw_g[:, s, :], out, sw_g[:, s, :], ALU.mult), t, tu)
                jj = j - FF_HALF * half
                t = sw_free[s] = split(ff_hi[:, jj, :], ff_lo[:, jj, :], sw_g[:, s, :], t)
                ff_done.append(t)
            after = lambda k, d=ff_done: d[k]
            if half == 0:
                o_done = fresh_groups(("down2", 0), ff_hi, ff_lo, after, wide, h_ready[-1])
                DVE.wait(*o_done)
            else:
                squares = RowSquares(junk[:, :], h_ready[-1])
                o_done = residual_groups(("down2", 1), ff_hi, ff_lo, after, wide, squares)
        run_deferred(True)
        folded_gate_ffn = fold_gate("g_post_ffn", 5)
        x_done, _ = gated_residual(5, squares, folded_gate_ffn, [h_ready[-1], h_ready[-1]])
        stored = sem("stored")
        for tt in range(TT):
            SP.wait(x_done[tt])
            SP.steps.append(lambda e, tt=tt: e.dma_start(OUT[tt * P:(tt + 1) * P, :], x[:, tt, :]).then_inc(stored, 16))
        SP.wait(("stored", stored, 16 * TT))

        assert state["prepared"] == state["loaded"] == len(widths), state
        assert not any(pieces_left[i] for i in range(len(widths)) if plan.kinds[i] == "split")

        block = ctx.enter_context(nc.Block())

        @block.sync
        def _(e):
            SP.play(e)

        @block.gpsimd
        def _(e):
            POOL.play(e)

        @block.scalar
        def _(e):
            ACTE.play(e)

        @block.vector
        def _(e):
            DVE.play(e)

        @block.tensor
        def _(e):
            PE.play(e)



def bucket_of(distance):
    n = np.maximum(distance, 0)
    exact = BUCKETS // 2
    nf = np.maximum(n, 1).astype(np.float32)
    large = exact + (np.log(nf / np.float32(exact)) / np.float32(np.log(MAX_DISTANCE / exact)) * (BUCKETS - exact)).astype(np.int32)
    return np.where(n < exact, n, np.minimum(large, BUCKETS - 1))


def by_partition(v):
    return np.ascontiguousarray(v.reshape(-1, P).T)


def pack(table, values):
    out = np.zeros((P, table["_width"]), np.float32)
    for name, v in values.items():
        a, b = table[name]
        out[:v.shape[0], a:b] = v
    return out


def layout(i):
    mats = {
        "w_in_v": np.concatenate([i["w_in"][0][:, 1024 + 512 * br + 256:1024 + 512 * br + 512] for br in (1, 2)], 1),
        "w_ada": i["w_ada_2"][0], "w_out": i["w_out"][0], "w_up": i["w_up"][0], "w_down": i["w_down"][0],
        "w_in_2": i["w_in_2"][0], "w_uk": i["w_uk_2"][0], "w_uv": i["w_uv_2"][0], "w_out_2": i["w_out_2"][0],
        "w_ffn_gate": i["w_ffn_gate_2"][0], "w_ffn_up": i["w_ffn_up_2"][0], "w_ffn_down": i["w_ffn_down_2"][0],
    }
    w_in = i["w_in"][0]
    mats["w_in"] = np.concatenate([w_in[:, q_columns()], w_in[:, HEADS * DH:]], 1)
    latent = Q_RANK + KV_RANK + ROPE
    a_g = latent + 2 * GLA_HEADS * GLA_K + GLA_HEADS * GLA_V
    w2 = mats["w_in_2"]
    mats["w_in_2_kv"] = np.concatenate([w2[:, Q_RANK:latent], w2[:, a_g:a_g + GATE_RANK]], 1)
    uq = i["w_uq_2"][0].reshape(Q_RANK, MLA_HEADS, NOPE + ROPE)
    mats["w_uq_nope"] = uq[:, :, :NOPE].reshape(Q_RANK, -1)
    mats["w_uq_rope"] = uq[:, :, NOPE:].reshape(Q_RANK, -1)
    w1 = i["cmp_w1"][0].reshape(2, CMP_LEN, DH, DH).transpose(2, 0, 1, 3).reshape(DH, -1)
    mats["cmp_w1"] = np.concatenate([w1, w1], 0)
    plan = make_plan()
    weights = np.empty(P * sum(chunk_widths(plan)), np.float32)
    at = 0
    for chunk in plan.chunks:
        w = sum(c[3] for c in chunk)
        view = weights[at:at + P * w].reshape(P, w)
        c0 = 0
        for mat, kt, col, n in chunk:
            view[:, c0:c0 + n] = mats[mat][kt * P:(kt + 1) * P, col:col + n]
            c0 += n
        at += P * w
    p, c = np.arange(P)[:, None], np.arange(2 * P)[None, :]
    conv_w = lambda w: w.T.reshape(-1, P, w.shape[0]).transpose(1, 0, 2).reshape(P, -1)
    lasting = pack(LASTING, {
        "identity": np.eye(P), "ones": np.ones((P, P)),
        "causal": np.where(P + p - c >= 0, 0.0, MASKED),
        "mix_norm_g": by_partition(i["mix_norm_g"][0]), "ffn_norm_g": by_partition(i["ffn_norm_g"][0]),
        "final_norm_g": by_partition(i["final_norm_g"]), "g_pre_mix": by_partition(i["g_pre_mix_2"][0]),
        "g_post_mix": by_partition(i["g_post_mix_2"][0]), "g_pre_ffn": by_partition(i["g_pre_ffn_2"][0]),
        "g_post_ffn": by_partition(i["g_post_ffn_2"][0]), "b_ada": by_partition(i["b_ada_2"][0]),
        "c": by_partition(i["c_2"][0]), "ffn_conv_w": conv_w(i["ffn_conv_w"][0]),
        "ffn_conv_b": by_partition(i["ffn_conv_b"][0]), "g_q": by_partition(i["g_q_2"][0]),
        "g_kv": by_partition(i["g_kv_2"][0]), "b_gate": by_partition(i["b_gate_2"][0]),
        "g_gla": by_partition(i["g_gla_2"][0]),
    })
    distance = np.arange(N_DIST) - DIST0
    one_hot = np.zeros((BUCKETS + 1, N_DIST), np.float32)
    one_hot[bucket_of(distance), np.arange(N_DIST)] = distance >= 0
    one_hot[BUCKETS] = distance < 0
    rel = np.concatenate([i["rel_bias"], np.full((1, HEADS), MASKED, np.float32)], 0)
    twice = lambda a: np.concatenate([a, a], 0)
    phase1 = pack(PHASE1, {
        "one_hot": one_hot, "one_hot_down": one_hot[:, [DIST0 + 2 * P - 1 - j for j in range(ROW)]], "rel_bias": rel,
        "cmp_w2": twice(i["cmp_w2"][0].transpose(1, 0, 2).reshape(DH, -1)),
        "cmp_pos": twice(i["cmp_pos"][0].transpose(2, 0, 1).reshape(DH, -1)),
        "conv_w": conv_w(i["conv_w"][0]), "conv_b": by_partition(i["conv_b"][0]),
        "conv_ln_g": by_partition(i["conv_ln_g"][0]), "conv_ln_b": by_partition(i["conv_ln_b"][0]),
        "any_block": (np.arange(T) >= CMP_LEN - 1).astype(np.float32).reshape(TT, P).T,
    })
    q, k = np.arange(P)[None, :], np.arange(P)[:, None]
    same = (q // GLA_CHUNK == k // GLA_CHUNK) & (k <= q)
    inv_freq = (1.0 / (np.float32(10000.0) ** (np.arange(0, ROPE, 2, dtype=np.float32) / np.float32(ROPE)))).astype(np.float32)
    phase2 = pack(PHASE2, {
        "w_gate_up": i["w_gate_up_2"][0], "inv_freq": np.broadcast_to(inv_freq, (P, ROPE2)),
        "chunk_restart": np.broadcast_to((np.arange(T) % GLA_CHUNK != 0).astype(np.float32), (P, T)),
        "chunk_causal": same.astype(np.float32),
    })
    return {
        "weights": weights, "x": np.ascontiguousarray(i["x"][0]), "params": lasting, "params1": phase1,
        "params2": phase2, "positions": np.ascontiguousarray(i["positions_2"][0].reshape(TT, P).T),
    }


def kernel(**inputs):
    import concourse.bacc as bacc
    from concourse.bass_utils import run_bass_kernel_spmd

    arrays = layout({name: np.asarray(v) for name, v in inputs.items()})
    nc = bacc.Bacc("TRN2", target_bir_lowering=False, num_devices=1)
    args = [nc.dram_tensor(name, a.shape, mybir.dt.from_np(a.dtype), kind="ExternalInput").ap()
            for name, a in arrays.items()]
    out = nc.dram_tensor("out", (T, D), F32, kind="ExternalOutput").ap()
    two_blocks(nc, *args, out)
    r = run_bass_kernel_spmd(nc, [arrays], core_ids=[0])
    return r.results[0]["out"].reshape(1, T, D)
```

```python
import concourse.bass as bass
from concourse import mybir
from contextlib import ExitStack
import numpy as np

F32 = mybir.dt.float32
F32R = mybir.dt.float32r
I32 = mybir.dt.int32
ALU = mybir.AluOpType
ACT = mybir.ActivationFunctionType
AX = mybir.AxisListType

P = 128
T = 256
TT = T // P
D = 2048
KD = D // P
HALF = 1024

HEADS, KV_HEADS, GQA, DH = 16, 4, 4, 64
CMP_LEN, CMP_STRIDE = 32, 16
NCMP = T // CMP_STRIDE - CMP_LEN // CMP_STRIDE + 1
N_BRANCH = 3
BUCKETS, MAX_DISTANCE = 32, 128
CONV_TAPS, CONV_CH = 31, 1024
CONV_TILES = CONV_CH // P
DFF = 5632
FF_TILES = DFF // P
FF_HALF = FF_TILES // 2
EPS = 1e-6
MASKED = -1e30

MLA_HEADS, Q_RANK, KV_RANK, NOPE, ROPE = 8, 512, 256, 128, 64
ROPE2 = ROPE // 2
MLA_SCALE = float(np.float32((NOPE + ROPE) ** -0.5))
GLA_HEADS, GLA_K, GLA_V, GLA_CHUNK, GATE_RANK = 4, 128, 256, 64, 16
N_CHUNKS = T // GLA_CHUNK
GLA_TAU = 16.0

CHUNK = 1024
RAW_SLOTS = 7
PART_SLOTS = 4
AHEAD = PART_SLOTS - 1
ADA_BESIDE_LATENT = 24



def q_columns():
    cols = []
    for pair in range(KV_HEADS // 2):
        for g in range(GQA):
            for hk in (2 * pair, 2 * pair + 1):
                h = hk * GQA + g
                cols += range(h * DH, (h + 1) * DH)
    return cols


def query_place(h):
    hk, g = divmod(h, GQA)
    return (hk // 2) * GQA + g, DH * (hk % 2)


MIX_ORDER = [*range(KD // 2, KD), *range(KD // 2)]


class Plan:

    def __init__(self):
        self.chunks = []
        self.kinds = []
        self.groups = {}
        self.ada = [(v, half, kt) for v in range(6) for half in range(2) for kt in range(KD)]
        self.rate = 0.0
        self.due = 0.0
        self.keep = 0
        self.on_pool = set()
        self.pool_rate = 0.0
        self.pool_due = 0.0
        self.open = False

    def new_chunk(self, kind):
        self.chunks.append([])
        self.kinds.append(kind)
        self.open = kind == "split"

    def put_ada(self):
        v, half, kt = self.ada.pop(0)
        self.new_chunk("ada")
        self.chunks[-1].append(("w_ada", kt, v * D + half * HALF, HALF))

    def piece(self, mat, kt, col, n):
        used = sum(x[3] for x in self.chunks[-1]) if self.open else CHUNK
        if used + n > CHUNK:
            self.due += self.rate
            while self.due >= 1 and len(self.ada) > self.keep:
                self.put_ada()
                self.due -= 1
            if len(self.ada) == self.keep:
                self.due = 0.0
            self.new_chunk("split")
            self.pool_due += self.pool_rate
            if self.pool_due >= 1:
                self.pool_due -= 1
                self.on_pool.add(len(self.chunks) - 1)
            used = 0
        self.chunks[-1].append((mat, kt, col, n))
        return len(self.chunks) - 1, used, kt

    def project(self, key, mat, col, n, k0=0, nk=KD, order=None):
        self.groups[key] = [self.piece(mat, kt, col, n) for kt in order or range(k0, k0 + nk)]

    def raw(self, key, mat, pieces):
        self.groups[key] = []
        for c in range(pieces):
            self.new_chunk("raw")
            self.chunks[-1].append((mat, 0, c * CHUNK, CHUNK))
            self.groups[key].append(len(self.chunks) - 1)

    def ada_until(self, left, rate):
        self.keep, self.rate = left, rate

    def finish_ada(self):
        while len(self.ada) > self.keep:
            self.put_ada()


def make_plan():
    p = Plan()
    kv = HEADS * DH
    for s in range(2):
        for j in range(2):
            p.project(("cmp", s, j), "w_in", kv + 256 * s + P * j, P)
    p.raw("cmp_w1", "cmp_w1", 2 * CMP_LEN * DH // CHUNK)
    for br in (1, 2):
        for j in range(2):
            p.project(("key", br, j), "w_in", kv + 512 * br + P * j, P)
    for j in range(8):
        p.project(("query", j), "w_in", P * j, P)
    p.project("value", "w_in_v", 0, 512)
    gates = kv + N_BRANCH * 512
    p.project("gates", "w_in", gates, N_BRANCH * HEADS)
    conv = gates + N_BRANCH * HEADS
    p.pool_rate = 0.6
    for j in range(CONV_TILES):
        p.project(("conv_a", j), "w_in", conv + P * j, P)
        p.project(("conv_g", j), "w_in", conv + CONV_CH + P * j, P)
    p.pool_rate = 0.34
    for first in (True, False):
        for n in range(2):
            p.project(("out1", first, n), "w_out", 512 * n, 512, 0 if first else KD // 2, KD // 2)
    for n in range(2, 4):
        p.project(("out1", n), "w_out", 512 * n, 512)
        p.ada_until(3 * 2 * KD, 0.35)
    for half in range(2):
        for j in range(FF_HALF * half, FF_HALF * (half + 1)):
            p.project(("up_a", j), "w_up", P * j, P)
            p.project(("up_g", j), "w_up", DFF + P * j, P)
        for n in range(4):
            p.project(("down1", half, n), "w_down", 512 * n, 512, FF_HALF * half, FF_HALF)
    p.finish_ada()
    p.pool_rate = 0.0
    p.project("c_q", "w_in_2", 0, Q_RANK)
    p.project("c_kv", "w_in_2_kv", 0, KV_RANK + ROPE + GATE_RANK)
    at = Q_RANK + KV_RANK + ROPE
    for h in range(GLA_HEADS):
        p.project(("gla_q", h), "w_in_2", at + P * h, P)
    at += GLA_HEADS * GLA_K
    for h in range(GLA_HEADS):
        p.project(("gla_k", h), "w_in_2", at + P * h, P)
    at += GLA_HEADS * GLA_K
    for n in range(2):
        p.project(("gla_v", n), "w_in_2", at + 512 * n, 512)
    at += GLA_HEADS * GLA_V + GATE_RANK
    for n in range(2):
        p.project(("gla_r", n), "w_in_2", at + 512 * n, 512)
    p.project("q_rope", "w_uq_rope", 0, MLA_HEADS * ROPE, 0, Q_RANK // P)
    for h in range(MLA_HEADS):
        p.project(("q_nope", h), "w_uq_nope", P * h, P, 0, Q_RANK // P)
    for h in range(MLA_HEADS):
        p.project(("k_nope", h), "w_uk", P * h, P, 0, KV_RANK // P)
    for n in range(2):
        p.project(("mla_v", n), "w_uv", 512 * n, 512, 0, KV_RANK // P)
    for _ in range(ADA_BESIDE_LATENT):
        p.put_ada()
    p.ada_until(2 * KD, 1.3)
    for n in range(4):
        p.project(("out2", n), "w_out_2", 512 * n, 512, order=MIX_ORDER)
    p.finish_ada()
    p.ada_until(0, 0.2)
    for half in range(2):
        for j in range(FF_HALF * half, FF_HALF * (half + 1)):
            p.project(("gate", j), "w_ffn_gate", P * j, P)
            p.project(("up", j), "w_ffn_up", P * j, P)
        for n in range(4):
            p.project(("down2", half, n), "w_ffn_down", 512 * n, 512, FF_HALF * half, FF_HALF)
    return p


def chunk_widths(plan):
    return [sum(x[3] for x in c) for c in plan.chunks]



def fields(sizes):
    at, out = 0, {}
    for name, n in sizes:
        out[name] = (at, at + n)
        at += n
    out["_width"] = at
    return out


LASTING = fields([
    ("identity", P), ("ones", P), ("causal", 2 * P), ("mix_norm_g", KD), ("ffn_norm_g", KD),
    ("final_norm_g", KD), ("g_pre_mix", KD), ("g_post_mix", KD), ("g_pre_ffn", KD),
    ("g_post_ffn", KD), ("b_ada", 6 * KD), ("c", KD), ("ffn_conv_w", 3 * 2 * FF_TILES),
    ("ffn_conv_b", 2 * FF_TILES), ("g_q", Q_RANK // P), ("g_kv", KV_RANK // P),
    ("b_gate", GLA_HEADS), ("g_gla", GLA_V // P),
])
ROW = 3 * P
PHASE1 = fields([
    ("one_hot", ROW), ("rel_bias", HEADS), ("cmp_w2", 2 * DH), ("cmp_pos", 2 * CMP_LEN),
    ("conv_w", CONV_TILES * CONV_TAPS), ("conv_b", CONV_TILES), ("conv_ln_g", CONV_TILES),
    ("conv_ln_b", CONV_TILES), ("any_block", TT),
])
PHASE2 = fields([
    ("w_gate_up", GLA_HEADS * GLA_K), ("chunk_restart", T), ("inv_freq", ROPE2),
    ("chunk_causal", P),
])



class Line:

    def __init__(self, sem, name):
        self.sem, self.name, self.count, self.seen, self.steps = sem, name, 0, {}, []

    def wait(self, *tokens):
        for t in tokens:
            if t is None:
                continue
            if isinstance(t, list):
                self.wait(*t)
                continue
            name, sem, value = t
            if self.seen.get(name, 0) < value:
                self.seen[name] = value
                self.steps.append(lambda e, s=sem, v=value: e.wait_ge(s, v))

    def do(self, step, *after, signal=True):
        self.wait(*after)
        if not signal:
            self.steps.append(step)
            return None
        self.count += 1
        self.steps.append(lambda e: step(e).then_inc(self.sem, 1))
        return self.name, self.sem, self.count

    def play(self, engine):
        for step in self.steps:
            step(engine)


def two_blocks(nc, WEIGHTS, X, PARAMS, PARAMS1, PARAMS2, POSITIONS, OUT):
    plan = make_plan()
    widths = chunk_widths(plan)
    starts = [P * s for s in np.concatenate([[0], np.cumsum(widths)]).tolist()]

    ctx = ExitStack()
    with ctx:
        base = -(-nc.sbuf_base // 64) * 64
        at = {}
        cursor = base
        LAST_BYTES = -(-LASTING["_width"] * 4 // 64) * 64
        PHASE_BYTES = -(-max(PHASE1["_width"] * 4, PHASE2["_width"] * 4 + 64) // 64) * 64
        for name, size in (
            ("raw", RAW_SLOTS * CHUNK * 4), ("hi", PART_SLOTS * CHUNK * 4), ("lo", PART_SLOTS * CHUNK * 4),
            ("h", 2 * KD * T * 4), ("mid", 2 * FF_HALF * T * 4), ("x", TT * D * 4), ("wide", TT * D * 4),
            ("acc", 2 * HALF * 4), ("last", LAST_BYTES), ("phase", PHASE_BYTES), ("stat", 2048),
        ):
            at[name] = cursor
            cursor += size
        at["free"] = cursor
        assert nc.sbuf_usable_end - cursor >= 19968 + 2048, nc.sbuf_usable_end - cursor

        def place(name, region, offset, shape, dt=F32):
            return nc.alloc_sbuf_tensor_at(name, shape, dt, offset=at[region] + offset)

        raw = place("raw", "raw", 0, [P, RAW_SLOTS, CHUNK])
        w_hi = place("w_hi", "hi", 0, [P, PART_SLOTS, CHUNK], F32R)
        w_lo = place("w_lo", "lo", 0, [P, PART_SLOTS, CHUNK], F32R)
        h_hi = place("h_hi", "h", 0, [P, KD, T], F32R)
        h_lo = place("h_lo", "h", KD * T * 4, [P, KD, T], F32R)
        mix_hi = place("mix_hi", "mid", 0, [P, KD, T], F32R)
        mix_lo = place("mix_lo", "mid", KD * T * 4, [P, KD, T], F32R)
        ff_hi = place("ff_hi", "mid", 0, [P, FF_HALF, T], F32R)
        ff_lo = place("ff_lo", "mid", FF_HALF * T * 4, [P, FF_HALF, T], F32R)
        mid_tail = 2 * KD * T * 4
        x = place("x", "x", 0, [P, TT, D])
        wide = place("wide", "wide", 0, [P, TT, D])
        ada_acc = place("ada_acc", "acc", 0, [P, 2, HALF])
        lasting = place("lasting", "last", 0, [P, LASTING["_width"]])
        stat = place("stat", "stat", 0, [P, 512])

        def param(name):
            a, b = LASTING[name]
            return lasting[:, a:b]

        identity, ones, causal = param("identity"), param("ones"), param("causal")

        stat_used = [0]

        def stats(n):
            a = stat_used[0]
            stat_used[0] += n
            assert stat_used[0] <= 512
            return stat[:, a:a + n]

        banks = [ctx.enter_context(nc.psum_tensor(f"bank{b}", [P, 512], F32)) for b in range(8)]
        bank_read = [None] * 8
        ODD_BANKS = (6, 7)

        def sem(name):
            return ctx.enter_context(nc.semaphore(name))

        PE = Line(sem("pe_done"), "pe")
        DVE = Line(sem("dve_done"), "dve")
        ACTE = Line(sem("act_done"), "act")
        POOL = Line(sem("pool_done"), "pool")
        SP = Line(sem("sp_done"), "sp")
        raw_sems = [sem(f"raw_landed{i}") for i in range(RAW_SLOTS)]

        def load(name, dst, src, *after, line=None):
            s = sem(name)
            (line or SP).wait(*after)
            (line or SP).steps.append(lambda e: e.dma_start(dst, src).then_inc(s, 16))
            return name, s, 16

        minus_half = stats(1)
        minus_half_done = POOL.do(lambda e: e.memset(minus_half, -0.5))

        released = [None] * len(widths)
        part_of = {}
        part_used = []
        pieces_left = [len(c) for c in plan.chunks]
        state = {"loaded": 0, "prepared": 0, "split": 0, "ada": None, "ada_slot": [None, None]}
        deferred = []

        def arrived(i):
            return f"raw{i % RAW_SLOTS}", raw_sems[i % RAW_SLOTS], 16 * (i // RAW_SLOTS + 1)

        def load_chunks():
            while state["loaded"] < len(widths):
                i = state["loaded"]
                if i >= RAW_SLOTS:
                    if released[i - RAW_SLOTS] is None:
                        return
                    SP.wait(released[i - RAW_SLOTS])
                src = WEIGHTS[starts[i]:starts[i + 1]].rearrange("(p w) -> p w", p=P)
                dst = raw[:, i % RAW_SLOTS, 0:widths[i]]
                SP.steps.append(lambda e, d=dst, s=src, k=i % RAW_SLOTS: e.dma_start(d, s).then_inc(raw_sems[k], 16))
                state["loaded"] += 1

        def split(dst_hi, dst_lo, src, *after):
            hi = ACTE.do(lambda e: e.activation(dst_hi, src, ACT.Copy), *after)
            return DVE.do(lambda e: e.tensor_tensor(dst_lo, src, dst_hi.bitcast(F32), ALU.subtract), hi)

        rounded = []

        def take_rests():
            while rounded:
                i, slot, hi = rounded.pop(0)
                w, line = widths[i], POOL if i in plan.on_pool else DVE
                token = line.do(lambda e, i=i, slot=slot, w=w: e.tensor_tensor(
                    w_lo[:, slot, 0:w], raw[:, i % RAW_SLOTS, 0:w], w_hi[:, slot, 0:w].bitcast(F32), ALU.subtract), hi)
                part_of[i] = slot, token
                released[i] = token
            load_chunks()

        def prepare(upto):
            take_rests()
            while state["prepared"] <= min(upto, len(widths) - 1):
                i = state["prepared"]
                if plan.kinds[i] == "split":
                    n = state["split"]
                    slot_free = part_used[n - PART_SLOTS] if n >= PART_SLOTS else None
                    slot = n % PART_SLOTS
                    hi = ACTE.do(lambda e, i=i, slot=slot, w=widths[i]: e.activation(w_hi[:, slot, 0:w], raw[:, i % RAW_SLOTS, 0:w], ACT.Copy),
                                 arrived(i), slot_free)
                    rounded.append((i, slot, hi))
                    state["split"] += 1
                elif plan.kinds[i] == "ada":
                    released[i] = ada_step(i, raw[:, i % RAW_SLOTS, 0:widths[i]])
                state["prepared"] += 1
                load_chunks()

        vectors = {}

        def ada_step(i, src):
            _, kt, col, _ = plan.chunks[i][0]
            v, half = col // D, (col % D) // HALF
            slot = (2 * v + half) % 2
            acc, s = ada_acc[:, slot, :], silu_c[:, kt:kt + 1]
            if kt == 0:
                t = DVE.do(lambda e: e.tensor_scalar(acc, src, s, None, ALU.mult), arrived(i),
                           state["ada_slot"][slot], silu_c_done)
            else:
                t = DVE.do(lambda e: e.scalar_tensor_tensor(acc, src, s, acc, ALU.mult, ALU.add),
                           arrived(i), state["ada"])
            state["ada"] = t
            if kt == KD - 1:
                deferred.append([AHEAD + 1, v, half, slot, t])
                state["ada_slot"][slot] = "pending"
            return t

        def ada_reduce(v, half, slot, acc_done):
            b = ODD_BANKS[0]
            n = HALF // P
            for k in range(n):
                t = PE.do(lambda e, k=k: e.matmul(banks[b][:, k:k + 1], ada_acc[:, slot, k * P:(k + 1) * P],
                                                  ones[:, 0:1], start=True, stop=True),
                          acc_done, bank_read[b], signal=k == n - 1)
            state["ada_slot"][slot] = t
            lo, hi = LASTING["b_ada"][0] + v * KD + half * n, LASTING["b_ada"][0] + v * KD + (half + 1) * n
            t = DVE.do(lambda e: e.tensor_tensor(lasting[:, lo:hi], banks[b][:, 0:n], lasting[:, lo:hi], ALU.add), t)
            bank_read[b] = t
            vectors[v, half] = t

        def run_deferred(now=False):
            while deferred and (now or deferred[0][0] <= 0):
                ada_reduce(*deferred.pop(0)[1:])
            for d in deferred:
                d[0] -= 1

        def piece_used(i, token):
            pieces_left[i] -= 1
            if pieces_left[i] == 0:
                part_used.append(token)
                run_deferred()

        def parts(i, off, n):
            slot, _ = part_of[i]
            return w_hi[:, slot, off:off + n], w_lo[:, slot, off:off + n]

        def projection(key, n, out_of, outs, act_hi, act_lo, after, tile, opens=True, closes=True):
            got = plan.groups[key]
            base_k = min(kt for _, _, kt in got)
            last = None
            for at_piece, (i, off, kt) in enumerate(got):
                prepare(i)
                if i not in part_of:
                    take_rests()
                k = kt - base_k
                hi, lo = parts(i, off, n)
                ends = pieces_left[i] == 1
                first_k, last_k = at_piece == 0, at_piece == len(got) - 1
                need = after(k) if callable(after) else after
                for o, out in enumerate(outs):
                    if tile:
                        a_hi, a_lo = act_hi[:, k, :], act_lo[:, k, :]
                        trio = ((hi, a_hi), (hi, a_lo), (lo, a_hi))
                    else:
                        a_hi, a_lo = act_hi[:, k, o * P:(o + 1) * P], act_lo[:, k, o * P:(o + 1) * P]
                        trio = ((a_hi, hi), (a_hi, lo), (a_lo, hi))
                    for q, (s, m) in enumerate(trio):
                        final = o == len(outs) - 1 and q == 2
                        last = PE.do(lambda e, s=s, m=m, out=out, st=opens and first_k and q == 0, en=closes and last_k and q == 2:
                                     e.matmul(out, s, m, start=st, stop=en),
                                     part_of[i][1], need, [bank_read[b] for b in out_of] if first_k else None,
                                     signal=final and (ends or last_k))
                if ends:
                    piece_used(i, last)
                    prepare(i + AHEAD)
                    if not last_k:
                        yield
                else:
                    pieces_left[i] -= 1
            return last

        turn = {"tile": 0, "group": 0, "odd": 0}
        use = {"tile": (4, 5, 2, 3), "group": ((0, 1), (2, 3))}

        def tile_steps(key, act_hi, act_lo, after, n=P):
            b = use["tile"][turn["tile"] % len(use["tile"])]
            turn["tile"] += 1
            out = banks[b][0:n, 0:T]
            return out, b, (yield from projection(key, n, [b], [out], act_hi, act_lo, after, True))

        def group_steps(key, n, act_hi, act_lo, after, pair=None, opens=True, closes=True):
            if pair is None:
                pair = use["group"][turn["group"] % len(use["group"])]
                turn["group"] += 1
            outs = [banks[b][:, 0:n] for b in pair]
            return outs, pair, (yield from projection(key, n, list(pair), outs, act_hi, act_lo, after, False, opens, closes))

        def finish(steps):
            while True:
                try:
                    next(steps)
                except StopIteration as end:
                    return end.value

        def tile(*args, **named):
            return finish(tile_steps(*args, **named))

        def group(*args, **named):
            return finish(group_steps(*args, **named))

        class Beside:

            def __init__(self, *stages):
                self.stages = list(stages)

            def step(self, n=1):
                while n > 0 and self.stages:
                    try:
                        next(self.stages[0])
                        n -= 1
                    except StopIteration:
                        self.stages.pop(0)

            def finish(self):
                while self.stages:
                    self.step()

        def odd_bank():
            b = ODD_BANKS[turn["odd"] % 2]
            turn["odd"] += 1
            return b

        def rms_power(out, squares, n, after):
            t = POOL.do(lambda e: e.tensor_scalar(out, squares, 1.0 / n, EPS, ALU.mult, ALU.add), after)
            return POOL.do(lambda e: e.tensor_tensor(out, out, minus_half, ALU.pow), t, minus_half_done)

        def rms_factors(src, n, junk, after):
            out, tokens, sq = stats(TT), [], stats(TT)
            t_act = None
            for tt in range(TT):
                t = t_act = ACTE.do(lambda e, tt=tt: e.activation(junk(tt), src(tt), ACT.Square, accum_out=sq[:, tt:tt + 1]),
                                    after(tt), t_act)
                tokens.append(rms_power(out[:, tt:tt + 1], sq[:, tt:tt + 1], n, t))
            return out, tokens

        class RowSquares:

            def __init__(self, junk, junk_free):
                self.parts, self.sum, self.out = stats(TT * 4), stats(TT), stats(TT)
                self.junk, self.junk_free, self.last = junk, junk_free, [None] * TT

            def add(self, tt, n, src, after):
                col = self.parts[:, tt * 4 + n:tt * 4 + n + 1]
                self.junk_free = self.last[tt] = ACTE.do(
                    lambda e: e.activation(self.junk, src, ACT.Square, accum_out=col), after, self.junk_free)

            def factors(self):
                tokens = []
                for tt in range(TT):
                    s, out = self.sum[:, tt:tt + 1], self.out[:, tt:tt + 1]
                    t = DVE.do(lambda e, tt=tt, s=s: e.tensor_reduce(s, self.parts[:, tt * 4:tt * 4 + 4], AX.X, ALU.add), self.last[tt])
                    tokens.append(rms_power(out, s, D, t))
                return self.out, tokens

        def transpose_split(src, nk, gain, shift, dst_hi, dst_lo, work, work_free, after, dst_free=None):
            done = []
            for k in range(nk):
                b = odd_bank()
                for tt in range(TT):
                    t = PE.do(lambda e, tt=tt, k=k, b=b: e.transpose(banks[b][:, tt * P:(tt + 1) * P], src(tt, k), identity),
                              after(tt, k), bank_read[b], signal=tt == TT - 1)
                g, hi, lo = gain(k), dst_hi(k), dst_lo(k)
                if shift is None:
                    t = ACTE.do(lambda e, b=b, hi=hi, g=g: e.activation(hi, banks[b][:, 0:T], ACT.Copy, scale=g), t, dst_free)
                    t = DVE.do(lambda e, b=b, hi=hi, lo=lo, g=g: e.scalar_tensor_tensor(lo, banks[b][:, 0:T], g, hi.bitcast(F32), ALU.mult, ALU.subtract), t)
                    bank_read[b] = t
                else:
                    tmp, free = work[:, k % 2, :], work_free[k % 2]
                    t = ACTE.do(lambda e, b=b, tmp=tmp, g=g, s=shift(k): e.activation(tmp, banks[b][:, 0:T], ACT.Identity, scale=g, bias=s), t, free)
                    bank_read[b] = t
                    if k % 2:
                        t = split(hi, lo, tmp, t, dst_free)
                    else:
                        t = DVE.do(lambda e, hi=hi, tmp=tmp: e.tensor_copy(hi, tmp), t, dst_free)
                        t = DVE.do(lambda e, hi=hi, lo=lo, tmp=tmp: e.tensor_tensor(lo, tmp, hi.bitcast(F32), ALU.subtract), t)
                    work_free[k % 2] = t
                done.append(t)
            return done

        def norm_to_h(rs, rs_done, after, gain, shift, work, work_free, wide_free, extra=None):
            scaled = {}
            for n in range(4):
                for tt in range(TT):
                    cols = slice(n * 512, (n + 1) * 512)
                    scaled[tt, n] = DVE.do(lambda e, tt=tt, cols=cols: e.tensor_scalar(wide[:, tt, cols], x[:, tt, cols], rs[:, tt:tt + 1], None, ALU.mult),
                                           rs_done[tt], after[tt], wide_free)
            ACTE.wait(extra)
            return transpose_split(lambda tt, k: wide[:, tt, k * P:(k + 1) * P], KD, gain, shift,
                                   lambda k: h_hi[:, k, :], lambda k: h_lo[:, k, :], work, work_free,
                                   lambda tt, k: scaled[tt, k // 4])

        x_landed = [load(f"x_landed{tt}", x[:, tt, :], X[tt * P:(tt + 1) * P, :]) for tt in range(TT)]
        params_landed = load("params_landed", lasting[:, :], PARAMS)
        phase1 = place("phase1", "phase", 0, [P, PHASE1["_width"]])
        params1_landed = load("params1_landed", phase1[:, :], PARAMS1)
        load_chunks()

        def param1(name):
            a, b = PHASE1[name]
            return phase1[:, a:b]

        work1 = place("work1", "free", 0, [P, 2, T])
        work1_free = [None, None]
        silu_c = stats(KD)
        silu_c_done = ACTE.do(lambda e: e.activation(silu_c, param("c"), ACT.Silu), params_landed)
        g1 = param("mix_norm_g")
        rs, rs_done = rms_factors(lambda tt: x[:, tt, :], D, lambda tt: wide[:, tt, :], lambda tt: x_landed[tt])
        h_ready = norm_to_h(rs, rs_done, x_landed, lambda k: g1[:, k:k + 1], None, work1, work1_free, rs_done, params_landed)
        h_of = lambda k: h_ready[k]

        FR = "free"
        bias = place("bias", "wide", 0, [P, HEADS, T])
        table = place("table", FR, 10240, [HEADS, ROW])
        rows_dram = nc.dram_tensor("bias_rows", (HEADS, P * ROW), F32, kind="Internal").ap()
        rel = param1("rel_bias")
        K1 = BUCKETS + 1
        t = PE.do(lambda e: e.matmul(banks[0][0:HEADS, 0:ROW], rel[0:K1, :], param1("one_hot")[0:K1, :], start=True, stop=True), params1_landed)
        t = bank_read[0] = DVE.do(lambda e: e.tensor_copy(table[:, :], banks[0][0:HEADS, 0:ROW]), t)
        rows_written = sem("bias_rows_written")
        POOL.wait(t)
        POOL.steps.append(lambda e: e.dma_start(rows_dram.rearrange("h (p w) -> h p w", p=P),
                                              table[:, :].unsqueeze(1).to_broadcast([HEADS, P, ROW])).then_inc(rows_written, 16))
        along = rows_dram[:, P - 1:P - 1 + P * (ROW - 1)].rearrange("h (p w) -> p h w", w=ROW - 1)[:, :, 0:T]
        bias_landed = ("bias_landed", sem("bias_landed"), 16)
        POOL.wait(("bias_rows", rows_written, 16), h_ready[-1])
        POOL.steps.append(lambda e: e.dma_start(bias[:, :, :], along).then_inc(bias_landed[1], 16))
        bias_done = [bias_landed]
        tokens = place("tokens", FR, 2048, [P, 2, 2, 2, T])
        pos = param1("cmp_pos").rearrange("p (s l) -> p s l", s=2)
        tokens_done = []
        for s in range(2):
            for j in range(2):
                out, b, t = tile(("cmp", s, j), h_hi, h_lo, h_of)
                for half in range(2):
                    add = pos[:, s, half * CMP_STRIDE:(half + 1) * CMP_STRIDE].unsqueeze(1).to_broadcast([P, T // CMP_STRIDE, CMP_STRIDE])
                    u = DVE.do(lambda e, s=s, j=j, half=half, out=out, add=add: e.tensor_tensor(
                        tokens[:, s, half, j, :].rearrange("p (n l) -> p n l", l=CMP_STRIDE),
                        out.rearrange("p (n l) -> p n l", l=CMP_STRIDE), add, ALU.add), t, params1_landed)
                bank_read[b] = u
                tokens_done.append(u)
        hidden = place("hidden", FR, 16640 + 1920 - 256, [P, 2, 2 * NCMP])
        kcmp = place("kcmp", FR, 16640 + 1920, [P, 2, 2, NCMP])
        kcmp_zero = DVE.do(lambda e: e.memset(kcmp[:, :, :, :], 0.0))
        vcmp = place("vcmp", FR, 16640 + 1920 + 384, [NCMP, KV_HEADS, DH])
        w2 = param1("cmp_w2").rearrange("p (s e) -> p s e", s=2)
        chunks_w1 = plan.groups["cmp_w1"]
        per = CHUNK // DH
        for s in range(2):
            b = odd_bank()
            for l in range(CMP_LEN):
                i = chunks_w1[(s * CMP_LEN + l) // per]
                for base_p in (0, DH):
                    rows = slice(base_p, base_p + DH)
                    w1_ap = raw[rows, i % RAW_SLOTS, (l % per) * DH:(l % per + 1) * DH]
                    half, within = divmod(l, CMP_STRIDE)
                    first = half * CMP_STRIDE + within
                    moving = tokens[rows, s, half, :, first:first + CMP_STRIDE * (NCMP - 1) + 1:CMP_STRIDE]
                    t = PE.do(lambda e, b=b, rows=rows, w1_ap=w1_ap, moving=moving, l=l: e.matmul(
                        banks[b][rows, 0:2 * NCMP].rearrange("p (j n) -> p j n", j=2), w1_ap, moving, start=l == 0, stop=l == CMP_LEN - 1),
                        arrived(i), tokens_done[2 * s + 1], bank_read[b],
                        signal=base_p == DH and l % per == per - 1)
                if l % per == per - 1:
                    released[i] = t
            prepare(chunks_w1[2 * s + 1])
            load_chunks()
            t = ACTE.do(lambda e, s=s, b=b: e.activation(hidden[:, s, :], banks[b][:, 0:2 * NCMP], ACT.Silu), t)
            bank_read[b] = t
            b2 = odd_bank()
            if s == 0:
                for base_p in (0, DH):
                    rows = slice(base_p, base_p + DH)
                    u = PE.do(lambda e, b=b2, rows=rows: e.matmul(banks[b][rows, 0:2 * NCMP], w2[rows, 0, :], hidden[rows, 0, :], start=True, stop=True),
                              t, bank_read[b2])
                for at_head in range(2):
                    rows = slice(DH * at_head, DH * at_head + DH)
                    kcmp_done = bank_read[b2] = DVE.do(lambda e, b=b2, rows=rows, at_head=at_head: e.tensor_copy(
                        kcmp[rows, :, at_head, :], banks[b][rows, 0:2 * NCMP].rearrange("p (j n) -> p j n", j=2)), u, kcmp_zero)
            else:
                u = None
                for hk in (0, 2, 1, 3):
                    base_p = DH * (hk % 2)
                    rows = slice(base_p, base_p + DH)
                    j = hk // 2
                    u = PE.do(lambda e, b=b2, rows=rows, hk=hk, j=j: e.matmul(banks[b][0:NCMP, hk * DH:(hk + 1) * DH], hidden[rows, 1, j * NCMP:(j + 1) * NCMP],
                                                                             w2[rows, 1, :], start=True, stop=True), t, u, bank_read[b2])
                vcmp_done = bank_read[b2] = DVE.do(lambda e, b=b2: e.tensor_copy(vcmp[:, :, :].rearrange("p h d -> p (h d)"), banks[b][0:NCMP, 0:KV_HEADS * DH]), u)
        w1_used = t

        keys = place("keys", "mid", mid_tail + 8192, [P, 2, 2, T])
        queries = place("queries", "mid", mid_tail, [P, 8, T])
        values = place("values", FR, 10240, [P, TT, 2, KV_HEADS * DH])
        gates = place("gates", FR, 14336, [P, TT, HEADS, N_BRANCH])
        for br in range(2):
            for j in range(2):
                out, b, t = tile(("key", br + 1, j), h_hi, h_lo, h_of)
                keys_done = bank_read[b] = ACTE.do(lambda e, br=br, j=j, out=out: e.activation(keys[:, br, j, :], out, ACT.Copy), t)
        for j in range(8):
            out, b, t = tile(("query", j), h_hi, h_lo, h_of)
            queries_done = bank_read[b] = ACTE.do(lambda e, j=j, out=out: e.activation(queries[:, j, :], out, ACT.Copy, scale=DH ** -0.5), t)
        outs, pair, t = group("value", 512, h_hi, h_lo, h_of)
        for tt in range(TT):
            values_done = bank_read[pair[tt]] = ACTE.do(
                lambda e, tt=tt, out=outs[tt]: e.activation(values[:, tt, :, :].rearrange("p b c -> p (b c)"), out, ACT.Copy), t, ("bias_rows", rows_written, 16))
        NG = N_BRANCH * HEADS
        gates_T = place("gates_T", FR, 0, [NG, T])
        out, b, t = tile("gates", h_hi, h_lo, h_of, n=NG)
        gates_T_done = bank_read[b] = ACTE.do(lambda e, out=out: e.activation(gates_T[:, :], out, ACT.Sigmoid), t, w1_used)
        for tt in range(TT):
            b = odd_bank()
            t = PE.do(lambda e, tt=tt, b=b: e.transpose(banks[b][:, 0:NG], gates_T[:, tt * P:(tt + 1) * P], identity[0:NG, 0:NG]), gates_T_done, bank_read[b])
            gates_done = bank_read[b] = ACTE.do(lambda e, tt=tt, b=b: e.activation(gates[:, tt, :, :].rearrange("p h b -> p (h b)"), banks[b][:, 0:NG], ACT.Copy), t)

        NU = TT * HEADS
        cmp_p = place("cmp_p", FR, 14336 + 384, [P, NU, NCMP])
        b = ODD_BANKS[0]
        into = banks[b][:, 0:NU * NCMP].rearrange("p (u n) -> p u n", n=NCMP)
        for tt in range(TT):
            for j in range(HEADS // 2):
                h = (2 * (j // GQA)) * GQA + j % GQA
                t = PE.do(lambda e, tt=tt, j=j, u=tt * HEADS + h: e.matmul(
                    into[:, u:u + GQA + 1:GQA, :], queries[:, j, tt * P:(tt + 1) * P], kcmp[:, j // GQA, :, :], start=True, stop=True),
                    queries_done, kcmp_done, bank_read[b], signal=(tt, j) == (TT - 1, HEADS // 2 - 1))
        flat = cmp_p[:, :, :].rearrange("p u n -> p (u n)")
        END = CMP_LEN - 1
        cmp_scores = banks[6][:, 0:NU * NCMP].rearrange("p (u n) -> p u n", n=NCMP)
        SEEN = (T - 1 - END - P) // CMP_STRIDE + 1
        m = DVE.do(lambda e: e.memset(cmp_p[:, 0:HEADS, SEEN:NCMP], MASKED))
        m = DVE.do(lambda e: e.tensor_tensor(cmp_p[:, 0:HEADS, 0:SEEN], cmp_scores[:, 0:HEADS, 0:SEEN], bias[:, :, P + END::CMP_STRIDE], ALU.add), t, bias_done[-1], m)
        t = DVE.do(lambda e: e.tensor_tensor(cmp_p[:, HEADS:NU, :], cmp_scores[:, HEADS:NU, :], bias[:, :, END::CMP_STRIDE], ALU.add), t, m)
        bank_read[b] = t
        cmp_max, cmp_sum, cmp_coef = stats(NU), stats(NU), stats(NU)
        t = DVE.do(lambda e: e.tensor_reduce(cmp_max, cmp_p[:, :, :], AX.X, ALU.max), t)
        t = DVE.do(lambda e: e.tensor_tensor(cmp_p[:, :, :], cmp_p[:, :, :], cmp_max.unsqueeze(2).to_broadcast([P, NU, NCMP]), ALU.subtract), t)
        t = ACTE.do(lambda e: e.activation(flat, flat, ACT.Exp), t)
        t = DVE.do(lambda e: e.tensor_reduce(cmp_sum, cmp_p[:, :, :], AX.X, ALU.add), t)
        t = DVE.do(lambda e: e.reciprocal(cmp_coef, cmp_sum), t)
        t = DVE.do(lambda e: e.tensor_tensor(cmp_coef.rearrange("p (t h) -> p t h", t=TT), cmp_coef.rearrange("p (t h) -> p t h", t=TT),
                                             gates[:, :, :, 0], ALU.mult), t, gates_done)
        some = param1("any_block").unsqueeze(2).to_broadcast([P, TT, HEADS])
        t = DVE.do(lambda e: e.tensor_tensor(cmp_coef.rearrange("p (t h) -> p t h", t=TT), cmp_coef.rearrange("p (t h) -> p t h", t=TT), some, ALU.mult), t)
        cmp_p_done = DVE.do(lambda e: e.tensor_tensor(cmp_p[:, :, :], cmp_p[:, :, :], cmp_coef.unsqueeze(2).to_broadcast([P, NU, NCMP]), ALU.mult), t)

        scores = [place("scores0", FR, 0, [P, 2, T]), place("scores1", FR, 2048, [P, 2, T]), place("scores2", FR, 19968, [P, 2, T])]
        weights_T = place("weights_T", FR, 4096, [P, 4, P])
        cmp_T = place("cmp_T", FR, 6144, [NCMP, P])
        conv_u = place("conv_u", "mid", (KD + KD // 2) * T * 4, [P, 4, T + CONV_TAPS - 1 + 2])
        PAD = CONV_TAPS - 1
        conv_y = place("conv_y", "acc", 0, [P, CONV_TILES, T])
        sig = place("sig", "mid", (KD + KD // 2) * T * 4 + 4608, [P, 2, T])
        neg_max, row_sum, coef = stats(2 * NU), stats(2 * NU), stats(2 * NU)
        unit_free = {"scores": [[w1_used, cmp_p_done]] * 3, "T": w1_used, "cmp_T": w1_used}
        units = [(h, tt) for h in range(HEADS) for tt in range(TT)]
        mix_ready = [None] * KD

        def unit_scores(u):
            h, tt = units[u]
            n = P * (tt + 1)
            j, base_p = query_place(h)
            rows = slice(base_p, base_p + DH)
            hk = h // GQA
            b = u % 2
            for br in range(2):
                t = PE.do(lambda e, br=br: e.matmul(banks[b][:, br * n:(br + 1) * n], queries[rows, j, tt * P:(tt + 1) * P],
                                                    keys[rows, br, hk // 2, 0:n], start=True, stop=True),
                          queries_done, keys_done, bank_read[b], signal=br == 1)
            s = scores[u % 3][:, :, 0:n]
            add = bias[:, h, T - n:T].unsqueeze(1).to_broadcast([P, 2, n])
            t = DVE.do(lambda e: e.tensor_tensor(s, banks[b][:, 0:2 * n].rearrange("p (b c) -> p b c", b=2), add, ALU.add),
                       t, unit_free["scores"][u % 3], bias_done[-1])
            bank_read[b] = t
            m = neg_max[:, 2 * u:2 * u + 2]
            return DVE.do(lambda e: e.tensor_reduce(m, s, AX.X, ALU.max, negate=True), t)

        def unit_exp(u, t):
            n = P * (units[u][1] + 1)
            s, m = scores[u % 3][:, :, 0:n], neg_max[:, 2 * u:2 * u + 2]
            for br in range(2):
                t = ACTE.do(lambda e, br=br: e.activation(s[:, br, :], s[:, br, :], ACT.Exp, bias=m[:, br:br + 1],
                                                          accum_out=row_sum[:, 2 * u + br:2 * u + br + 1]), t)
            return t

        def unit_weights(u, t):
            h, tt = units[u]
            n = P * (tt + 1)
            s = scores[u % 3][:, :, 0:n]
            c = coef[:, 2 * u:2 * u + 2]
            t = DVE.do(lambda e: e.reciprocal(c, row_sum[:, 2 * u:2 * u + 2]), t)
            t = DVE.do(lambda e: e.tensor_tensor(c, c, gates[:, tt, h, 1:3], ALU.mult), t, gates_done)
            v = DVE.do(lambda e: e.tensor_scalar(s[:, 0, :], s[:, 0, :], c[:, 0:1], None, ALU.mult), t)
            w = ACTE.do(lambda e: e.activation(s[:, 1, :], s[:, 1, :], ACT.Copy, scale=c[:, 1:2]), t)
            return [v, w]

        def unit_transpose(u, p_done):
            h, tt = units[u]
            nb = tt + 1
            t = PE.do(lambda e: e.transpose(banks[6][0:NCMP, 0:P], cmp_p[:, tt * HEADS + h, :], identity), cmp_p_done, bank_read[6])
            ct = bank_read[6] = ACTE.do(lambda e: e.activation(cmp_T[:, :], banks[6][0:NCMP, 0:P], ACT.Copy), t, unit_free["cmp_T"])
            for br in range(2):
                for sb in range(nb):
                    t = PE.do(lambda e, br=br, sb=sb: e.transpose(banks[3][:, (br * nb + sb) * P:(br * nb + sb + 1) * P],
                                                                  scores[u % 3][:, br, sb * P:(sb + 1) * P], identity),
                              p_done, bank_read[3], signal=br == 1 and sb == nb - 1)
            unit_free["scores"][u % 3] = t
            wt = ACTE.do(lambda e: e.activation(weights_T[:, 0:2 * nb, :].rearrange("p a c -> p (a c)"), banks[3][:, 0:2 * nb * P], ACT.Copy), t, unit_free["T"])
            bank_read[3] = wt
            return ct, wt

        def unit_output(u, ct, wt):
            h, tt = units[u]
            hk = h // GQA
            nb = tt + 1
            base_p = DH * (h % 2)
            rows = slice(base_p, base_p + DH)
            b = (2, 7)[u % 2]
            out = banks[b][rows, 0:P]
            PE.do(lambda e: e.matmul(out, vcmp[:, hk, :], cmp_T[:, :], start=True, stop=False), ct, vcmp_done, bank_read[b], signal=False)
            for br in range(2):
                for sb in range(nb):
                    end = br == 1 and sb == nb - 1
                    t = PE.do(lambda e, br=br, sb=sb, end=end: e.matmul(out, values[:, sb, br, hk * DH:(hk + 1) * DH],
                                                                        weights_T[:, br * nb + sb, :], start=False, stop=end),
                              wt, values_done, signal=end)
            unit_free["T"] = unit_free["cmp_T"] = t
            cols = slice(tt * P, (tt + 1) * P)
            hi = ACTE.do(lambda e: e.activation(mix_hi[rows, h // 2, cols], out, ACT.Copy), t)

            def rest():
                bank_read[b] = mix_ready[h // 2] = DVE.do(lambda e: e.tensor_tensor(
                    mix_lo[rows, h // 2, cols], out, mix_hi[rows, h // 2, cols].bitcast(F32), ALU.subtract), hi)
            return rest

        pad_done = [DVE.do(lambda e, s=s: e.memset(conv_u[:, s, 0:PAD], 0.0), w1_used) for s in range(4)]
        conv_w = param1("conv_w").rearrange("p (j t) -> p j t", j=CONV_TILES)
        conv_b = param1("conv_b")
        y_done = [None] * CONV_TILES
        u_ready = [None] * CONV_TILES
        ln_mean = place("ln_mean", FR, 16640, [P, T])
        ln_rs = place("ln_rs", FR, 16640 + 1024, [P, T])
        ln_q = place("ln_q", FR, 8960, [P, T])
        ln_sq = place("ln_sq", "mid", (KD // 2) * T * 4, [P, CONV_TILES, T])

        def conv_project():
            for j in range(CONV_TILES):
                out_a, ba, ta = yield from tile_steps(("conv_a", j), h_hi, h_lo, h_of)
                a_done = bank_read[ba] = ACTE.do(lambda e, j=j, out_a=out_a: e.activation(conv_u[:, j % 4, PAD:PAD + T], out_a, ACT.Copy), ta, y_done[j - 4], pad_done[3])
                yield
                out_g, bg, tg = yield from tile_steps(("conv_g", j), h_hi, h_lo, h_of)
                s = bank_read[bg] = ACTE.do(lambda e, j=j, out_g=out_g: e.activation(sig[:, j % 2, :], out_g, ACT.Sigmoid), tg, u_ready[j - 2])
                yield
                u = conv_u[:, j % 4, PAD:PAD + T]
                u_ready[j] = DVE.do(lambda e, u=u, j=j: e.tensor_tensor(u, u, sig[:, j % 2, :], ALU.mult), s, a_done)

        def conv_taps():
            for j0 in range(0, CONV_TILES, 2):
                while u_ready[j0 + 1] is None:
                    yield
                last = {}
                for tap in (PAD, *range(PAD)):
                    for j in (j0, j0 + 1):
                        u, y, w = conv_u[:, j % 4, tap:tap + T], conv_y[:, j, :], conv_w[:, j, tap:tap + 1]
                        if tap == PAD:
                            last[j] = DVE.do(lambda e, u=u, y=y, w=w, j=j: e.tensor_scalar(y, u, w, conv_b[:, j:j + 1], ALU.mult, ALU.add), u_ready[j])
                        else:
                            last[j] = DVE.do(lambda e, u=u, y=y, w=w: e.scalar_tensor_tensor(y, u, w, y, ALU.mult, ALU.add), last[j])
                        yield
                y_done[j0], y_done[j0 + 1] = last[j0], last[j0 + 1]

        def conv_norm():
            for j in range(CONV_TILES):
                t = PE.do(lambda e, j=j: e.matmul(banks[6][:, 0:T], ones, conv_y[:, j, :], start=j == 0, stop=j == CONV_TILES - 1),
                          y_done[j], bank_read[6], signal=j == CONV_TILES - 1)
            t = ACTE.do(lambda e: e.activation(ln_mean[:, :], banks[6][:, 0:T], ACT.Copy, scale=1.0 / CONV_CH), t, cmp_p_done)
            bank_read[6] = t
            yield
            centred = []
            for j in range(CONV_TILES):
                centred.append(DVE.do(lambda e, j=j: e.tensor_tensor(conv_y[:, j, :], conv_y[:, j, :], ln_mean[:, :], ALU.subtract), t))
                yield
            squared = [ACTE.do(lambda e, j=j: e.activation(ln_sq[:, j, :], conv_y[:, j, :], ACT.Square), centred[j]) for j in range(CONV_TILES)]
            yield
            for j in range(CONV_TILES):
                t = PE.do(lambda e, j=j: e.matmul(banks[6][:, 0:T], ones, ln_sq[:, j, :], start=j == 0, stop=j == CONV_TILES - 1),
                          squared[j], bank_read[6], signal=j == CONV_TILES - 1)
            yield
            v, r, q = ln_mean[:, :], ln_rs[:, :], ln_q[:, :]
            t = DVE.do(lambda e: e.tensor_scalar(v, banks[6][:, 0:T], 1.0 / CONV_CH, EPS, ALU.mult, ALU.add), t, centred[-1], u_ready[-1])
            bank_read[6] = t
            yield
            t = ACTE.do(lambda e: e.activation(r, v, ACT.Sqrt), t)
            t = DVE.do(lambda e: e.reciprocal(r, r), t)
            yield
            t = DVE.do(lambda e: e.scalar_tensor_tensor(q, v, -0.5, r, ALU.mult, ALU.mult), t)
            t = DVE.do(lambda e: e.tensor_tensor(q, q, r, ALU.mult), t)
            t = DVE.do(lambda e: e.scalar_tensor_tensor(r, q, 1.5, r, ALU.add, ALU.mult), t)
            ln_g, ln_b = param1("conv_ln_g"), param1("conv_ln_b")
            yield
            scaled = [DVE.do(lambda e, j=j: e.tensor_tensor(conv_y[:, j, :], conv_y[:, j, :], r, ALU.mult), t) for j in range(CONV_TILES)]
            yield
            swished = [ACTE.do(lambda e, j=j: e.activation(conv_y[:, j, :], conv_y[:, j, :], ACT.Silu, scale=ln_g[:, j:j + 1], bias=ln_b[:, j:j + 1]), scaled[j])
                       for j in range(CONV_TILES)]
            yield
            for j in range(CONV_TILES):
                mix_ready[KD // 2 + j] = split(mix_hi[:, KD // 2 + j, :], mix_lo[:, KD // 2 + j, :], conv_y[:, j, :], swished[j])
                if j % 3 == 2:
                    yield

        projecting, tapping = Beside(conv_project()), Beside(conv_taps(), conv_norm())
        use["tile"] = (4, 5)
        exped, weighted, turned = None, None, None
        for u in range(NU + 3):
            now = (u, unit_scores(u)) if u < NU else None
            projecting.step(1)
            tapping.step(4)
            rest = unit_output(*turned) if turned is not None else None
            turned = (weighted[0], *unit_transpose(*weighted)) if weighted is not None else None
            tapping.step(2)
            if u % 2 == 0:
                projecting.step(1)
            weighted = (exped[0], unit_weights(*exped)) if exped is not None else None
            exped = (u, unit_exp(*now)) if now is not None else None
            tapping.step(2)
            if rest is not None:
                rest()
            tapping.step(4)
        projecting.finish()
        tapping.finish()
        conv_done = mix_ready[KD - 1]
        attention_done = mix_ready[KD // 2 - 1]
        state["ada_slot"] = [conv_done, conv_done]
        use["tile"] = (4, 5, 2, 3)

        def residual_groups(name, act_hi, act_lo, after, add_to, squares=None, made=None, row=None):
            done = [None, None]
            for n in range(4):
                if n == 3 and row:
                    row(0, 1, 2)
                outs, pair, t = made[n] if made and n in made else group((*name, n), 512, act_hi, act_lo, after)
                for tt in range(TT):
                    dst = add_to[:, tt, n * 512:(n + 1) * 512]
                    done[tt] = bank_read[pair[tt]] = DVE.do(
                        lambda e, dst=dst, out=outs[tt]: e.tensor_tensor(dst, out, dst, ALU.add), t)
                    if squares is not None:
                        squares.add(tt, n, dst, done[tt])
            if row:
                row(3)
            return done

        def fresh_groups(name, act_hi, act_lo, after, dst_of, dst_free, squares=None, row=None):
            done = [None, None]
            for n in range(4):
                if n == 3 and row:
                    row(0, 1, 2)
                outs, pair, t = group((*name, n), 512, act_hi, act_lo, after)
                for tt in range(TT):
                    dst = dst_of[:, tt, n * 512:(n + 1) * 512]
                    done[tt] = bank_read[pair[tt]] = ACTE.do(
                        lambda e, dst=dst, out=outs[tt]: e.activation(dst, out, ACT.Copy), t, dst_free)
                    if squares is not None:
                        squares.add(tt, n, dst, done[tt])
            if row:
                row(3)
            return done

        junk = place("junk", FR, 10240, [P, 512])
        squares = RowSquares(junk[:, :], [attention_done, conv_done])
        for n in range(2):
            group(("out1", True, n), 512, mix_hi, mix_lo, lambda k: mix_ready[k], pair=(2 * n, 2 * n + 1), closes=False)
        upper = slice(KD // 2, KD)
        made = {n: group(("out1", False, n), 512, mix_hi[:, upper, :], mix_lo[:, upper, :], lambda k: mix_ready[KD // 2 + k],
                         pair=(2 * n, 2 * n + 1), opens=False) for n in range(2)}
        turn["group"] = 0
        x_done = residual_groups(("out1",), mix_hi, mix_lo, lambda k: mix_ready[k], x, squares, made)

        work2 = place("work2", FR, 0, [P, 2, T])
        work2_free = [conv_done, conv_done]
        g2 = param("ffn_norm_g")
        h_ready = norm_to_h(*squares.factors(), x_done, lambda k: g2[:, k:k + 1], None, work2, work2_free, None)
        ff_w = param("ffn_conv_w").rearrange("p (j t) -> p j t", t=3)
        ff_b = param("ffn_conv_b")
        ffn_a = place("ffn_a", FR, 2048, [P, 2, T])
        ffn_g = place("ffn_g", FR, 4096, [P, 2, T])
        ff_free = [conv_done, conv_done]

        def conv3(out, b, t, y, j, free):
            t = ACTE.do(lambda e: e.activation(y, out, ACT.Identity, scale=ff_w[:, j, 2:3], bias=ff_b[:, j:j + 1]), t, free)
            t = DVE.do(lambda e: e.scalar_tensor_tensor(y[:, 1:T], out[:, 0:T - 1], ff_w[:, j, 1:2], y[:, 1:T], ALU.mult, ALU.add), t)
            t = DVE.do(lambda e: e.scalar_tensor_tensor(y[:, 2:T], out[:, 0:T - 2], ff_w[:, j, 0:1], y[:, 2:T], ALU.mult, ALU.add), t)
            bank_read[b] = t
            return t

        def ffn_tail(j, ff_done):
            s = j % 2
            ya, yg = ff_conv[j]
            t = ACTE.do(lambda e, s=s: e.activation(ffn_g[:, s, :], ffn_g[:, s, :], ACT.Silu), yg)
            t = DVE.do(lambda e, s=s: e.tensor_tensor(ffn_a[:, s, :], ffn_a[:, s, :], ffn_g[:, s, :], ALU.mult), t, ya)
            yield
            jj = j % FF_HALF
            t = ff_free[s] = split(ff_hi[:, jj, :], ff_lo[:, jj, :], ffn_a[:, s, :], t)
            ff_done.append(t)

        ff_conv = {}

        def ffn_conv(j, ff_done, a, g):
            s = j % 2
            ya = conv3(*a, ffn_a[:, s, :], j, ff_free[s])
            yield
            ff_conv[j] = ya, conv3(*g(), ffn_g[:, s, :], FF_TILES + j, ff_free[s])
            yield
            yield from ffn_tail(j, ff_done)

        ROW_BANKS = (4, 5, 7, 0)

        def broadcast_row(vec, diag_free, vec_done, quarters):
            done = []
            for q in quarters:
                b = ROW_BANKS[q]
                for k in range(4):
                    t = DVE.do(lambda e, q=q, k=k: e.tensor_scalar(diag[:, q % 2, k * P:(k + 1) * P], identity, vec(4 * q + k), None, ALU.mult),
                               diag_free[q % 2], vec_done)
                diag_free[q % 2] = t = PE.do(lambda e, q=q, b=b: e.matmul(banks[b][:, :], ones, diag[:, q % 2, :], start=True, stop=True), t, bank_read[b])
                done.append(t)
            return done

        diag = place("diag", FR, 6144, [P, 2, 512])
        row_done = []
        gf = param("final_norm_g")
        diag_free = [conv_done, conv_done]
        final_row = lambda *quarters: row_done.extend(broadcast_row(lambda k: gf[:, k:k + 1], diag_free, params_landed, quarters))
        for half in range(2):
            ff_done = []
            following = Beside()
            for j in range(FF_HALF * half, FF_HALF * (half + 1)):
                made = {}
                for part in ("a", "g"):
                    steps = tile_steps(("up_" + part, j), h_hi, h_lo, h_of)
                    while True:
                        try:
                            next(steps)
                        except StopIteration as end:
                            made[part] = end.value
                            break
                        following.step(1)
                    if part == "a":
                        following.step(1)
                        following.stages.append(ffn_conv(j, ff_done, made["a"], lambda made=made: made["g"]))
            following.finish()
            squares = RowSquares(junk[:, :], squares.last[1]) if half else squares
            x_done = residual_groups(("down1", half), ff_hi, ff_lo, lambda k, d=ff_done: d[k], x, squares if half else None,
                                     row=final_row if half else None)
        prepare(plan.groups["c_q"][0][0] - 1)
        run_deferred(True)
        phase2 = place("phase2", "phase", 0, [P, PHASE2["_width"]])
        params2_landed = load("params2_landed", phase2[:, :], PARAMS2, conv_done)
        positions = place("positions", "phase", -(-PHASE2["_width"] * 4 // 64) * 64, [P, TT], I32)
        positions_landed = load("positions_landed", positions[:, :], POSITIONS, conv_done)

        def param2(name):
            a, b = PHASE2[name]
            return phase2[:, a:b]

        rs, rs_done = squares.factors()
        x_done = [None, None]
        squares = RowSquares(junk[:, :], squares.last[1])
        for q in range(4):
            for tt in range(TT):
                x_q = x[:, tt, q * 512:(q + 1) * 512]
                x_done[tt] = bank_read[ROW_BANKS[q]] = DVE.do(lambda e, tt=tt, q=q, x_q=x_q, rs=rs: e.scalar_tensor_tensor(
                    x_q, x_q, rs[:, tt:tt + 1], banks[ROW_BANKS[q]][:, :], ALU.mult, ALU.mult), rs_done[tt], row_done[q])
                squares.add(tt, q, x_q, x_done[tt])

        def ada(v):
            a = LASTING["b_ada"][0] + v * KD
            return lasting[:, a:a + KD]

        def ada_done(v):
            return [vectors[v, 0], vectors[v, 1]]

        def fold(gain, scale_v):
            return DVE.do(lambda e: e.scalar_tensor_tensor(ada(scale_v), ada(scale_v), 1.0, param(gain), ALU.add, ALU.mult), ada_done(scale_v))

        def fold_gate(gain, gate_v):
            return DVE.do(lambda e: e.tensor_tensor(ada(gate_v), ada(gate_v), param(gain), ALU.mult), ada_done(gate_v))

        folded = fold("g_pre_mix", 1)
        folded_gate = fold_gate("g_post_mix", 2)
        h_ready = norm_to_h(*squares.factors(), x_done, lambda k: ada(1)[:, k:k + 1], lambda k: ada(0)[:, k:k + 1],
                            work2, work2_free, None, [folded, ada_done(0)])
        wide_free = h_ready[-1]
        ffn1_done = ff_free[:]
        acc_free = ada_done(2)

        c_q = place("c_q", "acc", 0, [P, TT, Q_RANK])
        c_kv = place("c_kv", "acc", TT * Q_RANK * 4, [P, TT, KV_RANK + ROPE + GATE_RANK])
        outs, pair, t = group("c_q", Q_RANK, h_hi, h_lo, h_of)
        c_q_done, c_kv_done = [None] * TT, [None] * TT
        for tt in range(TT):
            c_q_done[tt] = bank_read[pair[tt]] = ACTE.do(lambda e, tt=tt, out=outs[tt]: e.activation(c_q[:, tt, :], out, ACT.Copy), t, acc_free)
        outs, pair, t = group("c_kv", KV_RANK + ROPE + GATE_RANK, h_hi, h_lo, h_of)
        for tt in range(TT):
            c_kv_done[tt] = bank_read[pair[tt]] = ACTE.do(lambda e, tt=tt, out=outs[tt]: e.activation(c_kv[:, tt, :], out, ACT.Copy), t, acc_free)
        small_junk = place("small_junk", FR, 4096, [P, Q_RANK])
        rs_q, rs_q_done = rms_factors(lambda tt: c_q[:, tt, :], Q_RANK, lambda tt: small_junk[:, :], lambda tt: [c_q_done[tt], ffn1_done])
        rs_kv, rs_kv_done = rms_factors(lambda tt: c_kv[:, tt, 0:KV_RANK], KV_RANK, lambda tt: small_junk[:, 0:KV_RANK], lambda tt: [c_kv_done[tt], rs_q_done])
        c_q_ok = [DVE.do(lambda e, tt=tt: e.tensor_scalar(c_q[:, tt, :], c_q[:, tt, :], rs_q[:, tt:tt + 1], None, ALU.mult), rs_q_done[tt]) for tt in range(TT)]
        c_kv_ok = [DVE.do(lambda e, tt=tt: e.tensor_scalar(c_kv[:, tt, 0:KV_RANK], c_kv[:, tt, 0:KV_RANK], rs_kv[:, tt:tt + 1], None, ALU.mult), rs_kv_done[tt]) for tt in range(TT)]

        rope_w = place("rope_w", FR, 6144, [P, 8, TT, ROPE2])
        pos_f = stats(TT)
        angle, turns_, cosine, sine = (rope_w[:, i, :, :] for i in range(4))
        r_t = DVE.do(lambda e: e.tensor_copy(pos_f, positions[:, :]), positions_landed)
        for tt in range(TT):
            r_u = DVE.do(lambda e, tt=tt: e.tensor_scalar(angle[:, tt, :], param2("inv_freq"), pos_f[:, tt:tt + 1], None, ALU.mult), r_t, params2_landed, row_done, ffn1_done)
        MAGIC = 12582912.0
        r_t = DVE.do(lambda e: e.tensor_scalar(turns_, angle, float(np.float32(1 / (2 * np.pi))), MAGIC, ALU.mult, ALU.add), r_u)
        r_t = DVE.do(lambda e: e.tensor_scalar(turns_, turns_, -MAGIC, None, ALU.add), r_t)
        rest = 2 * np.pi
        for bits in (7, 8, 8, 24):
            m, ex = np.frexp(rest)
            part = float(np.ldexp(np.round(m * 2 ** bits), int(ex) - bits))
            rest -= part
            r_t = DVE.do(lambda e, part=part: e.scalar_tensor_tensor(angle, turns_, -part, angle, ALU.mult, ALU.add), r_t)
        PI = float(np.float32(np.pi))
        PI_IN = float(np.nextafter(np.float32(np.pi), np.float32(0)))
        r_t = DVE.do(lambda e: e.tensor_scalar(angle, angle, PI_IN, -PI_IN, ALU.min, ALU.max), r_t)
        r_c = DVE.do(lambda e: e.tensor_scalar(cosine, angle, -1.0, None, ALU.mult), r_t)
        r_c = DVE.do(lambda e: e.tensor_tensor(cosine, cosine, angle, ALU.min), r_c)
        r_c = DVE.do(lambda e: e.tensor_scalar(cosine, cosine, PI / 2, None, ALU.add), r_c)
        ACTE.do(lambda e: e.activation(cosine, cosine, ACT.Sin), r_c)
        rope_done = ACTE.do(lambda e: e.activation(sine, angle, ACT.Sin), r_t)

        gla_q = place("gla_q", "mid", mid_tail, [P, GLA_HEADS, T])
        gla_k = place("gla_k", "mid", mid_tail + 4096, [P, GLA_HEADS, T])
        gla_kd = place("gla_kd", "mid", mid_tail + 8192, [P, GLA_HEADS, T])
        down_done = x_done[1]
        for h in range(GLA_HEADS):
            out, b, t = tile(("gla_q", h), h_hi, h_lo, h_of)
            gla_q_done = bank_read[b] = ACTE.do(lambda e, h=h, out=out: e.activation(gla_q[:, h, :], out, ACT.Copy, scale=float(np.float32(GLA_K ** -0.5))), t, down_done)
        for h in range(GLA_HEADS):
            out, b, t = tile(("gla_k", h), h_hi, h_lo, h_of)
            gla_k_done = bank_read[b] = ACTE.do(lambda e, h=h, out=out: e.activation(gla_k[:, h, :], out, ACT.Copy), t, down_done)

        KQ, KKV = Q_RANK // P, KV_RANK // P
        cq_hi = place("cq_hi", FR, 8192, [P, KQ, T], F32R)
        cq_lo = place("cq_lo", FR, 12288, [P, KQ, T], F32R)
        ckv_hi = place("ckv_hi", FR, 16384, [P, KKV, T], F32R)
        ckv_lo = place("ckv_lo", FR, 18432, [P, KKV, T], F32R)
        g_q, g_kv = param("g_q"), param("g_kv")
        c_free = [row_done, squares.last]
        cq_ready = transpose_split(lambda tt, k: c_q[:, tt, k * P:(k + 1) * P], KQ, lambda k: g_q[:, k:k + 1], None,
                                   lambda k: cq_hi[:, k, :], lambda k: cq_lo[:, k, :], work2, work2_free, lambda tt, k: c_q_ok[tt], c_free)
        ckv_ready = transpose_split(lambda tt, k: c_kv[:, tt, k * P:(k + 1) * P], KKV, lambda k: g_kv[:, k:k + 1], None,
                                    lambda k: ckv_hi[:, k, :], lambda k: ckv_lo[:, k, :], work2, work2_free, lambda tt, k: c_kv_ok[tt], c_free)
        a_lr = place("a_lr", FR, 2048, [GATE_RANK, T])
        b = odd_bank()
        for tt in range(TT):
            t = PE.do(lambda e, tt=tt, b=b: e.transpose(banks[b][0:GATE_RANK, tt * P:(tt + 1) * P], c_kv[:, tt, KV_RANK + ROPE:], identity),
                      c_kv_ok, bank_read[b])
        a_lr_done = bank_read[b] = DVE.do(lambda e, b=b: e.tensor_copy(a_lr[:, :], banks[b][0:GATE_RANK, 0:T]), t, ffn1_done)

        rope_last = [None]

        def rope(src1, src2, dst1, dst2, heads, tt, after, temps):
            cos_b = cosine[:, tt, :].unsqueeze(1).to_broadcast([P, heads, ROPE2])
            sin_b = sine[:, tt, :].unsqueeze(1).to_broadcast([P, heads, ROPE2])
            ta, tb = temps
            a = DVE.do(lambda e: e.tensor_tensor(ta, src1, cos_b, ALU.mult), after, rope_done, rope_last[0])
            b_ = DVE.do(lambda e: e.tensor_tensor(tb, src2, sin_b, ALU.mult), after)
            o1 = DVE.do(lambda e: e.tensor_tensor(dst1, ta, tb, ALU.subtract), a, b_)
            a = DVE.do(lambda e: e.tensor_tensor(ta, src2, cos_b, ALU.mult), o1)
            b_ = DVE.do(lambda e: e.tensor_tensor(tb, src1, sin_b, ALU.mult), o1)
            rope_last[0] = DVE.do(lambda e: e.tensor_tensor(dst2, ta, tb, ALU.add), a, b_)
            return rope_last[0]

        k_rot = place("k_rot", FR, 3072, [P, TT, 2, ROPE])
        tmp_k = rope_w[:, 4, :, :]
        b = odd_bank()
        for tt in range(TT):
            k1 = c_kv[:, tt, KV_RANK:KV_RANK + ROPE2].unsqueeze(1)
            k2 = c_kv[:, tt, KV_RANK + ROPE2:KV_RANK + ROPE].unsqueeze(1)
            t = rope(k1, k2, k_rot[:, tt, 0:1, 0:ROPE2], k_rot[:, tt, 0:1, ROPE2:ROPE], 1, tt, [c_kv_done[tt], ffn1_done],
                     (tmp_k[:, 0:1, :], tmp_k[:, 1:2, :]))
            t = DVE.do(lambda e, tt=tt: e.tensor_copy(k_rot[:, tt, 1, :], k_rot[:, tt, 0, :]), t)
            t = PE.do(lambda e, tt=tt, b=b: e.transpose(banks[b][:, tt * P:(tt + 1) * P], k_rot[:, tt, :, :].rearrange("p a c -> p (a c)"), identity), t, bank_read[b])
        k_rope_x = place("k_rope_x", FR, 5120, [P, T])
        k_rope_done = bank_read[b] = DVE.do(lambda e, b=b: e.tensor_copy(k_rope_x[:, :], banks[b][:, 0:T]), t, rs_kv_done)

        gv = place("decay_work", "mid", 0, [P, 2, 3, T])
        b_last, decay = stats(GLA_HEADS * N_CHUNKS), stats(GLA_HEADS * N_CHUNKS)
        keep = param2("chunk_causal").bitcast(I32)
        restart = param2("chunk_restart")
        wgu, b_gate = param2("w_gate_up"), param("b_gate")
        C = GLA_CHUNK
        decayed = [None] * GLA_HEADS
        decay_work_free = [down_done, down_done]

        def decays():
            for h in range(GLA_HEADS):
                g_a, g_b, g_sum = (gv[:, h % 2, i, :] for i in range(3))
                bl, dc = b_last[:, h * N_CHUNKS:(h + 1) * N_CHUNKS], decay[:, h * N_CHUNKS:(h + 1) * N_CHUNKS]
                free = decay_work_free[h % 2]
                b = odd_bank()
                t = PE.do(lambda e, h=h, b=b: e.matmul(banks[b][:, 0:T], wgu[0:GATE_RANK, h * P:(h + 1) * P], a_lr[:, :], start=True, stop=True),
                          a_lr_done, params2_landed, bank_read[b])
                bg = b_gate[:, h:h + 1]
                t1 = DVE.do(lambda e, b=b, bg=bg, o=g_sum: e.tensor_scalar(o, banks[b][:, 0:T], bg, 0.0, ALU.add, ALU.min), t, free)
                t2 = DVE.do(lambda e, b=b, bg=bg, o=g_b: e.tensor_scalar(o, banks[b][:, 0:T], bg, 0.0, ALU.add, ALU.max), t, free)
                bank_read[b] = t2
                t = DVE.do(lambda e, a=g_a, s=g_sum, b=g_b: e.tensor_tensor(a, s, b, ALU.subtract), t1, t2)
                yield
                t = ACTE.do(lambda e, a=g_a: e.activation(a, a, ACT.Exp), t)
                t = DVE.do(lambda e, a=g_a: e.tensor_scalar(a, a, 1.0, None, ALU.add), t)
                yield
                t = ACTE.do(lambda e, a=g_a: e.activation(a, a, ACT.Ln), t)
                t = DVE.do(lambda e, a=g_a, s=g_sum: e.tensor_tensor(a, s, a, ALU.subtract), t)
                sums = DVE.do(lambda e, a=g_a, s=g_sum: e.tensor_tensor_scan(s, restart, a, 0.0, ALU.mult, ALU.add), t)
                t = DVE.do(lambda e, s=g_sum, bl=bl: e.tensor_scalar(bl, s[:, C - 1::C], 1.0 / GLA_TAU, None, ALU.mult), sums)
                yield
                dec = ACTE.do(lambda e, bl=bl, dc=dc: e.activation(dc, bl, ACT.Exp), t)
                for n in range(N_CHUNKS):
                    cs = slice(n * C, (n + 1) * C)
                    u = ACTE.do(lambda e, n=n, cs=cs, a=g_a, s=g_sum, bl=bl: e.activation(a[:, cs], s[:, cs], ACT.Exp, scale=-1.0 / GLA_TAU, bias=bl[:, n:n + 1]), t)
                v = ACTE.do(lambda e, s=g_sum, b=g_b: e.activation(b, s, ACT.Exp, scale=1.0 / GLA_TAU), sums)
                yield
                kd = DVE.do(lambda e, h=h, a=g_a: e.tensor_tensor(gla_kd[:, h, :], gla_k[:, h, :], a, ALU.mult), u, gla_k_done)
                qd = DVE.do(lambda e, h=h, b=g_b: e.tensor_tensor(gla_q[:, h, :], gla_q[:, h, :], b, ALU.mult), v, gla_q_done)
                u = ACTE.do(lambda e, s=g_sum, a=g_a: e.activation(a, s, ACT.Exp, scale=-1.0 / GLA_TAU), kd)
                yield
                ki = DVE.do(lambda e, h=h, a=g_a: e.tensor_tensor(gla_k[:, h, :], gla_k[:, h, :], a, ALU.mult), u)
                decayed[h] = [kd, qd, ki, dec]
                decay_work_free[h % 2] = [ki, qd]
                yield

        decaying = Beside(decays())

        gla_v = place("gla_v", "wide", 0, [P, TT, GLA_HEADS * GLA_V])
        gla_o = place("gla_o", "wide", TT * GLA_HEADS * GLA_V * 4, [P, TT, GLA_HEADS * GLA_V])
        ready = {}
        for name, dst, func in (("gla_v", gla_v, ACT.Copy), ("gla_r", gla_o, ACT.Silu)):
            for n in range(2):
                steps = group_steps((name, n), 512, h_hi, h_lo, h_of)
                while True:
                    try:
                        next(steps)
                    except StopIteration as end:
                        outs, pair, t = end.value
                        break
                    if name == "gla_v" or n == 0:
                        decaying.step(1)
                h_used = t
                if name == "gla_r" and n == 0:
                    decaying.finish()
                for tt in range(TT):
                    ready[name] = bank_read[pair[tt]] = ACTE.do(lambda e, tt=tt, n=n, out=outs[tt], dst=dst, func=func: e.activation(
                        dst[:, tt, n * 512:(n + 1) * 512], out, func), t, wide_free)
        gla_v_done, gla_r_done = ready["gla_v"], ready["gla_r"]

        gla_ss, gla_rs = stats(GLA_HEADS * TT), stats(GLA_HEADS * TT)
        gw = []
        for i, off in enumerate((8192, 24576)):
            gw.append((place(f"g_kdn{i}", "mid", off, [P, TT, P]), place(f"g_at{i}", "mid", off + 1024, [P, TT, P]),
                       place(f"g_state{i}", "mid", off + 2048, [P, N_CHUNKS - 1, GLA_V]), place(f"g_junk{i}", "mid", off + 5120, [P, GLA_V])))
        at_zero = [DVE.do(lambda e, i=i: e.memset(gw[i][1][:, :, :], 0.0), down_done) for i in range(2)]
        gla_out = [None] * GLA_HEADS
        gla_read = [None] * GLA_HEADS

        def gla():
            for h in range(GLA_HEADS):
                kdn, at_, state_, junk_ = gw[h % 2]
                before = [gla_out[h - 2], gla_read[h - 2], down_done] if h >= 2 else [down_done]
                kd, qd, ki, dec = decayed[h]
                v_h = slice(h * GLA_V, (h + 1) * GLA_V)
                for tt in range(TT):
                    t = PE.do(lambda e, h=h, tt=tt: e.transpose(banks[6][:, tt * P:(tt + 1) * P], gla_kd[:, h, tt * P:(tt + 1) * P], identity), kd, bank_read[6])
                kdn_done = bank_read[6] = ACTE.do(lambda e, kdn=kdn: e.activation(kdn[:, :, :].rearrange("p t c -> p (t c)"), banks[6][:, 0:T], ACT.Copy), t, before)
                for tt in range(TT):
                    t = PE.do(lambda e, h=h, tt=tt: e.matmul(banks[7][:, tt * P:(tt + 1) * P], gla_k[:, h, tt * P:(tt + 1) * P],
                                                             gla_q[:, h, tt * P:(tt + 1) * P], start=True, stop=True), ki, qd, bank_read[7])
                for tt in range(TT):
                    a_done = DVE.do(lambda e, tt=tt, at_=at_: e.copy_predicated(at_[:, tt, :], keep, banks[7][:, tt * P:(tt + 1) * P]), t, before, at_zero)
                bank_read[7] = a_done
                yield
                s_prev = None
                for n in range(N_CHUNKS - 1):
                    b = 6 + n % 2
                    rows = slice(C * (n % 2), C * (n % 2) + C)
                    t = PE.do(lambda e, n=n, b=b, rows=rows, v_h=v_h, kdn=kdn: e.matmul(banks[b][:, 0:GLA_V], kdn[rows, n // 2, :], gla_v[rows, n // 2, v_h], start=True, stop=True),
                              kdn_done, gla_v_done, bank_read[b])
                    if n == 0:
                        s_prev = DVE.do(lambda e, b=b, s=state_: e.tensor_copy(s[:, 0, :], banks[b][:, 0:GLA_V]), t, before)
                    else:
                        dn = decay[:, h * N_CHUNKS + n:h * N_CHUNKS + n + 1]
                        s_prev = DVE.do(lambda e, b=b, n=n, s=state_, dn=dn: e.scalar_tensor_tensor(s[:, n, :], s[:, n - 1, :], dn, banks[b][:, 0:GLA_V], ALU.mult, ALU.add),
                                        t, s_prev, dec)
                    bank_read[b] = s_prev
                yield
                for tt in range(TT):
                    b = 2 + tt
                    out = banks[b][:, 0:GLA_V]
                    t = PE.do(lambda e, tt=tt, out=out, v_h=v_h, at_=at_: e.matmul(out, at_[:, tt, :], gla_v[:, tt, v_h], start=True, stop=False, skip_group_check=True),
                              a_done, gla_v_done, bank_read[b])
                    for n in (2 * tt, 2 * tt + 1):
                        if n == 0:
                            continue
                        rows = slice(C * (n % 2), C * (n % 2) + C)
                        t = PE.do(lambda e, n=n, h=h, b=b, rows=rows, s=state_: e.matmul(banks[b][rows, 0:GLA_V], gla_q[:, h, n * C:(n + 1) * C], s[:, n - 1, :],
                                                                                        start=False, stop=n % 2 == 1, skip_group_check=True), s_prev)
                    i = h * TT + tt
                    u = ACTE.do(lambda e, out=out, i=i, j=junk_: e.activation(j[:, :], out, ACT.Square, accum_out=gla_ss[:, i:i + 1]), t, before, gla_out[h] and gla_out[h][1])
                    w = rms_power(gla_rs[:, i:i + 1], gla_ss[:, i:i + 1], GLA_V, u)
                    bank_read[b] = DVE.do(lambda e, out=out, i=i, tt=tt, v_h=v_h: e.scalar_tensor_tensor(
                        gla_o[:, tt, v_h], out, gla_rs[:, i:i + 1], gla_o[:, tt, v_h], ALU.mult, ALU.mult), w, gla_r_done)
                    gla_out[h] = [t, u, bank_read[b]]
                gla_read[h] = [bank_read[2], bank_read[3], s_prev]
                yield

        g_gla = param("g_gla")
        gla_ready = [None] * (KD // 2)

        def gla_transpose():
            for h in range(GLA_HEADS):
                for q in range(2):
                    k = 2 * h + q
                    gla_ready[k] = transpose_split(lambda tt, _, k=k: gla_o[:, tt, k * P:(k + 1) * P], 1, lambda _, q=q: g_gla[:, q:q + 1], None,
                                                   lambda _, k=k: mix_hi[:, KD // 2 + k, :], lambda _, k=k: mix_lo[:, KD // 2 + k, :], None, None,
                                                   lambda tt, _, h=h: gla_read[h], [gla_out[GLA_HEADS - 1], gla_read[GLA_HEADS - 1], gla_out[GLA_HEADS - 2], gla_read[GLA_HEADS - 2]])[0]
                    yield

        linear = Beside(gla(), gla_transpose())

        q_nope = place("q_nope", "h", 0, [P, MLA_HEADS, T])
        k_nope = place("k_nope", "h", 8192, [P, MLA_HEADS, T])
        mla_v = place("mla_v", "h", 16384, [P, TT, MLA_HEADS * NOPE])
        q_rope_T = place("q_rope_T", "h", 24576, [P, 4, T])
        q_rot = place("q_rot", "acc", 0, [P, TT, MLA_HEADS * ROPE])
        rope_tmp = place("rope_tmp", "h", 29696, [P, 2, MLA_HEADS, ROPE2])
        use["tile"], use["group"] = (4, 5), ((0, 1),)
        outs, pair, t = group("q_rope", MLA_HEADS * ROPE, cq_hi, cq_lo, lambda k: cq_ready[k])
        linear.step(1)
        for tt in range(TT):
            src = outs[tt].rearrange("p (h c) -> p h c", h=MLA_HEADS)
            dst = q_rot[:, tt, :].rearrange("p (h c) -> p h c", h=MLA_HEADS)
            u = rope(src[:, :, 0:ROPE2], src[:, :, ROPE2:ROPE], dst[:, :, 0:ROPE2], dst[:, :, ROPE2:ROPE], MLA_HEADS, tt,
                     [t, h_used, cq_ready], (rope_tmp[:, 0, :, :], rope_tmp[:, 1, :, :]))
            bank_read[pair[tt]] = u
        q_rot_done = u
        for h in range(MLA_HEADS):
            out, b, t = tile(("q_nope", h), cq_hi, cq_lo, lambda k: cq_ready[k])
            q_nope_done = bank_read[b] = ACTE.do(lambda e, h=h, out=out: e.activation(q_nope[:, h, :], out, ACT.Copy, scale=MLA_SCALE), t, h_used)
            if h % 2:
                linear.step(1)
        for j in range(4):
            b = use["tile"][j % 2]
            for tt in range(TT):
                t = PE.do(lambda e, j=j, tt=tt, b=b: e.transpose(banks[b][:, tt * P:(tt + 1) * P], q_rot[:, tt, j * P:(j + 1) * P], identity), q_rot_done, bank_read[b])
            q_rope_done = bank_read[b] = ACTE.do(lambda e, j=j, b=b: e.activation(q_rope_T[:, j, :], banks[b][:, 0:T], ACT.Copy, scale=MLA_SCALE), t, h_used)
        state["ada_slot"] = [[q_rope_done, cq_ready, ckv_ready, k_rope_done, a_lr_done]] * 2
        for h in range(MLA_HEADS):
            out, b, t = tile(("k_nope", h), ckv_hi, ckv_lo, lambda k: ckv_ready[k])
            k_nope_done = bank_read[b] = ACTE.do(lambda e, h=h, out=out: e.activation(k_nope[:, h, :], out, ACT.Copy), t, h_used)
            if h % 4 == 3:
                linear.step(1)
        for n in range(2):
            outs, pair, t = group(("mla_v", n), 512, ckv_hi, ckv_lo, lambda k: ckv_ready[k])
            for tt in range(TT):
                mla_v_done = bank_read[pair[tt]] = ACTE.do(lambda e, tt=tt, n=n, out=outs[tt]: e.activation(
                    mla_v[:, tt, n * 512:(n + 1) * 512], out, ACT.Copy), t, h_used)
            linear.step(1)
        latents_used = t

        m_scores = place("m_scores", FR, 8192, [P, 3, T])
        m_T = place("m_T", FR, 8192 + 3072, [P, 2, TT, P])
        NM = MLA_HEADS * TT
        m_max, m_sum = stats(NM), stats(NM)
        m_units = [(h, tt) for h in range(MLA_HEADS) for tt in range(TT)]
        m_free = {"s": [latents_used] * 3, "T": [latents_used] * 2}
        mla_ready = [None] * MLA_HEADS

        def latent_scores(u):
            h, tt = m_units[u]
            n = P * (tt + 1)
            b = u % 2
            rows = slice(ROPE * (h % 2), ROPE * (h % 2) + ROPE)
            toks = slice(tt * P, (tt + 1) * P)
            PE.do(lambda e: e.matmul(banks[b][:, 0:n], q_nope[:, h, toks], k_nope[:, h, 0:n], start=True, stop=False),
                  q_nope_done, k_nope_done, bank_read[b], signal=False)
            t = PE.do(lambda e: e.matmul(banks[b][:, 0:n], q_rope_T[rows, h // 2, toks], k_rope_x[rows, 0:n], start=False, stop=True),
                      q_rope_done, k_rope_done)
            s = m_scores[:, u % 3, 0:n]
            t = DVE.do(lambda e: e.tensor_tensor(s, banks[b][:, 0:n], causal[:, T - n:T], ALU.add), t, m_free["s"][u % 3])
            bank_read[b] = t
            t = DVE.do(lambda e: e.tensor_reduce(m_max[:, u:u + 1], s, AX.X, ALU.max, negate=True), t)
            return t

        def latent_exp(u, t):
            s = m_scores[:, u % 3, 0:P * (m_units[u][1] + 1)]
            return ACTE.do(lambda e: e.activation(s, s, ACT.Exp, bias=m_max[:, u:u + 1], accum_out=m_sum[:, u:u + 1]), t)

        def latent_weights(u, t):
            h, tt = m_units[u]
            s = m_scores[:, u % 3, 0:P * (tt + 1)]
            t = DVE.do(lambda e: e.reciprocal(m_sum[:, u:u + 1], m_sum[:, u:u + 1]), t)
            return DVE.do(lambda e: e.tensor_scalar(s, s, m_sum[:, u:u + 1], None, ALU.mult), t)

        def latent_transpose(u, p_done):
            h, tt = m_units[u]
            for sb in range(tt + 1):
                t = PE.do(lambda e, sb=sb: e.transpose(banks[4][:, sb * P:(sb + 1) * P], m_scores[:, u % 3, sb * P:(sb + 1) * P], identity),
                          p_done, bank_read[4])
            m_free["s"][u % 3] = t
            wt = bank_read[4] = ACTE.do(lambda e: e.activation(m_T[:, u % 2, 0:tt + 1, :].rearrange("p a c -> p (a c)"), banks[4][:, 0:(tt + 1) * P], ACT.Copy), t, m_free["T"][u % 2])
            return wt

        def latent_output(u, wt):
            h, tt = m_units[u]
            for sb in range(tt + 1):
                t = PE.do(lambda e, sb=sb: e.matmul(banks[5][:, 0:P], mla_v[:, sb, h * NOPE:(h + 1) * NOPE], m_T[:, u % 2, sb, :], start=sb == 0, stop=sb == tt),
                          wt, mla_v_done, bank_read[5])
            m_free["T"][u % 2] = t
            toks = slice(tt * P, (tt + 1) * P)
            mla_ready[h] = bank_read[5] = split(mix_hi[:, h, toks], mix_lo[:, h, toks], banks[5][:, 0:P], t, decay_work_free)

        first_ada = plan.groups["mla_v", 1][-1][0] + 1
        exped, weighted, turned = None, None, None
        for u in range(NM + 3):
            now = (u, latent_scores(u)) if u < NM else None
            weighed = (exped[0], latent_weights(*exped)) if exped is not None else None
            turned_next = (weighted[0], latent_transpose(*weighted)) if weighted is not None else None
            if turned is not None:
                latent_output(*turned)
            linear.step(1)
            while state["prepared"] <= first_ada + ADA_BESIDE_LATENT * (u + 1) // NM and state["prepared"] < first_ada + ADA_BESIDE_LATENT:
                prepare(state["prepared"])
                run_deferred()
            exped = (u, latent_exp(*now)) if now is not None else None
            turned, weighted = turned_next, weighed
        linear.finish()
        assert turned is None and weighted is None
        use["tile"], use["group"] = (4, 5, 2, 3), ((0, 1), (2, 3))
        mix_ready = mla_ready + gla_ready
        attn_free = mla_ready[-1]

        def gate_row(gate_v, folded_token, free, done):
            diag_free = [free, free]
            return lambda *quarters: done.extend(broadcast_row(lambda k: ada(gate_v)[:, k:k + 1], diag_free, folded_token, quarters))

        def gated_residual(gate_v, squares, row_done):
            rs, rs_done = squares.factors()
            done = {}
            after = RowSquares(junk[:, :], squares.last[1])
            for q in range(4):
                for tt in range(TT):
                    w_q, x_q = wide[:, tt, q * 512:(q + 1) * 512], x[:, tt, q * 512:(q + 1) * 512]
                    u = bank_read[ROW_BANKS[q]] = DVE.do(lambda e, tt=tt, q=q, w_q=w_q: e.scalar_tensor_tensor(w_q, w_q, rs[:, tt:tt + 1], banks[ROW_BANKS[q]][:, :], ALU.mult, ALU.mult), rs_done[tt], row_done[q])
                    done[tt, q] = DVE.do(lambda e, w_q=w_q, x_q=x_q: e.tensor_tensor(x_q, x_q, w_q, ALU.add), u)
                    if gate_v == 2:
                        after.add(tt, q, x_q, done[tt, q])
            return done, after

        squares = RowSquares(junk[:, :], attn_free)
        row_done = []
        o_done = fresh_groups(("out2",), mix_hi, mix_lo, lambda k: mix_ready[k], wide, gla_ready[-1], squares,
                              row=gate_row(2, folded_gate, attn_free, row_done))
        prepare(plan.groups["gate", 0][0][0] - 1)
        run_deferred(True)
        done, squares = gated_residual(2, squares, row_done)
        x_done = [done[tt, 3] for tt in range(TT)]
        folded_ffn = fold("g_pre_ffn", 4)
        h_ready = norm_to_h(*squares.factors(), x_done, lambda k: ada(4)[:, k:k + 1], lambda k: ada(3)[:, k:k + 1], work2, work2_free,
                            x_done, [folded_ffn, ada_done(3), attn_free])

        sw_g = place("sw_g", FR, 2048, [P, 2, T])
        sw_free = [h_ready[-1], h_ready[-1]]
        for half in range(2):
            ff_done = []
            for j in range(FF_HALF * half, FF_HALF * (half + 1)):
                s = j % 2
                out_g, bg, t = tile(("gate", j), h_hi, h_lo, h_of)
                t = bank_read[bg] = ACTE.do(lambda e, s=s, out=out_g: e.activation(sw_g[:, s, :], out, ACT.Silu), t, sw_free[s])
                out_u, bu, tu = tile(("up", j), h_hi, h_lo, h_of)
                t = bank_read[bu] = DVE.do(lambda e, s=s, out=out_u: e.tensor_tensor(sw_g[:, s, :], out, sw_g[:, s, :], ALU.mult), t, tu)
                jj = j - FF_HALF * half
                t = sw_free[s] = split(ff_hi[:, jj, :], ff_lo[:, jj, :], sw_g[:, s, :], t)
                ff_done.append(t)
            after = lambda k, d=ff_done: d[k]
            if half == 0:
                o_done = fresh_groups(("down2", 0), ff_hi, ff_lo, after, wide, h_ready[-1])
                DVE.wait(*o_done)
            else:
                squares = RowSquares(junk[:, :], h_ready[-1])
                assert plan.groups["down2", 1, 2][0][0] > max(i for i, kind in enumerate(plan.kinds) if kind == "ada") + AHEAD
                folded_gate_ffn = fold_gate("g_post_ffn", 5)
                row_done = []
                o_done = residual_groups(("down2", 1), ff_hi, ff_lo, after, wide, squares,
                                         row=gate_row(5, folded_gate_ffn, h_ready[-1], row_done))
        done, _ = gated_residual(5, squares, row_done)
        stored = sem("stored")
        for q in range(4):
            for tt in range(TT):
                SP.wait(done[tt, q])
                SP.steps.append(lambda e, tt=tt, q=q: e.dma_start(
                    OUT[tt * P:(tt + 1) * P, q * 512:(q + 1) * 512], x[:, tt, q * 512:(q + 1) * 512]).then_inc(stored, 16))
        SP.wait(("stored", stored, 16 * TT * 4))

        assert state["prepared"] == state["loaded"] == len(widths), state
        assert not any(pieces_left[i] for i in range(len(widths)) if plan.kinds[i] == "split")

        block = ctx.enter_context(nc.Block())

        @block.sync
        def _(e):
            SP.play(e)

        @block.gpsimd
        def _(e):
            POOL.play(e)

        @block.scalar
        def _(e):
            ACTE.play(e)

        @block.vector
        def _(e):
            DVE.play(e)

        @block.tensor
        def _(e):
            PE.play(e)



def bucket_of(distance):
    n = np.maximum(distance, 0)
    exact = BUCKETS // 2
    nf = np.maximum(n, 1).astype(np.float32)
    large = exact + (np.log(nf / np.float32(exact)) / np.float32(np.log(MAX_DISTANCE / exact)) * (BUCKETS - exact)).astype(np.int32)
    return np.where(n < exact, n, np.minimum(large, BUCKETS - 1))


def by_partition(v):
    return np.ascontiguousarray(v.reshape(-1, P).T)


def pack(table, values):
    out = np.zeros((P, table["_width"]), np.float32)
    for name, v in values.items():
        a, b = table[name]
        out[:v.shape[0], a:b] = v
    return out


def layout(i):
    mats = {
        "w_in_v": np.concatenate([i["w_in"][0][:, 1024 + 512 * br + 256:1024 + 512 * br + 512] for br in (1, 2)], 1),
        "w_ada": i["w_ada_2"][0], "w_out": i["w_out"][0], "w_up": i["w_up"][0], "w_down": i["w_down"][0],
        "w_in_2": i["w_in_2"][0], "w_uk": i["w_uk_2"][0], "w_uv": i["w_uv_2"][0], "w_out_2": i["w_out_2"][0],
        "w_ffn_gate": i["w_ffn_gate_2"][0], "w_ffn_up": i["w_ffn_up_2"][0], "w_ffn_down": i["w_ffn_down_2"][0],
    }
    w_in = i["w_in"][0]
    mats["w_in"] = np.concatenate([w_in[:, q_columns()], w_in[:, HEADS * DH:]], 1)
    latent = Q_RANK + KV_RANK + ROPE
    a_g = latent + 2 * GLA_HEADS * GLA_K + GLA_HEADS * GLA_V
    w2 = mats["w_in_2"]
    mats["w_in_2_kv"] = np.concatenate([w2[:, Q_RANK:latent], w2[:, a_g:a_g + GATE_RANK]], 1)
    uq = i["w_uq_2"][0].reshape(Q_RANK, MLA_HEADS, NOPE + ROPE)
    mats["w_uq_nope"] = uq[:, :, :NOPE].reshape(Q_RANK, -1)
    mats["w_uq_rope"] = uq[:, :, NOPE:].reshape(Q_RANK, -1)
    w1 = i["cmp_w1"][0].reshape(2, CMP_LEN, DH, DH).transpose(2, 0, 1, 3).reshape(DH, -1)
    mats["cmp_w1"] = np.concatenate([w1, w1], 0)
    plan = make_plan()
    weights = np.empty(P * sum(chunk_widths(plan)), np.float32)
    at = 0
    for chunk in plan.chunks:
        w = sum(c[3] for c in chunk)
        view = weights[at:at + P * w].reshape(P, w)
        c0 = 0
        for mat, kt, col, n in chunk:
            view[:, c0:c0 + n] = mats[mat][kt * P:(kt + 1) * P, col:col + n]
            c0 += n
        at += P * w
    p, c = np.arange(P)[:, None], np.arange(2 * P)[None, :]
    conv_w = lambda w: w.T.reshape(-1, P, w.shape[0]).transpose(1, 0, 2).reshape(P, -1)
    lasting = pack(LASTING, {
        "identity": np.eye(P), "ones": np.ones((P, P)),
        "causal": np.where(P + p - c >= 0, 0.0, MASKED),
        "mix_norm_g": by_partition(i["mix_norm_g"][0]), "ffn_norm_g": by_partition(i["ffn_norm_g"][0]),
        "final_norm_g": by_partition(i["final_norm_g"]), "g_pre_mix": by_partition(i["g_pre_mix_2"][0]),
        "g_post_mix": by_partition(i["g_post_mix_2"][0]), "g_pre_ffn": by_partition(i["g_pre_ffn_2"][0]),
        "g_post_ffn": by_partition(i["g_post_ffn_2"][0]), "b_ada": by_partition(i["b_ada_2"][0]),
        "c": by_partition(i["c_2"][0]), "ffn_conv_w": conv_w(i["ffn_conv_w"][0]),
        "ffn_conv_b": by_partition(i["ffn_conv_b"][0]), "g_q": by_partition(i["g_q_2"][0]),
        "g_kv": by_partition(i["g_kv_2"][0]), "b_gate": by_partition(i["b_gate_2"][0]),
        "g_gla": by_partition(i["g_gla_2"][0]),
    })
    distance = 2 * P - 1 - np.arange(ROW)
    one_hot = np.zeros((BUCKETS + 1, ROW), np.float32)
    one_hot[bucket_of(distance), np.arange(ROW)] = distance >= 0
    one_hot[BUCKETS] = distance < 0
    rel = np.concatenate([i["rel_bias"], np.full((1, HEADS), MASKED, np.float32)], 0)
    twice = lambda a: np.concatenate([a, a], 0)
    phase1 = pack(PHASE1, {
        "one_hot": one_hot, "rel_bias": rel,
        "cmp_w2": twice(i["cmp_w2"][0].transpose(1, 0, 2).reshape(DH, -1)),
        "cmp_pos": twice(i["cmp_pos"][0].transpose(2, 0, 1).reshape(DH, -1)),
        "conv_w": conv_w(i["conv_w"][0]), "conv_b": by_partition(i["conv_b"][0]),
        "conv_ln_g": by_partition(i["conv_ln_g"][0]), "conv_ln_b": by_partition(i["conv_ln_b"][0]),
        "any_block": (np.arange(T) >= CMP_LEN - 1).astype(np.float32).reshape(TT, P).T,
    })
    q, k = np.arange(P)[None, :], np.arange(P)[:, None]
    same = (q // GLA_CHUNK == k // GLA_CHUNK) & (k <= q)
    inv_freq = (1.0 / (np.float32(10000.0) ** (np.arange(0, ROPE, 2, dtype=np.float32) / np.float32(ROPE)))).astype(np.float32)
    phase2 = pack(PHASE2, {
        "w_gate_up": i["w_gate_up_2"][0], "inv_freq": np.broadcast_to(inv_freq, (P, ROPE2)),
        "chunk_restart": np.broadcast_to((np.arange(T) % GLA_CHUNK != 0).astype(np.float32), (P, T)),
        "chunk_causal": same.astype(np.float32),
    })
    return {
        "weights": weights, "x": np.ascontiguousarray(i["x"][0]), "params": lasting, "params1": phase1,
        "params2": phase2, "positions": np.ascontiguousarray(i["positions_2"][0].reshape(TT, P).T),
    }


def kernel(**inputs):
    import concourse.bacc as bacc
    from concourse.bass_utils import run_bass_kernel_spmd

    arrays = layout({name: np.asarray(v) for name, v in inputs.items()})
    nc = bacc.Bacc("TRN2", target_bir_lowering=False, num_devices=1)
    args = [nc.dram_tensor(name, a.shape, mybir.dt.from_np(a.dtype), kind="ExternalInput").ap()
            for name, a in arrays.items()]
    out = nc.dram_tensor("out", (T, D), F32, kind="ExternalOutput").ap()
    two_blocks(nc, *args, out)
    r = run_bass_kernel_spmd(nc, [arrays], core_ids=[0])
    return r.results[0]["out"].reshape(1, T, D)
```
